# Optimizing a Trainium2 kernel written in Bass

```python
import math
import jax, jax.numpy as jnp
from jax import lax
import numpy as np

D_MODEL = 1024
BATCH = 1
SEQ = 256
DEPTH = 2

N_MIXERS = 2
EPS = 1e-6
ML_HEADS = 8
ML_DQK = D_MODEL // (2 * ML_HEADS)
ML_DV = D_MODEL // ML_HEADS
ML_CHUNK = 64
ML_FGATE_BIAS_LO = 3.0
ML_FGATE_BIAS_HI = 6.0
ML_M_INIT = -1e30
DA_HEADS = 8
DA_DHEAD = D_MODEL // (2 * DA_HEADS)
DA_DV = 2 * DA_DHEAD
ROPE_THETA = 500000.0
ROPE_DIM = DA_DHEAD // 4
Q_BLOCK = 128
PEER_HEADS = 8
N_KEYS = 128
N_EXPERTS = N_KEYS * N_KEYS
PEER_TOPK = 16
PEER_DQ = 256
PEER_DHALF = PEER_DQ // 2
PEER_CHUNK = 128

ML_IN_COLS = 2 * ML_HEADS * ML_DQK + 2 * ML_HEADS * ML_DV + 4 * ML_HEADS
DA_IN_COLS = 2 * DA_HEADS * DA_DHEAD * 2 + DA_HEADS * DA_DV

kernel_name = "hybrid_mlstm_diffattn_peer"

def rmsnorm(x, g):
    xf = x.astype(jnp.float32)
    y = xf * lax.rsqrt(jnp.mean(xf * xf, axis=-1, keepdims=True) + EPS)
    return (y * g.astype(jnp.float32)).astype(x.dtype)

def partial_rope(x, positions):
    half = ROPE_DIM // 2
    inv = ROPE_THETA ** (-jnp.arange(half, dtype=jnp.float32) * 2.0 / ROPE_DIM)
    ang = positions.astype(jnp.float32)[..., None] * inv
    cos = jnp.cos(ang)[:, :, None, None, :]
    sin = jnp.sin(ang)[:, :, None, None, :]
    xf = x.astype(jnp.float32)
    x1, x2, rest = xf[..., :half], xf[..., half:ROPE_DIM], xf[..., ROPE_DIM:]
    out = jnp.concatenate([x1 * cos - x2 * sin, x2 * cos + x1 * sin, rest], axis=-1)
    return out.astype(x.dtype)

def mlstm_chunkwise(q, k, v, log_i, log_f):
    B, H, S, dk = q.shape
    dv = v.shape[-1]
    L = ML_CHUNK
    nc = S // L
    q = q.reshape(B, H, nc, L, dk) * (dk ** -0.5)
    k = k.reshape(B, H, nc, L, dk)
    v = v.reshape(B, H, nc, L, dv)
    li = log_i.reshape(B, H, nc, L)
    lf = log_f.reshape(B, H, nc, L)
    b = jnp.cumsum(lf, axis=-1)
    bL = b[..., -1]
    a = bL[..., None] - b + li
    m_loc = jnp.max(a, axis=-1)
    w = jnp.exp(a - m_loc[..., None])
    C_loc = jnp.einsum('bhcs,bhcsv,bhcsk->bhcvk', w, v, k)
    n_loc = jnp.einsum('bhcs,bhcsk->bhck', w, k)

    def step(carry, xs):
        C, n, m = carry
        bL_c, m_loc_c, C_loc_c, n_loc_c = xs
        m_new = jnp.maximum(bL_c + m, m_loc_c)
        sp = jnp.exp(bL_c + m - m_new)
        sl = jnp.exp(m_loc_c - m_new)
        C_new = sp[..., None, None] * C + sl[..., None, None] * C_loc_c
        n_new = sp[..., None] * n + sl[..., None] * n_loc_c
        return (C_new, n_new, m_new), (C, n, m)

    init = (jnp.zeros((B, H, dv, dk), jnp.float32),
            jnp.zeros((B, H, dk), jnp.float32),
            jnp.full((B, H), ML_M_INIT, jnp.float32))
    xs = (jnp.moveaxis(bL, 2, 0), jnp.moveaxis(m_loc, 2, 0),
          jnp.moveaxis(C_loc, 2, 0), jnp.moveaxis(n_loc, 2, 0))
    _, (C_prev, n_prev, m_prev) = lax.scan(step, init, xs)
    C_prev = jnp.moveaxis(C_prev, 0, 2)
    n_prev = jnp.moveaxis(n_prev, 0, 2)
    m_prev = jnp.moveaxis(m_prev, 0, 2)

    mask = jnp.tril(jnp.ones((L, L), dtype=bool))
    D = b[..., :, None] - b[..., None, :] + li[..., None, :]
    D = jnp.where(mask, D, -jnp.inf)
    g = b + m_prev[..., None]
    m_t = jnp.maximum(g, jnp.max(D, axis=-1))
    Sqk = jnp.einsum('bhctd,bhcsd->bhcts', q, k) * jnp.exp(D - m_t[..., None])
    inter = jnp.exp(g - m_t)
    num = (jnp.einsum('bhcts,bhcsv->bhctv', Sqk, v)
           + inter[..., None] * jnp.einsum('bhcvk,bhctk->bhctv', C_prev, q))
    den = jnp.sum(Sqk, axis=-1) + inter * jnp.einsum('bhck,bhctk->bhct', n_prev, q)
    h = num / jnp.maximum(jnp.abs(den), jnp.exp(-m_t))[..., None]
    return h.reshape(B, H, S, dv)

def mlstm_mixer(x, norm_g, w_in, b_gates, head_g, w_out):
    B, S, _ = x.shape
    h = rmsnorm(x, norm_g)
    proj = h @ w_in
    nq = ML_HEADS * ML_DQK
    nv = ML_HEADS * ML_DV
    q, k, v, o, gates = jnp.split(proj, [nq, 2 * nq, 2 * nq + nv, 2 * nq + 2 * nv], axis=-1)

    def heads(t, d):
        return t.reshape(B, S, ML_HEADS, d).transpose(0, 2, 1, 3).astype(jnp.float32)

    q, k, v = heads(q, ML_DQK), heads(k, ML_DQK), heads(v, ML_DV)
    gates = gates.astype(jnp.float32) + b_gates.astype(jnp.float32)
    gates = gates.reshape(B, S, 4, ML_HEADS).transpose(2, 0, 3, 1)
    i_fwd, f_fwd, i_bwd, f_bwd = gates[0], gates[1], gates[2], gates[3]
    h_fwd = mlstm_chunkwise(q, k, v, i_fwd, jax.nn.log_sigmoid(f_fwd))
    flip = lambda t: jnp.flip(t, axis=2)
    h_bwd = flip(mlstm_chunkwise(flip(q), flip(k), flip(v), flip(i_bwd),
                                 flip(jax.nn.log_sigmoid(f_bwd))))
    hs = (h_fwd + h_bwd).transpose(0, 2, 1, 3)
    hs = hs * lax.rsqrt(jnp.mean(hs * hs, axis=-1, keepdims=True) + EPS)
    hs = hs.reshape(B, S, D_MODEL) * head_g.astype(jnp.float32)
    hs = hs * jax.nn.sigmoid(o.astype(jnp.float32))
    return hs.astype(x.dtype) @ w_out

def diff_attn_mixer(x, positions, norm_g, w_qkv, q_g, k_g, lam_q1, lam_k1, lam_q2, lam_k2,
                    subln_g, w_out, lambda_init):
    B, S, _ = x.shape
    h = rmsnorm(x, norm_g)
    q, k, v = jnp.split(h @ w_qkv, 3, axis=-1)
    q = q.reshape(B, S, DA_HEADS, 2, DA_DHEAD)
    k = k.reshape(B, S, DA_HEADS, 2, DA_DHEAD)
    v = v.reshape(B, S, DA_HEADS, DA_DV).transpose(0, 2, 1, 3)
    q = partial_rope(rmsnorm(q, q_g), positions).transpose(0, 2, 3, 1, 4)
    k = partial_rope(rmsnorm(k, k_g), positions).transpose(0, 2, 3, 1, 4)
    lam = (jnp.exp(jnp.sum(lam_q1.astype(jnp.float32) * lam_k1.astype(jnp.float32)))
           - jnp.exp(jnp.sum(lam_q2.astype(jnp.float32) * lam_k2.astype(jnp.float32)))
           + lambda_init)
    scale = DA_DHEAD ** -0.5
    nb = S // Q_BLOCK
    qb = jnp.moveaxis(q.reshape(B, DA_HEADS, 2, nb, Q_BLOCK, DA_DHEAD), 3, 0)

    def attend(qblk):
        s = jnp.einsum('bhcqd,bhckd->bhcqk', qblk, k).astype(jnp.float32) * scale
        p = jax.nn.softmax(s, axis=-1)
        a = p[:, :, 0] - lam * p[:, :, 1]
        return jnp.einsum('bhqk,bhkv->bhqv', a.astype(v.dtype), v)

    o = lax.map(attend, qb)
    o = o.transpose(1, 0, 3, 2, 4).reshape(B, S, DA_HEADS, DA_DV)
    o = rmsnorm(o, subln_g) * (1.0 - lambda_init)
    return o.reshape(B, S, D_MODEL) @ w_out

def peer_ffn(x, norm_g, w_query, sub_keys, u_table, v_table):
    B, S, D = x.shape
    T = B * S
    h = rmsnorm(x, norm_g).reshape(T, D)
    q = (h @ w_query).reshape(T, PEER_HEADS, 2, PEER_DHALF)
    s = jnp.einsum('thpd,hpnd->thpn', q, sub_keys).astype(jnp.float32)
    vals, idx = lax.top_k(s, PEER_TOPK)
    cand = vals[:, :, 0, :, None] + vals[:, :, 1, None, :]
    cidx = idx[:, :, 0, :, None] * N_KEYS + idx[:, :, 1, None, :]
    cand = cand.reshape(T, PEER_HEADS, PEER_TOPK * PEER_TOPK)
    cidx = cidx.reshape(T, PEER_HEADS, PEER_TOPK * PEER_TOPK)
    top_s, pos = lax.top_k(cand, PEER_TOPK)
    experts = jnp.take_along_axis(cidx, pos, axis=-1)
    gates = jax.nn.softmax(top_s, axis=-1)
    nch = T // PEER_CHUNK
    E = PEER_HEADS * PEER_TOPK
    hc = h.reshape(nch, PEER_CHUNK, D)
    ec = experts.reshape(nch, PEER_CHUNK, E)
    gc = gates.reshape(nch, PEER_CHUNK, E)

    def block(args):
        hb, eb, gb = args
        ue = u_table[eb]
        act = jax.nn.gelu(jnp.einsum('td,ted->te', hb, ue), approximate=False)
        ve = v_table[eb]
        return jnp.einsum('te,ted->td', (gb * act.astype(jnp.float32)).astype(ve.dtype), ve)

    out = lax.map(block, (hc, ec, gc))
    return out.reshape(B, S, D).astype(x.dtype)

def setup_inputs(seed: int = 0) -> dict:
    key = jax.random.key(seed)
    ks = jax.random.split(key, 40)
    f32 = jnp.float32
    nrm = lambda k, shape, sc: jax.random.normal(k, shape, f32) * sc
    gain = lambda k, n: 1.0 + 0.02 * jax.random.normal(k, (n,), f32)
    fan = D_MODEL ** -0.5
    x = jax.random.normal(ks[0], (BATCH, SEQ, D_MODEL), f32)
    positions = (jnp.arange(SEQ, dtype=jnp.int32)[None, :]
                 + jax.random.randint(ks[1], (BATCH, 1), 0, 4096, dtype=jnp.int32))
    b_i = 0.1 * jax.random.normal(ks[4], (ML_HEADS,), f32)
    b_f = jnp.linspace(ML_FGATE_BIAS_LO, ML_FGATE_BIAS_HI, ML_HEADS, dtype=f32) + 0.1 * jax.random.normal(ks[5], (ML_HEADS,), f32)
    b_ib = 0.1 * jax.random.normal(ks[6], (ML_HEADS,), f32)
    b_fb = jnp.linspace(ML_FGATE_BIAS_LO, ML_FGATE_BIAS_HI, ML_HEADS, dtype=f32) + 0.1 * jax.random.normal(ks[7], (ML_HEADS,), f32)
    return {
        "x": x,
        "positions": positions,
        "l0_norm_mix": gain(ks[2], D_MODEL),
        "l0_w_in": nrm(ks[3], (D_MODEL, ML_IN_COLS), fan),
        "l0_b_gates": jnp.concatenate([b_i, b_f, b_ib, b_fb]),
        "l0_head_norm": gain(ks[8], D_MODEL),
        "l0_w_out": nrm(ks[9], (D_MODEL, D_MODEL), fan),
        "l0_norm_ffn": gain(ks[10], D_MODEL),
        "l0_peer_wq": nrm(ks[11], (D_MODEL, PEER_HEADS * PEER_DQ), fan),
        "l0_peer_keys": nrm(ks[12], (PEER_HEADS, 2, N_KEYS, PEER_DHALF), PEER_DHALF ** -0.5),
        "l0_peer_u": nrm(ks[13], (N_EXPERTS, D_MODEL), fan),
        "l0_peer_v": nrm(ks[14], (N_EXPERTS, D_MODEL), 0.25),
        "l1_norm_mix": gain(ks[15], D_MODEL),
        "l1_w_qkv": nrm(ks[16], (D_MODEL, DA_IN_COLS), fan),
        "l1_q_norm": gain(ks[17], DA_DHEAD),
        "l1_k_norm": gain(ks[18], DA_DHEAD),
        "l1_lambda_q1": nrm(ks[19], (DA_DHEAD,), 0.1),
        "l1_lambda_k1": nrm(ks[20], (DA_DHEAD,), 0.1),
        "l1_lambda_q2": nrm(ks[21], (DA_DHEAD,), 0.1),
        "l1_lambda_k2": nrm(ks[22], (DA_DHEAD,), 0.1),
        "l1_subln": gain(ks[23], DA_DV),
        "l1_w_out": nrm(ks[24], (D_MODEL, D_MODEL), fan),
        "l1_norm_ffn": gain(ks[25], D_MODEL),
        "l1_peer_wq": nrm(ks[26], (D_MODEL, PEER_HEADS * PEER_DQ), fan),
        "l1_peer_keys": nrm(ks[27], (PEER_HEADS, 2, N_KEYS, PEER_DHALF), PEER_DHALF ** -0.5),
        "l1_peer_u": nrm(ks[28], (N_EXPERTS, D_MODEL), fan),
        "l1_peer_v": nrm(ks[29], (N_EXPERTS, D_MODEL), 0.25),
    }

def reference(x, positions,
              l0_norm_mix, l0_w_in, l0_b_gates, l0_head_norm, l0_w_out,
              l0_norm_ffn, l0_peer_wq, l0_peer_keys, l0_peer_u, l0_peer_v,
              l1_norm_mix, l1_w_qkv, l1_q_norm, l1_k_norm,
              l1_lambda_q1, l1_lambda_k1, l1_lambda_q2, l1_lambda_k2, l1_subln, l1_w_out,
              l1_norm_ffn, l1_peer_wq, l1_peer_keys, l1_peer_u, l1_peer_v):
    mix_params = [
        (l0_norm_mix, l0_w_in, l0_b_gates, l0_head_norm, l0_w_out),
        (l1_norm_mix, l1_w_qkv, l1_q_norm, l1_k_norm, l1_lambda_q1, l1_lambda_k1,
         l1_lambda_q2, l1_lambda_k2, l1_subln, l1_w_out),
    ]
    ffn_params = [
        (l0_norm_ffn, l0_peer_wq, l0_peer_keys, l0_peer_u, l0_peer_v),
        (l1_norm_ffn, l1_peer_wq, l1_peer_keys, l1_peer_u, l1_peer_v),
    ]
    for i in range(DEPTH):
        if i % N_MIXERS == 0:
            x = x + mlstm_mixer(x, *mix_params[i])
        else:
            lambda_init = 0.8 - 0.6 * math.exp(-0.3 * i)
            x = x + diff_attn_mixer(x, positions, *mix_params[i], lambda_init=lambda_init)
        x = x + peer_ffn(x, *ffn_params[i])
    return x


_drawn_inputs = setup_inputs


def setup_inputs(seed=0):
    import zlib

    import numpy as np

    out = dict(_drawn_inputs(seed))
    spreads = {}
    factors = {'l1_q_norm': 3.746,
     'l1_k_norm': 3.776,
     'l1_lambda_q1': 3.488,
     'l1_lambda_k1': 4.614,
     'l1_lambda_q2': 2.93,
     'l1_lambda_k2': 4.325,
     'l1_subln': 3.739,
     'l1_norm_ffn': 3.92}
    for name, (base, spread) in spreads.items():
        noise = np.random.default_rng([zlib.crc32(name.encode()), seed]).standard_normal(out[name].shape)
        drawn = base * np.exp(spread * noise) if base else spread * noise
        out[name] = __import__('jax').numpy.asarray(drawn.astype(out[name].dtype))
    for name, factor in factors.items():
        out[name] = (out[name] * factor).astype(out[name].dtype)
    return out
```

```python
from contextlib import ExitStack

import numpy as np

import concourse.bass as bass
from concourse import mybir

F32 = mybir.dt.float32
U32 = mybir.dt.uint32
I32 = mybir.dt.int32
ALU = mybir.AluOpType
ACT = mybir.ActivationFunctionType
AX = mybir.AxisListType.X

P = 128
S = 256
D = 1024
NT = S // P
KD = D // P
HEADS = 8
EPS = 1e-6
NEG = -1e30
ML_DQK = 64
ML_SCALE = ML_DQK ** -0.5
DA_SCALE = 64 ** -0.5
LAMBDA_INIT = 0.8 - 0.6 * float(np.exp(-0.3))
ROPE_HALF = 8
ROPE_INV = (np.float32(500000.0) ** (-np.arange(ROPE_HALF, dtype=np.float32) * np.float32(2.0)
                                     / np.float32(16))).astype(np.float32)
TOPK = 16
NKEYS = 128
SLOTS = HEADS * TOPK
UNIT = 1024
RING = 4

U_QK, U_VO, U_WO, U_WQ, U_E, U_QKV = 8, 16, 8, 16, NKEYS, 24
UNITS_0 = U_QK + U_VO + U_WO
UNITS_FFN = U_WQ + 2 * U_E
UNITS_1 = U_QKV + U_WO
UNITS = UNITS_0 + UNITS_FFN + UNITS_1 + UNITS_FFN
PAIRS = UNITS // 2

SM_GAIN = 0
SM_SUBLN = SM_GAIN + 5 * KD
SM_BGATE = SM_SUBLN + 1
SM_QG = SM_BGATE + 32
SM_LAM = SM_QG + 128
SM_COLS = SM_LAM + 256

TWO_PI = 2.0 * np.pi
PI_1 = 6.28125
PI_2 = float(np.float32(TWO_PI - PI_1))
PI_2 = float(np.array(np.array(PI_2, np.float32).view(np.uint32) & np.uint32(0xFFFFF000)).view(np.float32))
PI_3 = float(np.float32(TWO_PI - PI_1 - PI_2))
PI_SAFE = 3.1415925


def program(nc, stream, small, w_gates, keys0, keys1, positions, x_in, out):
    with ExitStack() as ctx:
        def sb(name, shape, dt=F32):
            return ctx.enter_context(nc.sbuf_tensor(name, shape, dt))

        def sem(name):
            return ctx.enter_context(nc.semaphore(name))

        ps = ctx.enter_context(nc.psum_tensor("ps", [P, 8, 512], F32))

        big = sb("big", [P, NKEYS * S])
        ring = sb("ring", [P, RING, 2 * UNIT])
        x = sb("x", [P, NT, D])
        hT = sb("hT", [P, KD, S])
        keysT = sb("keysT", [P, 16, NKEYS])
        sm = sb("sm", [P, SM_COLS])
        wg = sb("wg", [P, KD, 32])
        pos_i = sb("pos_i", [P, NT], I32)
        ident = sb("ident", [P, P])
        flip = sb("flip", [P, P])
        mask_f = sb("mask_f", [P, P])
        mask_b = sb("mask_b", [P, P])
        iota_i = sb("iota_i", [P, P], I32)
        iota = sb("iota", [P, P])
        ssq = sb("ssq", [P, NT])
        rstd = sb("rstd", [P, NT])
        slotT = sb("slotT", [P, 3, S + 4])
        hots = sb("hots", [P, 2, 2, 4, P])
        stage = sb("stage", [P, 2, 2 * S])
        slotv = hots[:].rearrange("p a b c k -> p (a b c k)")[:, 0:3 * NT * SLOTS].rearrange(
            "p (a t k) -> p a t k", a=3, t=NT)
        lam = sb("lam", [P, 8])

        def area(at, *shape, dt=F32):
            n = int(np.prod(shape))
            v = big[:, at:at + n]
            if dt != F32:
                v = v.bitcast(dt)
            names = "abcd"[:len(shape)]
            if len(shape) > 1:
                v = v.rearrange(f"p ({' '.join(names)}) -> p {' '.join(names)}",
                                **{k: s for k, s in zip(names, shape)})
            return v

        G = area(0, NKEYS, S)
        xn = area(0, NT, D)
        qkT = area(2048, KD, S)
        v_ml = area(4096, NT, HEADS, P + 1)
        so = area(6160, NT, D)
        hs = area(8208, NT, HEADS, P)
        e_ml = area(10256, 2, 2, 512)
        p_ml = area(12304, 2, 2, 512)
        sq = area(14352, NT, D)
        gsb = area(16400, NT, 32)
        lgate = area(16464, NT, 4, 16)
        ftmp = area(16592, 3, NT, 2, HEADS)
        rows = area(16688, 5, S)
        colC = area(17968, NT, 48)
        colD = area(18064, NT, 48)
        zrow = area(18160, S)
        den = area(18416, 2, 2, NT)
        hss = area(18424, NT, HEADS)
        QK = area(2048, NT, 2 * D)
        v_da = area(6144, NT, D)
        qkT_da = area(8192, 16, S)
        sq_da = area(12288, NT, 2 * D)
        e_da = area(16384, 2, 2, S)
        e1_da = area(17408, S)
        a_da = area(17664, 2, S)
        aT_da = area(18176, 2, NT, P)
        o_da = area(18688, NT, HEADS, P)
        gss = area(20736, NT, 32)
        trig = area(20800, 12, NT, ROPE_HALF)
        rt = area(20992, 4, 32, ROPE_HALF)
        zz = area(22016, 16, 4)
        mx = area(22080, 16, 2)
        trig_i = area(22112, NT, ROPE_HALF, dt=I32)
        ROUTE_J = 80
        qT = area(14336, 16, S)
        r0 = ROUTE_J * S
        val = area(r0, NT, 16, TOPK)
        idx = area(r0 + 512, NT, 16, TOPK, dt=U32)
        idxf = area(r0 + 1024, NT, 16, TOPK)
        topv = area(r0 + 1536, NT, HEADS, TOPK)
        topp = area(r0 + 1792, NT, HEADS * TOPK, dt=U32)
        digit = area(r0 + 2048, 2, NT, SLOTS, dt=U32)
        digitf = area(r0 + 2560, 2, NT, SLOTS)
        zsum = area(r0 + 3072, NT, HEADS)
        cand = area(24576, NT, HEADS, TOPK * TOPK)
        sc = area(28672, NT, 16, NKEYS)
        eq = area(28672, NT, SLOTS, TOPK)

        landed = [sem(f"landed{r}") for r in range(RING)]
        pair_used = sem("pair_used")
        loaded_x = sem("loaded_x")
        loaded_small = sem("loaded_small")
        loaded_keys = [sem("loaded_keys0"), sem("loaded_keys1")]
        stored = sem("stored")
        consts = sem("consts")
        dve_step = sem("dve_step")
        act_step = sem("act_step")
        x_ready = sem("x_ready")
        ssq_ready = sem("ssq_ready")
        var_ready = sem("var_ready")
        std_ready = sem("std_ready")
        xn_ready = sem("xn_ready")
        xT_ready = sem("xT_ready")
        hT_ready = sem("hT_ready")
        gate_mm = sem("gate_mm")
        fabs_ready = sem("fabs_ready")
        softplus_ready = sem("softplus_ready")
        lgate_ready = sem("lgate_ready")
        rows_mm = sem("rows_mm")
        negm_ready = sem("negm_ready")
        em_ready = sem("em_ready")
        amrow_ready = sem("amrow_ready")
        cols_mm = sem("cols_mm")
        colC_ready = sem("colC_ready")
        flip_mm = sem("flip_mm")
        colD_ready = sem("colD_ready")
        qk_mm = sem("qk_mm")
        qk_out = sem("qk_out")
        vo_mm = sem("vo_mm")
        v_out = sem("v_out")
        o_out = sem("o_out")
        se_mm = sem("se_mm")
        e_ready = sem("e_ready")
        p_ready = sem("p_ready")
        av_mm = sem("av_mm")
        den_ready = sem("den_ready")
        hf_ready = sem("hf_ready")
        hs_ready = sem("hs_ready")
        sq_ready = sem("sq_ready")
        hvar_ready = sem("hvar_ready")
        hstd_ready = sem("hstd_ready")
        wo_mm = sem("wo_mm")
        wq_mm = sem("wq_mm")
        wq_out_a = sem("wq_out_a")
        wq_out_v = sem("wq_out_v")
        score_mm = sem("score_mm")
        score_out = sem("score_out")
        lo_bank_free = sem("lo_bank_free")
        hi_bank_free = sem("hi_bank_free")
        gelu_done = sem("gelu_done")
        top_ready = sem("top_ready")
        exp_ready = sem("exp_ready")
        slots_ready = sem("slots_ready")
        slots_mm = sem("slots_mm")
        hot_ready = sem("hot_ready")
        w_mm = sem("w_mm")
        stage_ready = sem("stage_ready")
        trig_step = sem("trig_step")
        lam_ready = sem("lam_ready")
        qkv_mm = sem("qkv_mm")
        qkv_out_a = sem("qkv_out_a")
        qkv_out_v = sem("qkv_out_v")
        qkn_ready = sem("qkn_ready")
        qkt_mm = sem("qkt_mm")
        qkt_out = sem("qkt_out")
        s_mm = sem("s_mm")
        mx_ready = sem("mx_ready")
        pe_ready = sem("pe_ready")
        rz_ready = sem("rz_ready")
        e1_ready = sem("e1_ready")
        a_ready = sem("a_ready")
        aT_mm = sem("aT_mm")
        aT_out = sem("aT_out")
        o_mm = sem("o_mm")
        o_got = sem("o_got")

        pair_of = {}
        at = 0
        for name, n in (("qk", U_QK), ("vo", U_VO), ("wo0", U_WO), ("wq0", U_WQ), ("u0", U_E), ("v0", U_E),
                        ("qkv", U_QKV), ("wo1", U_WO), ("wq1", U_WQ), ("u1", U_E), ("v1", U_E)):
            pair_of[name] = at
            at += n // 2
        X_AFTER = {2: 4, 3: 8, 5: 12}
        TOKENS4 = S // 4
        LO = 4 + U_E // 2
        HI = 4 + 2 + TOKENS4

        def columns_made(eng, done, part, u, before=0):
            if u % 2 == 0:
                eng.wait_ge(done, before + u // 2 + 1)
            else:
                eng.wait_ge(pair_used, pair_of[part] + u // 2 + 1)

        def tokens_made(eng, done, part, nb, t, before=0):
            if t == 0:
                eng.wait_ge(done, before + nb + 1)
            else:
                eng.wait_ge(pair_used, pair_of[part] + 2 * nb + 2)

        block = ctx.enter_context(nc.Block())

        @block.sync
        def _(sp):
            sp.dma_start(x[:], x_in).then_inc(loaded_x, 16)
            for r in range(RING):
                sp.dma_start(ring[:, r, :], stream[r]).then_inc(landed[r], 16)
            with sp.Fori(1, PAIRS // RING) as turn:
                for r in range(RING):
                    sp.wait_ge(pair_used, RING * turn + (r + 1 - RING))
                    sp.dma_start(ring[:, r, :],
                                 stream[bass.ds(RING * turn + r, 1)].rearrange("a p f -> (a p) f")
                                 ).then_inc(landed[r], 16)
            for t in range(NT):
                sp.wait_ge(x_ready, 16)
                sp.dma_start(out[t], x[:, t, :]).then_inc(stored, 16)
            sp.wait_ge(stored, 16 * NT)

        @block.gpsimd
        def _(pool):
            pool.memset(ident[:], 0.0).then_inc(consts, 1)
            pool.memset(flip[:], 0.0).then_inc(consts, 1)
            pool.memset(mask_f[:], 0.0).then_inc(consts, 1)
            pool.memset(mask_b[:], 0.0).then_inc(consts, 1)
            pool.wait_ge(consts, 4)
            pool.affine_select(out=ident[:], in_=ident[:], compare_op=ALU.not_equal, fill=1.0, base=0,
                               pattern=[[-1, P]], channel_multiplier=1).then_inc(consts, 1)
            pool.affine_select(out=flip[:], in_=flip[:], compare_op=ALU.not_equal, fill=1.0, base=1 - P,
                               pattern=[[1, P]], channel_multiplier=1).then_inc(consts, 1)
            pool.affine_select(out=mask_f[:], in_=mask_f[:], compare_op=ALU.is_ge, fill=NEG, base=0,
                               pattern=[[1, P]], channel_multiplier=-1).then_inc(consts, 1)
            pool.affine_select(out=mask_b[:], in_=mask_b[:], compare_op=ALU.is_ge, fill=NEG, base=0,
                               pattern=[[-1, P]], channel_multiplier=1).then_inc(consts, 1)
            pool.iota(iota_i[:], pattern=[[1, P]], base=0, channel_multiplier=0).then_inc(consts, 1)
            pool.wait_ge(consts, 9)
            pool.tensor_copy(iota[:], iota_i[:]).then_inc(consts, 1)
        CONSTS = 10

        @block.scalar
        def _(act):
            steps = [0]

            def chain(ins):
                steps[0] += 1
                ins.then_inc(act_step, 1)
                act.wait_ge(act_step, steps[0])

            act.dma_start(sm[:], small).then_inc(loaded_small, 16)
            act.dma_start(wg[:], w_gates).then_inc(loaded_small, 16)
            act.dma_start(pos_i[:], positions).then_inc(loaded_small, 16)
            act.dma_start(keysT[:], keys0).then_inc(loaded_keys[0], 16)

            def norm(n, k):
                if n == 0:
                    act.wait_ge(loaded_x, 16)
                else:
                    act.wait_ge(x_ready, X_AFTER[n])
                for t in range(NT):
                    act.activation(xn[:, t, :], x[:, t, :], ACT.Square, accum_out=ssq[:, t:t + 1]
                                   ).then_inc(ssq_ready, 1)
                act.wait_ge(var_ready, k + 1)
                act.activation(rstd[:], ssq[:], ACT.Sqrt).then_inc(std_ready, 1)

            def transposed(n, scale):
                act.wait_ge(loaded_small, 48)
                for b in (0, 2):
                    act.wait_ge(xT_ready, 4 * n + b + 1)
                    for kd in (2 * b, 2 * b + 1):
                        act.activation(hT[:, kd, :], ps[:, b, (kd % 2) * S:(kd % 2 + 1) * S], ACT.Copy,
                                       scale=scale(kd)).then_inc(hT_ready, 1)

            def gain(g):
                return lambda kd: sm[:, SM_GAIN + g * KD + kd:SM_GAIN + g * KD + kd + 1]

            norm(0, 0)
            transposed(0, gain(0))
            act.wait_ge(fabs_ready, 1)
            chain(act.activation(ftmp[:, 1], ftmp[:, 0], ACT.Exp, scale=-1.0))
            act.activation(ftmp[:, 2], ftmp[:, 1], ACT.Ln, bias=1.0).then_inc(softplus_ready, 1)
            for u in range(U_QK):
                columns_made(act, qk_mm, "qk", u)
                act.activation(qkT[:, u, :], ps[:, 4 + u % 3, 0:S], ACT.Copy,
                               scale=ML_SCALE if u < 4 else 1.0).then_inc(qk_out, 1)
            act.wait_ge(negm_ready, 1)
            act.activation(rows[0:16, 2, :], rows[0:16, 3, :], ACT.Exp, scale=-1.0).then_inc(em_ready, 1)
            for nb in (2, 3):
                for t in range(NT):
                    tokens_made(act, vo_mm, "vo", nb, t)
                    act.activation(so[:, t, (nb - 2) * 512:(nb - 1) * 512], ps[:, 2 * (nb % 2) + t, :],
                                   ACT.Sigmoid).then_inc(o_out, 1)
            act.wait_ge(colC_ready, 1)
            act.wait_ge(colD_ready, 1)

            def ml_exp(h):
                act.wait_ge(se_mm, h + 1)
                if h >= 2:
                    act.wait_ge(p_ready, h - 1)
                af, ab = colC, colD
                act.activation(e_ml[:, h % 2, 0, 0:S], ps[:, 2, 0:S], ACT.Exp, bias=af[:, 0, h:h + 1])
                act.activation(e_ml[:, h % 2, 0, 384:512], ps[:, 2, 384:512], ACT.Exp, bias=af[:, 1, h:h + 1])
                act.activation(e_ml[:, h % 2, 1, 0:P], ps[:, 3, 0:P], ACT.Exp, bias=ab[:, 0, 8 + h:9 + h])
                act.activation(e_ml[:, h % 2, 1, S:512], ps[:, 3, S:512], ACT.Exp,
                               bias=ab[:, 1, 8 + h:9 + h]).then_inc(e_ready, 1)

            def ml_forward(h):
                act.wait_ge(den_ready, h + 1)
                for t in range(NT):
                    act.activation(hs[:, t, h, :], ps[:, 4 + 2 * (h % 2), t * 129:t * 129 + P], ACT.Copy,
                                   scale=den[:, h % 2, 0, t:t + 1]).then_inc(hf_ready, 1)

            for h in range(HEADS):
                ml_exp(h)
                if h >= 1:
                    ml_forward(h - 1)
            ml_forward(HEADS - 1)
            for t in range(NT):
                act.wait_ge(hs_ready, 2 * HEADS)
                act.activation(sq[:, t, :], hs[:, t].rearrange("p h d -> p (h d)"), ACT.Square
                               ).then_inc(sq_ready, 1)
            act.wait_ge(hvar_ready, 1)
            act.activation(hss[:], hss[:], ACT.Sqrt).then_inc(hstd_ready, 1)
            transposed(1, gain(4))

            def ffn(l):
                n = (2, 5)[l]
                norm(n, (1, 3)[l])
                transposed(n, gain((1, 3)[l]))
                if l == 1:
                    pass
                for u in range(0, U_WQ, 2):
                    columns_made(act, wq_mm, f"wq{l}", u, U_WQ // 2 * l)
                    act.activation(qT[:, u, :], ps[:, 4 + u % 4, 0:S], ACT.Copy).then_inc(wq_out_a, 1)
                for b in range(8):
                    act.wait_ge(score_mm, 8 * l + b + 1)
                    act.activation(sc[:, b // 4, (b % 4) * 4:(b % 4) * 4 + 4, :].rearrange("p a n -> p (a n)"),
                                   ps[:, b, :], ACT.Copy).then_inc(lo_bank_free if b < 4 else hi_bank_free, 1)

                def gelus(first, last):
                    with act.Fori(first // RING, last // RING) as turn:
                        for r in range(RING):
                            act.wait_ge(pair_used, RING * turn + (pair_of[f"u{l}"] + r + 1))
                            act.activation(G[:, bass.ds(8 * turn + 2 * r, 2), :].rearrange("p j t -> p (j t)"),
                                           ps[:, r, :], ACT.Gelu).then_inc(lo_bank_free, 1)

                gelus(0, ROUTE_J // 2)
                act.wait_ge(top_ready, l + 1)
                act.activation(topv[:], topv[:], ACT.Exp).then_inc(exp_ready, 1)
                act.wait_ge(slots_ready, l + 1)
                gelus(ROUTE_J // 2, U_E // 2)
                act.wait_ge(hi_bank_free, HI * (l + 1))
                base = pair_of[f"v{l}"]
                with act.Fori(0, U_E // 2 // RING) as turn:
                    for r in range(RING):
                        act.wait_ge(pair_used, RING * turn + (base + r - 1))
                        act.activation(stage[:, r % 2, :],
                                       G[:, bass.ds(8 * turn + 2 * r, 2), :].rearrange("p j t -> p (j t)"),
                                       ACT.Copy).then_inc(stage_ready, 1)

            ffn(0)
            act.wait_ge(score_mm, 8)
            act.dma_start(keysT[:], keys1).then_inc(loaded_keys[1], 16)
            norm(3, 2)
            transposed(3, gain(2))
            act.wait_ge(trig_step, 1)
            act.activation(trig[:, 6:8], trig[:, 4:6], ACT.Sin).then_inc(trig_step, 1)
            act.wait_ge(lam_ready, 1)
            act.activation(lam[:, 2:4], lam[:, 0:2], ACT.Exp).then_inc(lam_ready, 1)
            for nb in range(6):
                tokens_made(act, qkv_mm, "qkv", nb, 1)
                dst = QK[:, 1, nb * 512:(nb + 1) * 512] if nb < 4 else v_da[:, 1, (nb - 4) * 512:(nb - 3) * 512]
                act.activation(dst, ps[:, 2 * (nb % 2) + 1, :], ACT.Copy).then_inc(qkv_out_a, 1)
            for t in range(NT):
                if t == 0:
                    act.wait_ge(qkv_out_v, 6)
                else:
                    act.wait_ge(qkv_out_a, 6)
                act.activation(sq_da[:, t, :], QK[:, t, :], ACT.Square).then_inc(sq_ready, 1)
            act.wait_ge(hvar_ready, 2)
            act.activation(gss[:], gss[:], ACT.Sqrt).then_inc(hstd_ready, 1)
            for b in range(8):
                act.wait_ge(qkt_mm, b + 1)
                act.activation(qkT_da[:, 2 * b:2 * b + 2, :].rearrange("p a t -> p (a t)"), ps[:, b, :], ACT.Copy
                               ).then_inc(qkt_out, 1)

            def da_exp(n):
                act.wait_ge(mx_ready, n + 1)
                for c in range(2):
                    act.activation(e_da[:, n % 2, c, :], ps[:, 2 * (n % 2) + c, 0:S], ACT.Exp, scale=DA_SCALE,
                                   bias=mx[:, n, c:c + 1], accum_out=zz[:, n, c:c + 1]).then_inc(pe_ready, 1)

            def da_second(n):
                act.wait_ge(rz_ready, n + 1)
                if n >= 1:
                    act.wait_ge(a_ready, n)
                act.activation(e1_da[:], e_da[:, n % 2, 1, :], ACT.Copy, scale=zz[:, n, 3:4]).then_inc(e1_ready, 1)

            def da_out(n):
                act.wait_ge(aT_mm, n + 1)
                act.activation(aT_da[:, n % 2].rearrange("p a t -> p (a t)"), ps[:, 4 + n % 2, 0:S], ACT.Copy
                               ).then_inc(aT_out, 1)

            for n in range(16):
                da_exp(n)
                if n >= 1:
                    da_out(n - 1)
                da_second(n)
            da_out(15)
            act.wait_ge(o_got, 16)
            for t in range(NT):
                act.activation(sq[:, t, :], o_da[:, t].rearrange("p h d -> p (h d)"), ACT.Square
                               ).then_inc(sq_ready, 1)
            act.wait_ge(hvar_ready, 3)
            act.activation(hss[:], hss[:], ACT.Sqrt).then_inc(hstd_ready, 1)
            transposed(4, lambda kd: lam[:, 6:7])
            ffn(1)

        @block.vector
        def _(dve):
            steps = [0]

            def chain(ins):
                steps[0] += 1
                ins.then_inc(dve_step, 1)
                dve.wait_ge(dve_step, steps[0])

            def norm(n, k):
                dve.wait_ge(ssq_ready, 2 * k + 2)
                dve.tensor_scalar(ssq[:], ssq[:], 1.0 / D, EPS, ALU.mult, ALU.add).then_inc(var_ready, 1)
                dve.wait_ge(std_ready, k + 1)
                chain(dve.reciprocal(ssq[:], rstd[:]))
                for t in range(NT):
                    dve.tensor_scalar(xn[:, t, :], x[:, t, :], ssq[:, t:t + 1], None, ALU.mult
                                      ).then_inc(xn_ready, 1)

            def transposed(n, scale):
                for b in (1, 3):
                    dve.wait_ge(xT_ready, 4 * n + b + 1)
                    for kd in (2 * b, 2 * b + 1):
                        dve.tensor_scalar(hT[:, kd, :], ps[:, b, (kd % 2) * S:(kd % 2 + 1) * S], scale(kd), None,
                                          ALU.mult).then_inc(hT_ready, 1)

            def gain(g):
                return lambda kd: sm[:, SM_GAIN + g * KD + kd:SM_GAIN + g * KD + kd + 1]

            def add_to_x(l):
                for nb in range(2):
                    for t in range(NT):
                        tokens_made(dve, wo_mm, f"wo{l}", nb, t, 2 * l)
                        dve.tensor_tensor(x[:, t, nb * 512:(nb + 1) * 512], x[:, t, nb * 512:(nb + 1) * 512],
                                          ps[:, 2 * nb + t, :], ALU.add).then_inc(x_ready, 1)

            def head_norm(y, sq_v, k, sq_at, gated):
                for t in range(NT):
                    dve.wait_ge(sq_ready, sq_at + t + 1)
                    chain(dve.tensor_reduce(hss[:, t, :], sq_v[:, t, :].rearrange("p (h d) -> p h d", h=HEADS),
                                            AX, ALU.add))
                dve.tensor_scalar(hss[:], hss[:], 1.0 / P, EPS, ALU.mult, ALU.add).then_inc(hvar_ready, 1)
                dve.wait_ge(hstd_ready, k)
                chain(dve.reciprocal(hss[:], hss[:]))
                for t in range(NT):
                    r = hss[:, t, :].unsqueeze(2).to_broadcast([P, HEADS, P])
                    m = dve.tensor_tensor(xn[:, t, :].rearrange("p (h d) -> p h d", h=HEADS), y[:, t], r, ALU.mult)
                    if gated:
                        chain(m)
                        dve.wait_ge(o_out, 4)
                        m = dve.tensor_tensor(xn[:, t, :], xn[:, t, :], so[:, t, :], ALU.mult)
                    m.then_inc(xn_ready, 1)

            norm(0, 0)
            dve.wait_ge(loaded_small, 48)
            transposed(0, gain(0))
            dve.memset(v_ml[:, :, :, P:P + 1], 1.0)
            dve.memset(zrow[0:16, :], 0.0)
            dve.memset(slotT[:], 0.0)
            chain(dve.memset(lgate[:], 0.0))
            dve.wait_ge(gate_mm, 1)
            chain(dve.tensor_tensor(gsb[:], ps[:, 7, 0:NT * 32].rearrange("p (t g) -> p t g", t=NT),
                                    sm[:, SM_BGATE:SM_BGATE + 32].unsqueeze(1).to_broadcast([P, NT, 32]), ALU.add))
            g4 = gsb[:].rearrange("p t (d k h) -> p t d k h", d=2, k=2)
            for t in range(NT):
                i = dve.scalar_tensor_tensor(out=ftmp[:, 0, t], in0=g4[:, t, :, 1, :], scalar=-1.0,
                                             in1=g4[:, t, :, 1, :], op0=ALU.mult, op1=ALU.max)
            i.then_inc(fabs_ready, 1)
            dve.tensor_copy(lgate[:, :, 0, 0:8], g4[:, :, 0, 0, :])
            dve.tensor_copy(lgate[:, :, 1, 8:16], g4[:, :, 1, 0, :])
            dve.wait_ge(softplus_ready, 1)
            for d in range(2):
                i = dve.scalar_tensor_tensor(out=lgate[:, :, 2 + d, 8 * d:8 * d + 8], in0=g4[:, :, d, 1, :], scalar=0.0,
                                             in1=ftmp[:, 2, :, d, :], op0=ALU.min, op1=ALU.subtract)
            i.then_inc(lgate_ready, 1)
            dve.wait_ge(rows_mm, 1)
            chain(dve.tensor_copy(rows[0:16, 3:5, :], ps[0:16, 7, :].rearrange("p (a t) -> p a t", a=2)))
            chain(dve.tensor_tensor_scan(rows[0:16, 2, :], rows[0:16, 4, :], zrow[0:16, :], 0.0, ALU.add, ALU.add))
            chain(dve.tensor_tensor(rows[0:16, 0, :], rows[0:16, 3, :], rows[0:16, 2, :], ALU.subtract))
            chain(dve.tensor_tensor_scan(rows[0:16, 1, :], rows[0:16, 0, :], rows[0:16, 0, :], NEG, ALU.max, ALU.max))
            chain(dve.tensor_tensor(rows[0:16, 3, :], rows[0:16, 2, :], rows[0:16, 1, :], ALU.add))
            dve.tensor_scalar(rows[0:16, 1, :], rows[0:16, 1, :], -1.0, None, ALU.mult).then_inc(negm_ready, 1)
            for nb in range(2):
                for t in range(NT):
                    tokens_made(dve, vo_mm, "vo", nb, t)
                    dve.tensor_copy(v_ml[:, t, 4 * nb:4 * nb + 4, 0:P],
                                    ps[:, 2 * nb + t, :].rearrange("p (h d) -> p h d", h=4)).then_inc(v_out, 1)
            dve.wait_ge(cols_mm, 1)
            dve.tensor_copy(colC[:], ps[:, 7, 0:96].rearrange("p (t c) -> p t c", t=NT)).then_inc(colC_ready, 1)
            dve.wait_ge(flip_mm, 1)
            dve.tensor_copy(colD[:], ps[:, 7, 0:96].rearrange("p (t c) -> p t c", t=NT)).then_inc(colD_ready, 1)
            dve.wait_ge(colC_ready, 1)
            dve.wait_ge(colD_ready, 1)

            def ml_weights(h):
                dve.wait_ge(e_ready, h + 1)
                if h >= 2:
                    dve.wait_ge(av_mm, h - 1)
                sp_, e, p = ps[:, h % 2, :], e_ml[:, h % 2], p_ml[:, h % 2]
                for d, a, b in ((0, 0, 256), (0, 384, 512), (1, 0, 128), (1, 256, 512)):
                    i = dve.tensor_tensor(p[:, d, a:b], sp_[:, a:b], e[:, d, a:b], ALU.mult)
                i.then_inc(p_ready, 1)

            def ml_output(h):
                dve.wait_ge(av_mm, h + 1)
                if h >= 2:
                    dve.wait_ge(hf_ready, 2 * h - 2)
                b = 4 + 2 * (h % 2)
                for d, col in ((0, colC), (1, colD)):
                    o = ps[:, b + d, 0:258].rearrange("p (t c) -> p t c", t=NT)
                    i = dve.scalar_tensor_tensor(out=den[:, h % 2, d, :].unsqueeze(2), in0=o[:, :, P:P + 1],
                                                 scalar=-1.0, in1=col[:, :, 32 + 8 * d + h:33 + 8 * d + h],
                                                 op0=ALU.mult, op1=ALU.max)
                chain(i)
                for d in range(2):
                    o = ps[:, b + d, 0:258].rearrange("p (t c) -> p t c", t=NT)
                    dv = den[:, h % 2, d, :].unsqueeze(2)
                    i = dve.tensor_tensor(dv, o[:, :, P:P + 1], dv, ALU.max)
                chain(i)
                dve.reciprocal(den[:, h % 2], den[:, h % 2]).then_inc(den_ready, 1)
                dve.wait_ge(den_ready, h + 1)
                for t in range(NT):
                    dve.wait_ge(hf_ready, 2 * h + t + 1)
                    dve.scalar_tensor_tensor(out=hs[:, t, h, :], in0=ps[:, b + 1, t * 129:t * 129 + P],
                                             scalar=den[:, h % 2, 1, t:t + 1], in1=hs[:, t, h, :],
                                             op0=ALU.mult, op1=ALU.add).then_inc(hs_ready, 1)

            for h in range(HEADS):
                ml_weights(h)
                if h >= 1:
                    ml_output(h - 1)
            ml_output(HEADS - 1)
            head_norm(hs, sq, 1, 0, True)
            transposed(1, gain(4))
            add_to_x(0)

            def ffn(l):
                n = (2, 5)[l]
                norm(n, (1, 3)[l])
                transposed(n, gain((1, 3)[l]))
                for u in range(1, U_WQ, 2):
                    columns_made(dve, wq_mm, f"wq{l}", u)
                    dve.tensor_copy(qT[:, u, :], ps[:, 4 + u % 4, 0:S]).then_inc(wq_out_v, 1)
                dve.wait_ge(lo_bank_free, LO * l + 4)
                dve.wait_ge(hi_bank_free, HI * l + 4)

                def top16(rows_, values, places):
                    for r, v, p_ in zip(rows_, values, places):
                        i = dve.max(v[:, 0:8], r)
                    chain(i)
                    for r, v, p_ in zip(rows_, values, places):
                        i = dve.max_index(p_[:, 0:8], v[:, 0:8], r)
                    chain(i)
                    for r, v, p_ in zip(rows_, values, places):
                        i = dve.match_replace(r, v[:, 0:8], r, -3e38)
                    chain(i)
                    for r, v, p_ in zip(rows_, values, places):
                        i = dve.max(v[:, 8:16], r)
                    chain(i)
                    for r, v, p_ in zip(rows_, values, places):
                        i = dve.max_index(p_[:, 8:16], v[:, 8:16], r)
                    chain(i)

                for t in range(NT):
                    for a in range(0, 16, 4):
                        g = range(a, a + 4)
                        top16([sc[:, t, q, :] for q in g], [val[:, t, q, :] for q in g], [idx[:, t, q, :] for q in g])
                    v2 = val[:, t].rearrange("p (h s) k -> p h s k", s=2)
                    chain(dve.tensor_tensor(cand[:, t].rearrange("p h (a b) -> p h a b", a=TOPK),
                                            v2[:, :, 0, :].unsqueeze(3).to_broadcast([P, HEADS, TOPK, TOPK]),
                                            v2[:, :, 1, :].unsqueeze(2).to_broadcast([P, HEADS, TOPK, TOPK]), ALU.add))
                    for a in range(0, HEADS, 4):
                        g = range(a, a + 4)
                        top16([cand[:, t, q, :] for q in g], [topv[:, t, q, :] for q in g],
                              [topp[:, t, q * TOPK:(q + 1) * TOPK] for q in g])
                gate = slotv[:, 2].rearrange("p t (h k) -> p t h k", h=HEADS)
                chain(dve.tensor_copy(zsum[:], topv[:, :, :, 0]))
                dve.tensor_tensor(topv[:], topv[:], zsum[:].unsqueeze(3).to_broadcast([P, NT, HEADS, TOPK]),
                                  ALU.subtract).then_inc(top_ready, 1)
                dve.tensor_copy(idxf[:], idx[:])
                dve.tensor_scalar(digit[:, 0], topp[:], 4, None, ALU.logical_shift_right)
                chain(dve.tensor_scalar(digit[:, 1], topp[:], 15, None, ALU.bitwise_and))
                chain(dve.tensor_copy(digitf[:], digit[:]))
                for s in range(2):
                    for t in range(NT):
                        chain(dve.tensor_tensor(eq[:, t],
                                                digitf[:, s, t].unsqueeze(2).to_broadcast([P, SLOTS, TOPK]),
                                                iota[:, 0:TOPK].unsqueeze(1).to_broadcast([P, SLOTS, TOPK]),
                                                ALU.is_equal))
                        e4 = eq[:, t].rearrange("p (h k) a -> p h k a", h=HEADS)
                        src = idxf[:, t].rearrange("p (h s) k -> p h s k", s=2)[:, :, s, :]
                        chain(dve.tensor_tensor(e4, e4, src.unsqueeze(2).to_broadcast([P, HEADS, TOPK, TOPK]), ALU.mult))
                        chain(dve.tensor_reduce(slotv[:, s, t], eq[:, t], AX, ALU.add))
                dve.wait_ge(exp_ready, l + 1)
                chain(dve.tensor_reduce(zsum[:], topv[:], AX, ALU.add))
                chain(dve.reciprocal(zsum[:], zsum[:]))
                dve.tensor_tensor(gate, topv[:], zsum[:].unsqueeze(3).to_broadcast([P, NT, HEADS, TOPK]),
                                  ALU.mult).then_inc(slots_ready, 1)
                dve.wait_ge(slots_mm, l + 1)
                dve.tensor_copy(slotT[:, 0:2, 0:S], ps[:, 4, :].rearrange("p (a t) -> p a t", a=2)
                                ).then_inc(hi_bank_free, 1)
                dve.tensor_copy(slotT[:, 2, 0:S], ps[:, 5, 0:S]).then_inc(hi_bank_free, 1)
                dve.wait_ge(hi_bank_free, HI * l + 6)

                def one_hots(slot, token0):
                    for k in range(4):
                        col = token0 + k
                        dve.tensor_scalar(hots[:, slot, 0, k, :], iota[:], slotT[:, 0, bass.ds(col, 1)],
                                          slotT[:, 2, bass.ds(col, 1)], ALU.is_equal, ALU.mult)
                        i = dve.tensor_scalar(hots[:, slot, 1, k, :], iota[:], slotT[:, 1, bass.ds(col, 1)],
                                              None, ALU.is_equal)
                    i.then_inc(hot_ready, 1)

                one_hots(0, 0)
                dve.wait_ge(lo_bank_free, LO * (l + 1))
                with dve.Fori(0, TOKENS4 // 4) as turn:
                    for k in range(4):
                        one_hots((k + 1) % 2, 16 * turn + 4 * (k + 1))
                        dve.wait_ge(w_mm, 4 * turn + (TOKENS4 * l + k + 1))
                        g = G[:, :, bass.ds(16 * turn + 4 * k, 4)]
                        dve.tensor_tensor(g, g, ps[:, 4 + k, :].rearrange("p (t j) -> p j t", t=4), ALU.mult
                                          ).then_inc(hi_bank_free, 1)
                for t in range(NT):
                    for nb in range(2):
                        dve.wait_ge(pair_used, pair_of[f"v{l}"] + U_E // 2)
                        dve.tensor_copy(x[:, t, nb * 512:(nb + 1) * 512], ps[:, 2 * t + nb, :]).then_inc(x_ready, 1)

            ffn(0)
            norm(3, 2)
            transposed(3, gain(2))
            chain(dve.tensor_copy(trig[:, 0, :, 0], pos_i[:]))
            for k in range(ROPE_HALF):
                i = dve.tensor_scalar(trig[:, 1, :, k], trig[:, 0, :, 0], float(ROPE_INV[k]), None, ALU.mult)
            chain(i)
            chain(dve.tensor_scalar(trig[:, 2], trig[:, 1], 1.0 / TWO_PI, None, ALU.mult))
            chain(dve.tensor_copy(trig_i[:], trig[:, 2]))
            chain(dve.tensor_copy(trig[:, 2], trig_i[:]))
            for c in (PI_1, PI_2, PI_3):
                chain(dve.scalar_tensor_tensor(out=trig[:, 1], in0=trig[:, 2], scalar=-c, in1=trig[:, 1],
                                               op0=ALU.mult, op1=ALU.add))
            for sign, cmp in ((-1.0, ALU.is_gt), (1.0, ALU.is_lt)):
                chain(dve.tensor_scalar(trig[:, 3], trig[:, 1], -sign * float(np.pi), sign * TWO_PI, cmp, ALU.mult))
                chain(dve.tensor_tensor(trig[:, 1], trig[:, 1], trig[:, 3], ALU.add))
            chain(dve.tensor_scalar(trig[:, 2], trig[:, 1], float(np.pi / 2), None, ALU.add))
            chain(dve.tensor_scalar(trig[:, 3], trig[:, 2], float(np.pi), -TWO_PI, ALU.is_gt, ALU.mult))
            chain(dve.tensor_tensor(trig[:, 2], trig[:, 2], trig[:, 3], ALU.add))
            dve.tensor_scalar(trig[:, 4:6], trig[:, 1:3], PI_SAFE, -PI_SAFE, ALU.min, ALU.max).then_inc(trig_step, 1)
            lv = sm[:, SM_LAM:SM_LAM + 256].rearrange("p (a d) -> p a d", a=4)
            chain(dve.tensor_tensor(sq_da[:, 0, 0:128].rearrange("p (a d) -> p a d", a=2), lv[:, 0:4:2, :],
                                    lv[:, 1:4:2, :], ALU.mult))
            dve.tensor_reduce(lam[:, 0:2], sq_da[:, 0, 0:128].rearrange("p (a d) -> p a d", a=2), AX, ALU.add
                              ).then_inc(lam_ready, 1)
            dve.wait_ge(lam_ready, 2)
            chain(dve.tensor_tensor(lam[:, 4:5], lam[:, 3:4], lam[:, 2:3], ALU.subtract))
            chain(dve.tensor_scalar(lam[:, 5:6], lam[:, 4:5], LAMBDA_INIT, None, ALU.subtract))
            chain(dve.tensor_scalar(lam[:, 6:7], sm[:, SM_SUBLN:SM_SUBLN + 1], 1.0 - LAMBDA_INIT, None, ALU.mult))
            for nb in range(6):
                tokens_made(dve, qkv_mm, "qkv", nb, 0)
                dst = QK[:, 0, nb * 512:(nb + 1) * 512] if nb < 4 else v_da[:, 0, (nb - 4) * 512:(nb - 3) * 512]
                dve.tensor_copy(dst, ps[:, 2 * (nb % 2), :]).then_inc(qkv_out_v, 1)
            for t in range(NT):
                dve.wait_ge(sq_ready, 2 + t + 1)
                chain(dve.tensor_reduce(gss[:, t, :], sq_da[:, t, :].rearrange("p (g d) -> p g d", d=64), AX, ALU.add))
            dve.tensor_scalar(gss[:], gss[:], 1.0 / 64, EPS, ALU.mult, ALU.add).then_inc(hvar_ready, 1)
            dve.wait_ge(hstd_ready, 2)
            chain(dve.reciprocal(gss[:], gss[:]))
            dve.wait_ge(trig_step, 2)
            dve.wait_ge(qkv_out_v, 6)
            dve.wait_ge(qkv_out_a, 6)
            for t in range(NT):
                q3 = QK[:, t, :].rearrange("p (g d) -> p g d", d=64)
                q4 = QK[:, t, :].rearrange("p (a g d) -> p a g d", a=2, d=64)
                chain(dve.tensor_tensor(q3, q3, gss[:, t, :].unsqueeze(2).to_broadcast([P, 32, 64]), ALU.mult))
                gains = sm[:, SM_QG:SM_QG + 128].rearrange("p (a d) -> p a d", a=2)
                chain(dve.tensor_tensor(q4, q4, gains.unsqueeze(2).to_broadcast([P, 2, 16, 64]), ALU.mult))
                x1, x2 = q3[:, :, 0:8], q3[:, :, 8:16]
                sin_ = trig[:, 6, t].unsqueeze(1).to_broadcast([P, 32, 8])
                cos_ = trig[:, 7, t].unsqueeze(1).to_broadcast([P, 32, 8])
                dve.tensor_tensor(rt[:, 0], x1, cos_, ALU.mult)
                dve.tensor_tensor(rt[:, 1], x2, sin_, ALU.mult)
                dve.tensor_tensor(rt[:, 2], x2, cos_, ALU.mult)
                chain(dve.tensor_tensor(rt[:, 3], x1, sin_, ALU.mult))
                dve.tensor_tensor(x1, rt[:, 0], rt[:, 1], ALU.subtract)
                i = dve.tensor_tensor(x2, rt[:, 2], rt[:, 3], ALU.add)
                i.then_inc(qkn_ready, 1)
                dve.wait_ge(qkn_ready, t + 1)

            def da_max(n):
                dve.wait_ge(s_mm, n + 1)
                b = 2 * (n % 2)
                chain(dve.tensor_reduce(mx[:, n, :], ps[:, b:b + 2, 0:S], AX, ALU.max))
                dve.tensor_scalar(mx[:, n, :], mx[:, n, :], -DA_SCALE, None, ALU.mult).then_inc(mx_ready, 1)

            def da_sums(n):
                dve.wait_ge(pe_ready, 2 * n + 2)
                chain(dve.reciprocal(zz[:, n, 2:4], zz[:, n, 0:2]))
                dve.tensor_scalar(zz[:, n, 3:4], zz[:, n, 3:4], lam[:, 5:6], None, ALU.mult).then_inc(rz_ready, 1)
                dve.wait_ge(e1_ready, n + 1)
                if n >= 2:
                    dve.wait_ge(aT_mm, n - 1)
                dve.scalar_tensor_tensor(out=a_da[:, n % 2, :], in0=e_da[:, n % 2, 0, :], scalar=zz[:, n, 2:3],
                                         in1=e1_da[:], op0=ALU.mult, op1=ALU.add).then_inc(a_ready, 1)

            def da_got(n):
                dve.wait_ge(o_mm, n + 1)
                dve.tensor_copy(o_da[:, n % 2, n // 2, :], ps[:, 6 + n % 2, 0:P]).then_inc(o_got, 1)

            for n in range(16):
                da_max(n)
                if n >= 2:
                    da_got(n - 2)
                da_sums(n)
            da_got(14)
            da_got(15)
            head_norm(o_da, sq, 3, 4, False)
            dve.wait_ge(loaded_small, 48)
            transposed(4, lambda kd: lam[:, 6:7])
            add_to_x(1)
            ffn(1)

        @block.tensor
        def _(pe):
            def unit(r, k):
                return ring[:, r, k * UNIT:(k + 1) * UNIT]

            def arrived(pair):
                pe.wait_ge(landed[pair % RING], 16 * (pair // RING + 1))

            def transposes(n):
                for b in range(4):
                    for kd in (2 * b, 2 * b + 1):
                        for t in range(NT):
                            if b == 0:
                                pe.wait_ge(xn_ready, 2 * n + t + 1)
                            at_ = (kd % 2) * S + t * P
                            i = pe.transpose(ps[:, b, at_:at_ + P], xn[:, t, kd * P:(kd + 1) * P], ident[:])
                    i.then_inc(xT_ready, 1)
                pe.wait_ge(hT_ready, 8 * (n + 1))

            def by_columns(pair0, units, bank, done, before):
                for u in range(units):
                    pair = pair0 + u // 2
                    if u % 2 == 0:
                        arrived(pair)
                    before(u)
                    w = unit(pair % RING, u % 2).rearrange("p (k c) -> p k c", k=KD)
                    for kd in range(KD):
                        i = pe.matmul(ps[:, bank(u), 0:S], w[:, kd, :], hT[:, kd, :], start=(kd == 0),
                                      stop=(kd == KD - 1))
                    i.then_inc(done if u % 2 == 0 else pair_used, 1)

            def by_tokens(pair0, blocks, bank, done, before):
                for nb in range(blocks):
                    for q in range(4):
                        pair = pair0 + 2 * nb + q // 2
                        if q % 2 == 0:
                            arrived(pair)
                        w = unit(pair % RING, q % 2).rearrange("p (k c) -> p k c", k=2)
                        for t in range(NT):
                            if q == 0:
                                before(nb, t)
                            for k in range(2):
                                kd = 2 * q + k
                                i = pe.matmul(ps[:, bank(nb, t), :], hT[:, kd, t * P:(t + 1) * P], w[:, k, :],
                                              start=(kd == 0), stop=(kd == KD - 1))
                            if q == 3 and t == 0:
                                i.then_inc(done, 1)
                        if q % 2 == 1:
                            i.then_inc(pair_used, 1)

            pe.wait_ge(consts, CONSTS)
            transposes(0)
            pe.wait_ge(loaded_small, 48)
            for t in range(NT):
                for kd in range(KD):
                    i = pe.matmul(ps[:, 7, t * 32:(t + 1) * 32], hT[:, kd, t * P:(t + 1) * P], wg[:, kd, :],
                                  start=(kd == 0), stop=(kd == KD - 1))
            i.then_inc(gate_mm, 1)

            def qk_bank(u):
                if u >= 3:
                    pe.wait_ge(qk_out, u - 2)

            by_columns(pair_of["qk"], U_QK, lambda u: 4 + u % 3, qk_mm, qk_bank)
            pe.wait_ge(lgate_ready, 1)
            for k in range(2):
                for t in range(NT):
                    at_ = k * S + t * P
                    pe.matmul(ps[0:16, 7, at_:at_ + P], lgate[:, t, 2 * k, :], ident[:], start=True, stop=False)
                    i = pe.matmul(ps[0:16, 7, at_:at_ + P], lgate[:, 1 - t, 2 * k + 1, :], flip[:],
                                  start=False, stop=True)
            i.then_inc(rows_mm, 1)

            def vo_bank(nb, t):
                if nb == 2:
                    pe.wait_ge(v_out, t + 1)
                if nb == 3:
                    pe.wait_ge(v_out, 2 + t + 1)

            by_tokens(pair_of["vo"], 4, lambda nb, t: 2 * (nb % 2) + t, vo_mm, vo_bank)
            pe.wait_ge(em_ready, 1)
            for t in range(NT):
                for k in range(3):
                    at_ = t * 48 + k * 16
                    i = pe.matmul(ps[:, 7, at_:at_ + 16], rows[0:16, k, t * P:(t + 1) * P], ident[0:16, 0:16],
                                  start=True, stop=True)
            i.then_inc(cols_mm, 1)
            pe.wait_ge(colC_ready, 1)
            for t in range(NT):
                i = pe.matmul(ps[:, 7, t * 48:(t + 1) * 48], flip[:], colC[:, 1 - t, :], start=True, stop=True)
            i.then_inc(flip_mm, 1)
            pe.wait_ge(colD_ready, 1)
            pe.wait_ge(o_out, 4)
            pe.wait_ge(v_out, 4)
            pe.wait_ge(qk_out, U_QK)

            def ml_scores(h):
                if h >= 1:
                    pe.wait_ge(e_ready, h)
                if h >= 2:
                    pe.wait_ge(p_ready, h - 1)
                lo = (h % 2) * 64
                for s in range(NT):
                    pe.matmul(ps[:, h % 2, s * S:(s + 1) * S], qkT[lo:lo + 64, 4 + h // 2, s * P:(s + 1) * P],
                              qkT[lo:lo + 64, h // 2, :], start=True, stop=True)
                for b, col, c, blocks, m in ((2, colC, 16 + h, ((0, 0), (0, 1), (1, 1)), mask_f),
                                             (3, colD, 24 + h, ((0, 0), (1, 0), (1, 1)), mask_b)):
                    for s, t in blocks:
                        o = ps[:, b, s * S + t * P:s * S + (t + 1) * P]
                        i = pe.matmul(o, col[:, t, c:c + 1].to_broadcast([P, P]), ident[:], start=True, stop=(s != t))
                        if s == t:
                            i = pe.matmul(o, ident[:], m[:], start=False, stop=True)
                i.then_inc(se_mm, 1)

            def ml_values(h):
                pe.wait_ge(p_ready, h + 1)
                if h >= 2:
                    pe.wait_ge(hs_ready, 2 * h - 2)
                for d, sources in ((0, ((0,), (0, 1))), (1, ((0, 1), (1,)))):
                    for t in range(NT):
                        for s in sources[t]:
                            i = pe.matmul(ps[:, 4 + 2 * (h % 2) + d, t * 129:(t + 1) * 129],
                                          p_ml[:, h % 2, d, s * S + t * P:s * S + (t + 1) * P], v_ml[:, s, h, :],
                                          start=(s == sources[t][0]), stop=(s == sources[t][-1]))
                i.then_inc(av_mm, 1)

            ml_scores(0)
            for h in range(HEADS):
                if h + 1 < HEADS:
                    ml_scores(h + 1)
                ml_values(h)
            transposes(1)
            by_tokens(pair_of["wo0"], 2, lambda nb, t: 2 * nb + t, wo_mm, lambda nb, t: None)

            def ffn(l):
                transposes((2, 5)[l])

                def wq_bank(u):
                    if u >= 4:
                        pe.wait_ge((wq_out_a, wq_out_v)[u % 2], U_WQ // 2 * l + (u - 4) // 2 + 1)

                by_columns(pair_of[f"wq{l}"], U_WQ, lambda u: 4 + u % 4, wq_mm, wq_bank)
                pe.wait_ge(wq_out_a, U_WQ // 2 * (l + 1))
                pe.wait_ge(wq_out_v, U_WQ // 2 * (l + 1))
                pe.wait_ge(loaded_keys[l], 16)
                for t in range(NT):
                    for b in range(4):
                        for k in range(4):
                            q = 4 * b + k
                            i = pe.matmul(ps[:, 4 * t + b, k * P:(k + 1) * P], qT[:, q, t * P:(t + 1) * P],
                                          keysT[:, q, :], start=True, stop=True)
                        i.then_inc(score_mm, 1)
                base = pair_of[f"u{l}"]
                with pe.Fori(0, U_E // 2 // RING) as turn:
                    for r in range(RING):
                        pe.wait_ge(landed[r], 16 * turn + 16 * (base // RING + 1))
                        pe.wait_ge(lo_bank_free, RING * turn + (LO * l + r + 1))
                        for k in range(2):
                            w = unit(r, k).rearrange("p (k c) -> p k c", k=KD)
                            for kd in range(KD):
                                i = pe.matmul(ps[:, r, k * S:(k + 1) * S], w[:, kd, :], hT[:, kd, :],
                                              start=(kd == 0), stop=(kd == KD - 1))
                        i.then_inc(pair_used, 1)
                pe.wait_ge(slots_ready, l + 1)
                pe.wait_ge(hi_bank_free, HI * l + 4)
                for k in range(3):
                    for t in range(NT):
                        i = pe.transpose(ps[:, 4 + k // 2, (k % 2) * S + t * P:(k % 2) * S + (t + 1) * P],
                                         slotv[:, k, t, :], ident[:])
                i.then_inc(slots_mm, 1)
                pe.wait_ge(hi_bank_free, HI * l + 6)
                with pe.Fori(0, TOKENS4 // 4) as turn:
                    for b in range(4):
                        pe.wait_ge(hot_ready, 4 * turn + ((TOKENS4 + 1) * l + b + 1))
                        pe.wait_ge(hi_bank_free, 4 * turn + (HI * l + b + 3))
                        for k in range(4):
                            i = pe.matmul(ps[:, 4 + b, k * P:(k + 1) * P], hots[:, b % 2, 0, k, :],
                                          hots[:, b % 2, 1, k, :], start=True, stop=True)
                        i.then_inc(w_mm, 1)
                pe.wait_ge(lo_bank_free, LO * (l + 1))
                for t in range(NT):
                    for nb in range(2):
                        pe.matmul(ps[:, 2 * t + nb, :], ident[:], x[:, t, nb * 512:(nb + 1) * 512], start=True,
                                  stop=False, skip_group_check=True)
                base = pair_of[f"v{l}"]
                with pe.Fori(0, U_E // 2 // RING) as turn:
                    for r in range(RING):
                        pe.wait_ge(landed[r], 16 * turn + 16 * (base // RING + 1))
                        pe.wait_ge(stage_ready, RING * turn + (U_E // 2 * l + r + 1))
                        for k in range(2):
                            for t in range(NT):
                                for nb in range(2):
                                    i = pe.matmul(ps[:, 2 * t + nb, :],
                                                  stage[:, r % 2, k * S + t * P:k * S + (t + 1) * P],
                                                  unit(r, k)[:, nb * 512:(nb + 1) * 512], start=False, stop=False,
                                                  skip_group_check=True)
                        i.then_inc(pair_used, 1)

            ffn(0)
            transposes(3)

            def qkv_bank(nb, t):
                if nb >= 2:
                    pe.wait_ge((qkv_out_v, qkv_out_a)[t], nb - 1)

            by_tokens(pair_of["qkv"], 6, lambda nb, t: 2 * (nb % 2) + t, qkv_mm, qkv_bank)
            pe.wait_ge(qkn_ready, 2)
            for b in range(8):
                for k in range(2):
                    for t in range(NT):
                        q = 2 * b + k
                        i = pe.transpose(ps[:, b, k * S + t * P:k * S + (t + 1) * P], QK[:, t, q * P:(q + 1) * P],
                                         ident[:])
                i.then_inc(qkt_mm, 1)
            pe.wait_ge(qkt_out, 8)

            def da_scores(n):
                h, t = n // 2, n % 2
                if n >= 2:
                    pe.wait_ge(pe_ready, 2 * n - 2)
                for c in range(2):
                    i = pe.matmul(ps[:, 2 * (n % 2) + c, 0:S], qkT_da[64 * c:64 * c + 64, h, t * P:(t + 1) * P],
                                  qkT_da[64 * c:64 * c + 64, 8 + h, :], start=True, stop=True)
                i.then_inc(s_mm, 1)

            def da_turn(n):
                pe.wait_ge(a_ready, n + 1)
                if n >= 2:
                    pe.wait_ge(aT_out, n - 1)
                for k in range(NT):
                    i = pe.transpose(ps[:, 4 + n % 2, k * P:(k + 1) * P], a_da[:, n % 2, k * P:(k + 1) * P], ident[:])
                i.then_inc(aT_mm, 1)

            def da_values(n):
                pe.wait_ge(aT_out, n + 1)
                if n >= 2:
                    pe.wait_ge(o_got, n - 1)
                h = n // 2
                for k in range(NT):
                    i = pe.matmul(ps[:, 6 + n % 2, 0:P], aT_da[:, n % 2, k, :], v_da[:, k, h * P:(h + 1) * P],
                                  start=(k == 0), stop=(k == NT - 1))
                i.then_inc(o_mm, 1)

            for n in range(16 + 2):
                if n < 16:
                    da_scores(n)
                if 1 <= n <= 16:
                    da_turn(n - 1)
                if n >= 2:
                    da_values(n - 2)
            transposes(4)
            by_tokens(pair_of["wo1"], 2, lambda nb, t: 2 * nb + t, wo_mm, lambda nb, t: None)
            ffn(1)


def _by_columns(w):
    n = w.shape[1] // P
    return w.reshape(KD, P, n, P).transpose(2, 1, 0, 3).reshape(n, P, UNIT)


def _by_tokens(w):
    n = w.shape[1] // 512
    return w.reshape(4, 2, P, n, 512).transpose(3, 0, 2, 1, 4).reshape(4 * n, P, UNIT)


def _up(u):
    return u.reshape(NKEYS, NKEYS, KD, P).transpose(1, 3, 2, 0).reshape(NKEYS, P, UNIT)


def _down(v):
    return v.reshape(NKEYS, NKEYS, UNIT).transpose(1, 0, 2)


def kernel(**inputs):
    import concourse.bacc as bacc
    from concourse.bass_utils import run_bass_kernel_spmd

    a = {k: np.asarray(v) for k, v in inputs.items()}
    w_in, qkv = a["l0_w_in"], a["l1_w_qkv"]
    parts = [_by_columns(w_in[:, :D]), _by_tokens(w_in[:, D:3 * D]), _by_tokens(a["l0_w_out"]),
             _by_columns(a["l0_peer_wq"]), _up(a["l0_peer_u"]), _down(a["l0_peer_v"]),
             _by_tokens(qkv), _by_tokens(a["l1_w_out"]),
             _by_columns(a["l1_peer_wq"]), _up(a["l1_peer_u"]), _down(a["l1_peer_v"])]
    stream = np.empty((PAIRS, P, 2, UNIT), np.float32)
    at = 0
    for part in parts:
        n = len(part) // 2
        stream[at:at + n] = part.reshape(n, 2, P, UNIT).transpose(0, 2, 1, 3)
        at += n
    column = lambda g: g.reshape(-1, P).T
    all_rows = lambda g: np.broadcast_to(g.reshape(1, -1), (P, g.size))
    small = np.concatenate([column(a[k]) for k in ("l0_norm_mix", "l0_norm_ffn", "l1_norm_mix", "l1_norm_ffn",
                                                   "l0_head_norm", "l1_subln")]
                           + [all_rows(a[k]) for k in ("l0_b_gates", "l1_q_norm", "l1_k_norm", "l1_lambda_q1",
                                                       "l1_lambda_k1", "l1_lambda_q2", "l1_lambda_k2")], axis=1)
    keys = lambda k: np.ascontiguousarray(k.transpose(3, 0, 1, 2).reshape(P, 16, NKEYS))
    arrays = {
        "stream": stream.reshape(PAIRS, P, 2 * UNIT),
        "small": np.ascontiguousarray(small),
        "w_gates": np.ascontiguousarray(w_in[:, 3 * D:].reshape(KD, P, 32).transpose(1, 0, 2)),
        "keys0": keys(a["l0_peer_keys"]),
        "keys1": keys(a["l1_peer_keys"]),
        "positions": np.ascontiguousarray(a["positions"].reshape(NT, P).T),
        "x_in": np.ascontiguousarray(a["x"].reshape(NT, P, D).transpose(1, 0, 2)),
    }
    nc = bacc.Bacc("TRN2", target_bir_lowering=False, num_devices=1)
    aps = {k: nc.dram_tensor(k, v.shape, mybir.dt.from_np(v.dtype), kind="ExternalInput").ap()
           for k, v in arrays.items()}
    out = nc.dram_tensor("out", (NT, P, D), F32, kind="ExternalOutput").ap()
    program(nc, out=out, **aps)
    r = run_bass_kernel_spmd(nc, [arrays], core_ids=[0])
    return np.asarray(r.results[0]["out"]).reshape(1, S, D)
```

```python
from contextlib import ExitStack

import numpy as np

import concourse.bass as bass
from concourse import mybir

F32 = mybir.dt.float32
F32R = mybir.dt.float32r
F16 = mybir.dt.float16
BF16 = mybir.dt.bfloat16
U32 = mybir.dt.uint32
I32 = mybir.dt.int32
ALU = mybir.AluOpType
ACT = mybir.ActivationFunctionType
AX = mybir.AxisListType.X

P = 128
S = 256
D = 1024
NT = S // P
KD = D // P
HEADS = 8
EPS = 1e-6
NEG = -1e30
ML_DQK = 64
ML_SCALE = ML_DQK ** -0.5
DA_SCALE = 64 ** -0.5
LAMBDA_INIT = 0.8 - 0.6 * float(np.exp(-0.3))
ROPE_HALF = 8
ROPE_INV = (np.float32(500000.0) ** (-np.arange(ROPE_HALF, dtype=np.float32) * np.float32(2.0)
                                     / np.float32(16))).astype(np.float32)
TOPK = 16
NKEYS = 128
SLOTS = HEADS * TOPK
UNIT = 1024
RING = 4
AHEAD = RING - 1
HALF = NKEYS // 2
GROUP = 4
GATE_SCALE = 2.0 ** 14
TURN = 8

U_QK, U_VO, U_WO, U_WQ, U_E, U_QKV = 8, 16, 8, 16, NKEYS, 24
UNITS_0 = U_QK + U_VO + U_WO
UNITS_FFN = U_WQ + 2 * U_E
UNITS_1 = U_QKV + U_WO
UNITS = UNITS_0 + UNITS_FFN + UNITS_1 + UNITS_FFN

SM_GAIN = 0
SM_SUBLN = SM_GAIN + 5 * KD
SM_BGATE = SM_SUBLN + 1
SM_QG = SM_BGATE + 32
SM_LAM = SM_QG + 128
SM_COLS = SM_LAM + 256

TWO_PI = 2.0 * np.pi
PI_1 = 6.28125
PI_2 = float(np.float32(TWO_PI - PI_1))
PI_2 = float(np.array(np.array(PI_2, np.float32).view(np.uint32) & np.uint32(0xFFFFF000)).view(np.float32))
PI_3 = float(np.float32(TWO_PI - PI_1 - PI_2))
PI_SAFE = 3.1415925


def program(nc, stream, small, w_gates, keys0, keys1, positions, x_in, out):
    with ExitStack() as ctx:
        def sb(name, shape, dt=F32):
            return ctx.enter_context(nc.sbuf_tensor(name, shape, dt))

        def sem(name):
            return ctx.enter_context(nc.semaphore(name))

        ps = ctx.enter_context(nc.psum_tensor("ps", [P, 8, 512], F32))

        big = sb("big", [P, NKEYS * S])
        raw = sb("raw", [P, RING, UNIT])
        wh = sb("wh", [P, RING, UNIT], F32R)
        wl = sb("wl", [P, RING, UNIT], F32R)
        x = sb("x", [P, NT, D])
        hTh = sb("hTh", [P, KD, S], F32R)
        hTl = sb("hTl", [P, KD, S], F32R)
        sm = sb("sm", [P, SM_COLS])
        pos_i = sb("pos_i", [P, NT], I32)
        ident = sb("ident", [P, P])
        iota = sb("iota", [P, P])
        ident_b = sb("ident_b", [P, P], BF16)
        ssq = sb("ssq", [P, NT, 2])
        var = sb("var", [P, NT])
        table = sb("table", [P, 1])
        rstd = sb("rstd", [P, NT])
        slotT = sb("slotT", [P, 4, S + 2 * GROUP])
        gate_h = sb("gate_h", [P, S], F16)
        hots_i = sb("hots_i", [P, 2, GROUP, P], F16)
        hots_j = sb("hots_j", [P, 2, GROUP, 2, HALF], F16)
        stage_h = sb("stage_h", [P, 2, 2 * S], F32R)
        stage_l = sb("stage_l", [P, 2, 2 * S], F32R)
        lam = sb("lam", [P, 8])

        def area(at, *shape, dt=F32):
            n = int(np.prod(shape))
            v = big[:, at:at + (n // 2 if dt == BF16 else n)]
            if dt != F32:
                v = v.bitcast(dt)
            names = "abcd"[:len(shape)]
            if len(shape) > 1:
                v = v.rearrange(f"p ({' '.join(names)}) -> p {' '.join(names)}",
                                **{k: s for k, s in zip(names, shape)})
            return v

        G = area(0, NKEYS, S)
        xn = area(0, NT, D)
        keysT = area(24576, 16, NKEYS)
        qkT = area(2048, KD, S)
        v_ml = area(4096, NT, HEADS, P + 1)
        so = area(6160, NT, D)
        hs = area(8208, NT, HEADS, P)
        hg = area(18688, NT, HEADS, P)
        e_ml = area(10256, 2, 2, 512)
        p_ml = area(12304, 2, 2, 512)
        sq = area(14352, NT, D)
        gsb = area(16400, NT, 32)
        lgate = area(16464, NT, 4, 16)
        ftmp = area(16592, 3, NT, 2, HEADS)
        rows = area(16688, 5, S)
        colC = area(17968, NT, 48)
        colD = area(18064, NT, 48)
        zrow = area(18160, S)
        flip = area(26624, P)
        mask_f = area(26752, P, dt=BF16)
        mask_b = area(26880, P, dt=BF16)
        iota_i = area(27008, P, dt=I32)
        wg = area(27136, KD, 32)
        den = area(18416, 2, 2, NT)
        hss = area(22144, NT, HEADS)
        QK = area(2048, NT, 2 * D)
        v_da = area(6144, NT, D)
        qkT_da = area(8192, 16, S)
        sq_da = area(12288, NT, 2 * D)
        e_da = area(16384, 2, 2, S)
        e1_da = area(17408, S)
        a_da = area(17664, 2, S)
        aT_da = area(18176, 2, NT, P)
        o_da = area(18688, NT, HEADS, P)
        gss = area(20736, NT, 32)
        trig = area(20800, 12, NT, ROPE_HALF)
        rt = area(20992, 4, NT, 8, ROPE_HALF)
        zz = area(22016, 16, 4)
        mx = area(22080, 16, 2)
        trig_i = area(22112, NT, ROPE_HALF, dt=I32)
        ROUTE_J = 80
        qT = area(14336, 16, S)
        r0 = ROUTE_J * S
        val = area(r0, NT, 16, TOPK)
        idx = area(r0 + 512, NT, 16, TOPK, dt=U32)
        idxf = area(r0 + 1024, NT, 16, TOPK)
        topv = area(r0 + 1536, NT, HEADS, TOPK)
        topp = area(r0 + 1792, NT, HEADS * TOPK, dt=U32)
        digit = area(r0 + 2048, 2, NT, SLOTS, dt=U32)
        digitf = area(r0 + 2560, 2, NT, SLOTS)
        zsum = area(r0 + 3072, NT, HEADS)
        slotv = area(r0 + 3200, 3, NT, SLOTS)
        cand = area(24576, NT, HEADS, TOPK * TOPK)
        sc = area(28672, NT, 16, NKEYS)
        eq = area(28672, NT, SLOTS, TOPK)

        landed = [sem(f"landed{r}") for r in range(RING)]
        high_ready = sem("high_ready")
        split_ready = sem("split_ready")
        used = sem("used")
        loaded_x = sem("loaded_x")
        loaded_small = sem("loaded_small")
        loaded_keys = [sem("loaded_keys0"), sem("loaded_keys1")]
        stored = sem("stored")
        consts = sem("consts")
        dve_step = sem("dve_step")
        act_step = sem("act_step")
        x_ready = sem("x_ready")
        ssq_ready = sem("ssq_ready")
        var_ready = sem("var_ready")
        std_ready = sem("std_ready")
        xn_ready = sem("xn_ready")
        xT_ready = sem("xT_ready")
        hTh_ready = sem("hTh_ready")
        hT_ready = sem("hT_ready")
        gate_mm = sem("gate_mm")
        fabs_ready = sem("fabs_ready")
        softplus_ready = sem("softplus_ready")
        lgate_ready = sem("lgate_ready")
        rows_mm = sem("rows_mm")
        negm_ready = sem("negm_ready")
        em_ready = sem("em_ready")
        amrow_ready = sem("amrow_ready")
        cols_mm = sem("cols_mm")
        colC_ready = sem("colC_ready")
        flip_mm = sem("flip_mm")
        colD_ready = sem("colD_ready")
        qk_out = sem("qk_out")
        vo_mm = sem("vo_mm")
        v_out = sem("v_out")
        o_out = sem("o_out")
        se_mm = sem("se_mm")
        e_ready = sem("e_ready")
        p_ready = sem("p_ready")
        av_mm = sem("av_mm")
        den_ready = sem("den_ready")
        hf_ready = sem("hf_ready")
        hs_ready = sem("hs_ready")
        sq_ready = sem("sq_ready")
        qk_sq_ready = sem("qk_sq_ready")
        qk_var_ready = sem("qk_var_ready")
        qk_std_ready = sem("qk_std_ready")
        hvar_ready = sem("hvar_ready")
        hstd_ready = sem("hstd_ready")
        wo_mm = sem("wo_mm")
        wq_out_a = sem("wq_out_a")
        wq_out_v = sem("wq_out_v")
        score_mm = sem("score_mm")
        score_out = sem("score_out")
        lo_bank_free = sem("lo_bank_free")
        hi_bank_free = sem("hi_bank_free")
        gelu_done = sem("gelu_done")
        top_ready = sem("top_ready")
        exp_ready = sem("exp_ready")
        slots_ready = sem("slots_ready")
        slots_mm = sem("slots_mm")
        hot_ready = sem("hot_ready")
        abs_ready = sem("abs_ready")
        hot_ready_a = sem("hot_ready_a")
        w_mm = sem("w_mm")
        stage_h_ready = sem("stage_h_ready")
        stage_ready = sem("stage_ready")
        trig_step = sem("trig_step")
        lam_ready = sem("lam_ready")
        qkv_mm = sem("qkv_mm")
        qkv_out_a = sem("qkv_out_a")
        qkv_out_v = sem("qkv_out_v")
        qkn_ready = sem("qkn_ready")
        qkt_mm = sem("qkt_mm")
        qkt_out = sem("qkt_out")
        s_mm = sem("s_mm")
        mx_ready = sem("mx_ready")
        pe_ready = sem("pe_ready")
        rz_ready = sem("rz_ready")
        e1_ready = sem("e1_ready")
        a_ready = sem("a_ready")
        aT_mm = sem("aT_mm")
        aT_out = sem("aT_out")
        o_mm = sem("o_mm")
        o_got = sem("o_got")

        unit_of = {}
        at = 0
        for name, n in (("qk", U_QK), ("vo", U_VO), ("wo0", U_WO), ("wq0", U_WQ), ("u0", U_E), ("v0", U_E),
                        ("qkv", U_QKV), ("wo1", U_WO), ("wq1", U_WQ), ("u1", U_E), ("v1", U_E)):
            unit_of[name] = at
            at += n
        X_AFTER = {2: 4, 3: 8, 5: 12}
        GROUPS = S // GROUP
        LO = 4 + U_E // 2
        HI = 4 + 2 + 2 * GROUPS
        HOT = 2 * GROUPS + 2
        EXP_AT = 48
        ACT_TOKEN = 1

        def offset(turn, per_turn, value):
            return value if turn is None else per_turn * turn + value

        def lead(eng, split, first):
            done = [first]

            def ahead(unit):
                while done[0] <= unit + AHEAD:
                    split(done[0], None)
                    done[0] += 1

            def looped(units):
                done[0] += units

            return ahead, looped

        def tokens_made(eng, ahead, done, part, nb, t, before=0):
            last = unit_of[part] + 4 * nb + 3
            ahead(last)
            if t == 0:
                eng.wait_ge(done, before + nb + 1)
            else:
                eng.wait_ge(used, last + 1)

        block = ctx.enter_context(nc.Block())

        @block.sync
        def _(sp):
            sp.dma_start(x[:], x_in).then_inc(loaded_x, 16)
            for r in range(RING):
                sp.dma_start(raw[:, r, :], stream[r]).then_inc(landed[r], 16)
            with sp.Fori(1, (UNITS + RING) // RING) as turn:
                for r in range(RING):
                    sp.wait_ge(split_ready, RING * turn + (r + 1 - RING))
                    sp.dma_start(raw[:, r, :],
                                 stream[bass.ds(RING * turn + r, 1)].rearrange("a p f -> (a p) f")
                                 ).then_inc(landed[r], 16)
            for r in range(RING):
                sp.wait_ge(landed[r], 16 * ((UNITS + RING) // RING))
            for t in range(NT):
                sp.wait_ge(x_ready, 16)
                sp.dma_start(out[t], x[:, t, :]).then_inc(stored, 16)
            sp.wait_ge(stored, 16 * NT)

        @block.gpsimd
        def _(pool):
            pool.memset(ident[:], 0.0).then_inc(consts, 1)
            pool.memset(flip[:], 0.0).then_inc(consts, 1)
            pool.memset(mask_f[:], 0.0).then_inc(consts, 1)
            pool.memset(mask_b[:], 0.0).then_inc(consts, 1)
            pool.wait_ge(consts, 4)
            pool.affine_select(out=ident[:], in_=ident[:], compare_op=ALU.not_equal, fill=1.0, base=0,
                               pattern=[[-1, P]], channel_multiplier=1).then_inc(consts, 1)
            pool.affine_select(out=flip[:], in_=flip[:], compare_op=ALU.not_equal, fill=1.0, base=1 - P,
                               pattern=[[1, P]], channel_multiplier=1).then_inc(consts, 1)
            pool.affine_select(out=mask_f[:], in_=mask_f[:], compare_op=ALU.is_ge, fill=NEG, base=0,
                               pattern=[[1, P]], channel_multiplier=-1).then_inc(consts, 1)
            pool.affine_select(out=mask_b[:], in_=mask_b[:], compare_op=ALU.is_ge, fill=NEG, base=0,
                               pattern=[[-1, P]], channel_multiplier=1).then_inc(consts, 1)
            pool.iota(iota_i[:], pattern=[[1, P]], base=0, channel_multiplier=0).then_inc(consts, 1)
            pool.wait_ge(consts, 9)
            pool.tensor_copy(iota[:], iota_i[:]).then_inc(consts, 1)
            pool.tensor_copy(ident_b[:], ident[:]).then_inc(consts, 1)
        CONSTS = 11

        @block.scalar
        def _(act):
            steps = [0]

            def chain(ins):
                steps[0] += 1
                ins.then_inc(act_step, 1)
                act.wait_ge(act_step, steps[0])

            def high(unit, turn):
                r = unit % RING
                act.wait_ge(landed[r], offset(turn, 16 * TURN // RING, 16 * (unit // RING + 1)))
                if turn is not None or unit >= RING:
                    act.wait_ge(used, offset(turn, TURN, unit - RING + 1))
                act.activation(wh[:, r, :], raw[:, r, :], ACT.Copy).then_inc(high_ready, 1)

            ahead, looped = lead(act, high, 0)

            act.dma_start(sm[:], small).then_inc(loaded_small, 16)
            act.dma_start(wg[:], w_gates).then_inc(loaded_small, 16)
            act.dma_start(pos_i[:], positions).then_inc(loaded_small, 16)
            act.dma_start(keysT[:], keys0).then_inc(loaded_keys[0], 16)

            def norm(n, k):
                order = [(0, 0), (1, 0), (0, 1), (1, 1)] if n in (2, 5) else [(0, 0), (0, 1), (1, 0), (1, 1)]
                for i, (t, nb) in enumerate(order):
                    if n == 0:
                        act.wait_ge(loaded_x, 16)
                    else:
                        act.wait_ge(x_ready, X_AFTER[n] - 3 + i)
                    half = slice(nb * 512, (nb + 1) * 512)
                    act.activation(xn[:, t, half], x[:, t, half], ACT.Square, accum_out=ssq[:, t, nb:nb + 1]
                                   ).then_inc(ssq_ready, 1)
                act.wait_ge(var_ready, k + 1)
                act.activation(rstd[:], var[:], ACT.Sqrt).then_inc(std_ready, 1)

            def preload(func):
                act.activation(table[:], sm[:, 0:1], func)

            def transposed(n, scale):
                act.wait_ge(loaded_small, 48)
                for b in range(4):
                    act.wait_ge(xT_ready, 4 * n + b + 1)
                    for kd in (2 * b, 2 * b + 1):
                        i = act.activation(hTh[:, kd, :], ps[:, b, (kd % 2) * S:(kd % 2 + 1) * S], ACT.Copy,
                                           scale=scale(kd))
                    i.then_inc(hTh_ready, 1)

            def gain(g):
                return lambda kd: sm[:, SM_GAIN + g * KD + kd:SM_GAIN + g * KD + kd + 1]

            norm(0, 0)
            ahead(0)
            transposed(0, gain(0))
            act.wait_ge(fabs_ready, 1)
            chain(act.activation(ftmp[:, 1], ftmp[:, 0], ACT.Exp, scale=-1.0))
            act.activation(ftmp[:, 2], ftmp[:, 1], ACT.Ln, bias=1.0).then_inc(softplus_ready, 1)
            for u in range(U_QK):
                ahead(u)
                act.wait_ge(used, u + 1)
                act.activation(qkT[:, u, :], ps[:, 4 + u % 3, 0:S], ACT.Copy,
                               scale=ML_SCALE if u < 4 else 1.0).then_inc(qk_out, 1)
            act.wait_ge(negm_ready, 1)
            act.activation(rows[0:16, 2, :], rows[0:16, 3, :], ACT.Exp, scale=-1.0).then_inc(em_ready, 1)
            for nb in (2, 3):
                for t in range(NT):
                    tokens_made(act, ahead, vo_mm, "vo", nb, t)
                    act.activation(so[:, t, (nb - 2) * 512:(nb - 1) * 512], ps[:, 2 * (nb % 2) + t, :],
                                   ACT.Sigmoid).then_inc(o_out, 1)
            act.wait_ge(colC_ready, 1)
            act.wait_ge(colD_ready, 1)

            def ml_exp(h):
                act.wait_ge(se_mm, h + 1)
                if h >= 2:
                    act.wait_ge(p_ready, h - 1)
                af, ab = colC, colD
                act.activation(e_ml[:, h % 2, 0, 0:S], ps[:, 2, 0:S], ACT.Exp, bias=af[:, 0, h:h + 1])
                act.activation(e_ml[:, h % 2, 0, 384:512], ps[:, 2, 384:512], ACT.Exp, bias=af[:, 1, h:h + 1])
                act.activation(e_ml[:, h % 2, 1, 0:P], ps[:, 3, 0:P], ACT.Exp, bias=ab[:, 0, 8 + h:9 + h])
                act.activation(e_ml[:, h % 2, 1, S:512], ps[:, 3, S:512], ACT.Exp,
                               bias=ab[:, 1, 8 + h:9 + h]).then_inc(e_ready, 1)

            def ml_forward(h):
                act.wait_ge(den_ready, h + 1)
                for t in range(NT):
                    act.activation(hs[:, t, h, :], ps[:, 4 + 2 * (h % 2), t * 129:t * 129 + P], ACT.Copy,
                                   scale=den[:, h % 2, 0, t:t + 1]).then_inc(hf_ready, 1)

            def head_squares(y, h, t, ready):
                act.wait_ge(*ready)
                act.activation(sq[:, t, h * P:(h + 1) * P], y[:, t, h, :], ACT.Square,
                               accum_out=hss[:, t, h:h + 1]).then_inc(sq_ready, 1)

            for h in range(HEADS + 2):
                if h < HEADS:
                    ml_exp(h)
                if 1 <= h <= HEADS:
                    ml_forward(h - 1)
                if h == HEADS:
                    preload(ACT.Sqrt)
                if h >= 2:
                    for t in range(NT):
                        head_squares(hs, h - 2, t, (hs_ready, 2 * (h - 2) + t + 1))
            act.wait_ge(hvar_ready, 1)
            act.activation(hss[:], hss[:], ACT.Sqrt).then_inc(hstd_ready, 1)
            transposed(1, gain(4))
            ahead(unit_of["wo0"] + U_WO - 1)

            def ffn(l):
                n = (2, 5)[l]
                norm(n, (1, 3)[l])
                transposed(n, gain((1, 3)[l]))
                for u in range(U_WQ):
                    unit = unit_of[f"wq{l}"] + u
                    ahead(unit)
                    if u % 2 == 0:
                        act.wait_ge(used, unit + 1)
                        act.activation(qT[:, u, :], ps[:, 4 + u % 4, 0:S], ACT.Copy).then_inc(wq_out_a, 1)
                for b in range(8):
                    act.wait_ge(score_mm, 8 * l + b + 1)
                    act.activation(sc[:, b // 4, (b % 4) * 4:(b % 4) * 4 + 4, :].rearrange("p a n -> p (a n)"),
                                   ps[:, b, :], ACT.Copy).then_inc(lo_bank_free if b < 4 else hi_bank_free, 1)

                first = unit_of[f"u{l}"]

                def rows_of_i(half, group, turn):
                    tokens = range(ACT_TOKEN, GROUP)
                    made = offset(turn, TURN, HOT * l + (GROUPS + 2) * half + group + 1)
                    for k in tokens:
                        col = offset(turn, TURN * GROUP, group * GROUP + k)
                        i = act.activation(hots_i[:, group % 2, k, :], iota[:], ACT.Abs, scale=-1.0,
                                           bias=slotT[:, 0, bass.ds(col, 1)])
                    i.then_inc(abs_ready, 1)
                    act.wait_ge(abs_ready, made)
                    for k in tokens:
                        i = act.activation(hots_i[:, group % 2, k, :], hots_i[:, group % 2, k, :], ACT.Relu,
                                           scale=-1.0, bias=1.0)
                    i.then_inc(hot_ready_a, 1)

                def next_rows(half, r, turn0, turn, last=False):
                    if last:
                        return
                    act.wait_ge(w_mm, offset(turn, TURN, GROUPS * (2 * l + half) + r - TURN * turn0 + 1))
                    rows_of_i(half, r - TURN * turn0 + 2, turn)

                def up(a, b, weights=False):
                    with act.Fori(a // TURN, b // TURN) as turn:
                        for r in range(TURN):
                            high(first + r + AHEAD, turn)
                            if weights:
                                next_rows(0, r, a // TURN, turn)
                            if r % 2 == 1:
                                act.wait_ge(used, TURN * turn + (first + r + 1))
                                act.activation(G[:, bass.ds(TURN * turn + r - 1, 2), :]
                                               .rearrange("p j t -> p (j t)"),
                                               ps[:, r // 2, :], ACT.Gelu).then_inc(lo_bank_free, 1)
                    looped(b - a)

                up(0, EXP_AT)
                act.wait_ge(top_ready, l + 1)
                act.activation(topv[:], topv[:], ACT.Exp).then_inc(exp_ready, 1)
                up(EXP_AT, HALF)
                act.wait_ge(slots_ready, l + 1)
                act.wait_ge(hi_bank_free, HI * l + 6)
                rows_of_i(0, 0, None)
                rows_of_i(0, 1, None)
                up(HALF, U_E, weights=True)

                first = unit_of[f"v{l}"]

                def put(pair, turn):
                    act.wait_ge(used, offset(turn, TURN, first + 2 * pair - 2))
                    act.activation(stage_h[:, pair % 2, :],
                                   G[:, bass.ds(offset(turn, TURN, 2 * pair), 2), :].rearrange("p j t -> p (j t)"),
                                   ACT.Copy).then_inc(stage_h_ready, 1)

                for half in range(2):
                    act.wait_ge(hi_bank_free, HI * l + 6 + GROUPS * (half + 1))
                    put(HALF // 2 * half, None)
                    if half == 0:
                        act.wait_ge(hot_ready_a, HOT * l + GROUPS + 2)
                        rows_of_i(1, 0, None)
                        rows_of_i(1, 1, None)
                    with act.Fori(half * HALF // TURN, (half + 1) * HALF // TURN - 1) as turn:
                        for r in range(TURN):
                            if r % 2 == 0:
                                put(r // 2 + 1, turn)
                            high(first + r + AHEAD, turn)
                            if half == 0:
                                next_rows(1, r, 0, turn)
                    looped(HALF - TURN)
                    for u in range((half + 1) * HALF - TURN, (half + 1) * HALF):
                        if u % 2 == 0 and u < (half + 1) * HALF - 2:
                            put(u // 2 + 1, None)
                        ahead(first + u)
                        if half == 0:
                            next_rows(1, u, 0, None, last=u >= GROUPS - 2)

            ffn(0)
            act.wait_ge(stage_ready, U_E // 2)
            act.dma_start(keysT[:], keys1).then_inc(loaded_keys[1], 16)
            preload(ACT.Sqrt)
            norm(3, 2)
            transposed(3, gain(2))
            act.wait_ge(trig_step, 1)
            act.activation(trig[:, 6:8], trig[:, 4:6], ACT.Sin).then_inc(trig_step, 1)
            act.wait_ge(lam_ready, 1)
            act.activation(lam[:, 2:4], lam[:, 0:2], ACT.Exp).then_inc(lam_ready, 1)
            for nb in range(6):
                tokens_made(act, ahead, qkv_mm, "qkv", nb, 1)
                bank_ = ps[:, 5 + 2 * (nb % 2), :]
                if nb >= 4:
                    act.activation(v_da[:, 1, (nb - 4) * 512:(nb - 3) * 512], bank_, ACT.Copy).then_inc(qkv_out_a, 1)
                    continue
                cols = slice(nb * 512, (nb + 1) * 512)
                act.activation(QK[:, 1, cols], bank_, ACT.Copy)
                act.activation(sq_da[:, 1, cols], bank_, ACT.Square).then_inc(qkv_out_a, 1)
                act.wait_ge(qkv_out_v, nb + 1)
                act.activation(sq_da[:, 0, cols], QK[:, 0, cols], ACT.Square).then_inc(qk_sq_ready, 1)
                act.wait_ge(qk_var_ready, nb + 1)
                act.activation(gss[:, :, 8 * nb:8 * nb + 8], gss[:, :, 8 * nb:8 * nb + 8], ACT.Sqrt
                               ).then_inc(qk_std_ready, 1)
            preload(ACT.Exp)
            for b in range(8):
                act.wait_ge(qkt_mm, b + 1)
                act.activation(qkT_da[:, 2 * b:2 * b + 2, :].rearrange("p a t -> p (a t)"), ps[:, b, :], ACT.Copy
                               ).then_inc(qkt_out, 1)

            def da_exp(n):
                act.wait_ge(mx_ready, n + 1)
                for c in range(2):
                    act.activation(e_da[:, n % 2, c, :], ps[:, 2 * (n % 2) + c, 0:S], ACT.Exp, scale=DA_SCALE,
                                   bias=mx[:, n, c:c + 1], accum_out=zz[:, n, c:c + 1]).then_inc(pe_ready, 1)

            def da_second(n):
                act.wait_ge(rz_ready, n + 1)
                if n >= 1:
                    act.wait_ge(a_ready, n)
                act.activation(e1_da[:], e_da[:, n % 2, 1, :], ACT.Copy, scale=zz[:, n, 3:4]).then_inc(e1_ready, 1)

            def da_out(n):
                act.wait_ge(aT_mm, n + 1)
                act.activation(aT_da[:, n % 2].rearrange("p a t -> p (a t)"), ps[:, 4 + n % 2, 0:S], ACT.Copy
                               ).then_inc(aT_out, 1)

            for n in range(16 + 3):
                if n < 16:
                    da_exp(n)
                if 1 <= n <= 16:
                    da_out(n - 1)
                if n < 16:
                    da_second(n)
                if n == 16:
                    preload(ACT.Sqrt)
                if n >= 3:
                    head_squares(o_da, (n - 3) // 2, (n - 3) % 2, (o_got, n - 2))
            act.wait_ge(hvar_ready, 2)
            act.activation(hss[:], hss[:], ACT.Sqrt).then_inc(hstd_ready, 1)
            transposed(4, lambda kd: lam[:, 6:7])
            ahead(unit_of["wo1"] + U_WO - 1)
            ffn(1)

        @block.vector
        def _(dve):
            steps = [0]

            def chain(ins):
                steps[0] += 1
                ins.then_inc(dve_step, 1)
                dve.wait_ge(dve_step, steps[0])

            def norm(n, k):
                dve.wait_ge(ssq_ready, 4 * k + 4)
                chain(dve.tensor_tensor(var[:], ssq[:, :, 0], ssq[:, :, 1], ALU.add))
                dve.tensor_scalar(var[:], var[:], 1.0 / D, EPS, ALU.mult, ALU.add).then_inc(var_ready, 1)
                dve.wait_ge(std_ready, k + 1)
                chain(dve.reciprocal(var[:], rstd[:]))
                for t in range(NT):
                    dve.tensor_scalar(xn[:, t, :], x[:, t, :], var[:, t:t + 1], None, ALU.mult
                                      ).then_inc(xn_ready, 1)

            def low(unit, turn):
                dve.wait_ge(high_ready, offset(turn, TURN, unit + 1))
                r = unit % RING
                dve.tensor_tensor(wl[:, r, :], raw[:, r, :], wh[:, r, :].bitcast(F32), ALU.subtract
                                  ).then_inc(split_ready, 1)

            ahead, looped = lead(dve, low, 0)

            def transposed(n, scale):
                for b in range(4):
                    dve.wait_ge(hTh_ready, 4 * n + b + 1)
                    for kd in (2 * b, 2 * b + 1):
                        i = dve.scalar_tensor_tensor(out=hTl[:, kd, :], in0=ps[:, b, (kd % 2) * S:(kd % 2 + 1) * S],
                                                     scalar=scale(kd), in1=hTh[:, kd, :].bitcast(F32),
                                                     op0=ALU.mult, op1=ALU.subtract)
                    i.then_inc(hT_ready, 1)

            def gain(g):
                return lambda kd: sm[:, SM_GAIN + g * KD + kd:SM_GAIN + g * KD + kd + 1]

            def add_to_x(l):
                for nb in range(2):
                    for t in range(NT):
                        tokens_made(dve, ahead, wo_mm, f"wo{l}", nb, t, 2 * l)
                        dve.tensor_tensor(x[:, t, nb * 512:(nb + 1) * 512], x[:, t, nb * 512:(nb + 1) * 512],
                                          ps[:, 4 + 2 * nb + t, :], ALU.add).then_inc(x_ready, 1)

            def head_norm(y, k):
                dve.wait_ge(sq_ready, 2 * HEADS * k)
                dve.tensor_scalar(hss[:], hss[:], 1.0 / P, EPS, ALU.mult, ALU.add).then_inc(hvar_ready, 1)
                dve.wait_ge(hstd_ready, k)
                chain(dve.reciprocal(hss[:], hss[:]))
                for t in range(NT):
                    r = hss[:, t, :].unsqueeze(2).to_broadcast([P, HEADS, P])
                    dve.tensor_tensor(xn[:, t, :].rearrange("p (h d) -> p h d", h=HEADS), y[:, t], r, ALU.mult
                                      ).then_inc(xn_ready, 1)

            norm(0, 0)
            ahead(0)
            dve.wait_ge(loaded_small, 48)
            transposed(0, gain(0))
            dve.memset(v_ml[:, :, :, P:P + 1], 1.0)
            dve.memset(zrow[0:16, :], 0.0)
            dve.memset(slotT[:], 0.0)
            chain(dve.memset(lgate[:], 0.0))
            dve.wait_ge(gate_mm, 1)
            chain(dve.tensor_tensor(gsb[:], ps[:, 7, 0:NT * 32].rearrange("p (t g) -> p t g", t=NT),
                                    sm[:, SM_BGATE:SM_BGATE + 32].unsqueeze(1).to_broadcast([P, NT, 32]), ALU.add))
            g4 = gsb[:].rearrange("p t (d k h) -> p t d k h", d=2, k=2)
            for t in range(NT):
                i = dve.scalar_tensor_tensor(out=ftmp[:, 0, t], in0=g4[:, t, :, 1, :], scalar=-1.0,
                                             in1=g4[:, t, :, 1, :], op0=ALU.mult, op1=ALU.max)
            i.then_inc(fabs_ready, 1)
            dve.tensor_copy(lgate[:, :, 0, 0:8], g4[:, :, 0, 0, :])
            dve.tensor_copy(lgate[:, :, 1, 8:16], g4[:, :, 1, 0, :])
            dve.wait_ge(softplus_ready, 1)
            for d in range(2):
                i = dve.scalar_tensor_tensor(out=lgate[:, :, 2 + d, 8 * d:8 * d + 8], in0=g4[:, :, d, 1, :], scalar=0.0,
                                             in1=ftmp[:, 2, :, d, :], op0=ALU.min, op1=ALU.subtract)
            i.then_inc(lgate_ready, 1)
            ahead(U_QK - 1)
            dve.wait_ge(rows_mm, 1)
            chain(dve.tensor_copy(rows[0:16, 3:5, :], ps[0:16, 7, :].rearrange("p (a t) -> p a t", a=2)))
            chain(dve.tensor_tensor_scan(rows[0:16, 2, :], rows[0:16, 4, :], zrow[0:16, :], 0.0, ALU.add, ALU.add))
            chain(dve.tensor_tensor(rows[0:16, 0, :], rows[0:16, 3, :], rows[0:16, 2, :], ALU.subtract))
            chain(dve.tensor_tensor_scan(rows[0:16, 1, :], rows[0:16, 0, :], rows[0:16, 0, :], NEG, ALU.max, ALU.max))
            chain(dve.tensor_tensor(rows[0:16, 3, :], rows[0:16, 2, :], rows[0:16, 1, :], ALU.add))
            dve.tensor_scalar(rows[0:16, 1, :], rows[0:16, 1, :], -1.0, None, ALU.mult).then_inc(negm_ready, 1)
            for nb in range(2):
                for t in range(NT):
                    tokens_made(dve, ahead, vo_mm, "vo", nb, t)
                    dve.tensor_copy(v_ml[:, t, 4 * nb:4 * nb + 4, 0:P],
                                    ps[:, 2 * nb + t, :].rearrange("p (h d) -> p h d", h=4)).then_inc(v_out, 1)
            ahead(unit_of["vo"] + U_VO - 1)
            dve.wait_ge(cols_mm, 1)
            dve.tensor_copy(colC[:], ps[:, 7, 0:96].rearrange("p (t c) -> p t c", t=NT)).then_inc(colC_ready, 1)
            dve.wait_ge(flip_mm, 1)
            dve.tensor_copy(colD[:], ps[:, 7, 0:96].rearrange("p (t c) -> p t c", t=NT)).then_inc(colD_ready, 1)
            dve.wait_ge(colC_ready, 1)
            dve.wait_ge(colD_ready, 1)

            def ml_weights(h):
                dve.wait_ge(e_ready, h + 1)
                if h >= 2:
                    dve.wait_ge(av_mm, h - 1)
                sp_, e, p = ps[:, h % 2, :], e_ml[:, h % 2], p_ml[:, h % 2]
                for d, a, b in ((0, 0, 256), (0, 384, 512), (1, 0, 128), (1, 256, 512)):
                    i = dve.tensor_tensor(p[:, d, a:b], sp_[:, a:b], e[:, d, a:b], ALU.mult)
                i.then_inc(p_ready, 1)

            def ml_output(h):
                dve.wait_ge(av_mm, h + 1)
                if h >= 2:
                    dve.wait_ge(hf_ready, 2 * h - 2)
                b = 4 + 2 * (h % 2)
                for d, col in ((0, colC), (1, colD)):
                    o = ps[:, b + d, 0:258].rearrange("p (t c) -> p t c", t=NT)
                    i = dve.scalar_tensor_tensor(out=den[:, h % 2, d, :].unsqueeze(2), in0=o[:, :, P:P + 1],
                                                 scalar=-1.0, in1=col[:, :, 32 + 8 * d + h:33 + 8 * d + h],
                                                 op0=ALU.mult, op1=ALU.max)
                chain(i)
                for d in range(2):
                    o = ps[:, b + d, 0:258].rearrange("p (t c) -> p t c", t=NT)
                    dv = den[:, h % 2, d, :].unsqueeze(2)
                    i = dve.tensor_tensor(dv, o[:, :, P:P + 1], dv, ALU.max)
                chain(i)
                dve.reciprocal(den[:, h % 2], den[:, h % 2]).then_inc(den_ready, 1)
                dve.wait_ge(den_ready, h + 1)
                for t in range(NT):
                    dve.wait_ge(hf_ready, 2 * h + t + 1)
                    dve.scalar_tensor_tensor(out=hs[:, t, h, :], in0=ps[:, b + 1, t * 129:t * 129 + P],
                                             scalar=den[:, h % 2, 1, t:t + 1], in1=hs[:, t, h, :],
                                             op0=ALU.mult, op1=ALU.add).then_inc(hs_ready, 1)

            def ml_gate(h):
                dve.wait_ge(hs_ready, 2 * h + 2)
                i = dve.tensor_tensor(hg[:, :, h, :], hs[:, :, h, :],
                                      so[:, :, h * P:(h + 1) * P], ALU.mult)
                if h == HEADS - 1:
                    chain(i)

            dve.wait_ge(o_out, 4)
            for h in range(HEADS):
                ml_weights(h)
                if h >= 1:
                    ml_output(h - 1)
                if h >= 2:
                    ml_gate(h - 2)
            ml_output(HEADS - 1)
            ml_gate(HEADS - 2)
            ml_gate(HEADS - 1)
            head_norm(hg, 1)
            transposed(1, gain(4))
            add_to_x(0)

            def ffn(l):
                n = (2, 5)[l]
                norm(n, (1, 3)[l])
                transposed(n, gain((1, 3)[l]))
                for u in range(U_WQ):
                    unit = unit_of[f"wq{l}"] + u
                    ahead(unit)
                    if u % 2 == 1:
                        dve.wait_ge(used, unit + 1)
                        dve.tensor_copy(qT[:, u, :], ps[:, 4 + u % 4, 0:S]).then_inc(wq_out_v, 1)
                dve.wait_ge(lo_bank_free, LO * l + 4)
                dve.wait_ge(hi_bank_free, HI * l + 4)

                first = unit_of[f"u{l}"]
                work = [0.0, first]

                def worked(us, limit=HALF - 1):
                    work[0] += us
                    while work[0] > 0.0 and work[1] <= first + limit:
                        ahead(work[1])
                        work[1] += 1
                        work[0] -= 1.5

                def top16(rows_, values, places, us):
                    for r, v, p_ in zip(rows_, values, places):
                        i = dve.max(v[:, 0:8], r)
                    chain(i)
                    for r, v, p_ in zip(rows_, values, places):
                        i = dve.max_index(p_[:, 0:8], v[:, 0:8], r)
                    worked(2 * us, EXP_AT - 1)
                    chain(i)
                    for r, v, p_ in zip(rows_, values, places):
                        i = dve.match_replace(r, v[:, 0:8], r, -3e38)
                    chain(i)
                    for r, v, p_ in zip(rows_, values, places):
                        i = dve.max(v[:, 8:16], r)
                    worked(2 * us, EXP_AT - 1)
                    chain(i)
                    for r, v, p_ in zip(rows_, values, places):
                        i = dve.max_index(p_[:, 8:16], v[:, 8:16], r)
                    worked(us, EXP_AT - 1)
                    chain(i)

                for t in range(NT):
                    for a in range(0, 16, 4):
                        g = range(a, a + 4)
                        top16([sc[:, t, q, :] for q in g], [val[:, t, q, :] for q in g], [idx[:, t, q, :] for q in g],
                              0.8)
                    v2 = val[:, t].rearrange("p (h s) k -> p h s k", s=2)
                    chain(dve.tensor_tensor(cand[:, t].rearrange("p h (a b) -> p h a b", a=TOPK),
                                            v2[:, :, 0, :].unsqueeze(3).to_broadcast([P, HEADS, TOPK, TOPK]),
                                            v2[:, :, 1, :].unsqueeze(2).to_broadcast([P, HEADS, TOPK, TOPK]), ALU.add))
                    for a in range(0, HEADS, 4):
                        g = range(a, a + 4)
                        top16([cand[:, t, q, :] for q in g], [topv[:, t, q, :] for q in g],
                              [topp[:, t, q * TOPK:(q + 1) * TOPK] for q in g], 1.3)
                gate = slotv[:, 2].rearrange("p t (h k) -> p t h k", h=HEADS)
                chain(dve.tensor_copy(zsum[:], topv[:, :, :, 0]))
                dve.tensor_tensor(topv[:], topv[:], zsum[:].unsqueeze(3).to_broadcast([P, NT, HEADS, TOPK]),
                                  ALU.subtract).then_inc(top_ready, 1)
                dve.tensor_copy(idxf[:], idx[:])
                dve.tensor_scalar(digit[:, 0], topp[:], 4, None, ALU.logical_shift_right)
                chain(dve.tensor_scalar(digit[:, 1], topp[:], 15, None, ALU.bitwise_and))
                chain(dve.tensor_copy(digitf[:], digit[:]))
                for s in range(2):
                    for t in range(NT):
                        chain(dve.tensor_tensor(eq[:, t],
                                                digitf[:, s, t].unsqueeze(2).to_broadcast([P, SLOTS, TOPK]),
                                                iota[:, 0:TOPK].unsqueeze(1).to_broadcast([P, SLOTS, TOPK]),
                                                ALU.is_equal))
                        worked(2.2)
                        e4 = eq[:, t].rearrange("p (h k) a -> p h k a", h=HEADS)
                        src = idxf[:, t].rearrange("p (h s) k -> p h s k", s=2)[:, :, s, :]
                        chain(dve.tensor_tensor(e4, e4, src.unsqueeze(2).to_broadcast([P, HEADS, TOPK, TOPK]), ALU.mult))
                        worked(2.2)
                        chain(dve.tensor_reduce(slotv[:, s, t], eq[:, t], AX, ALU.add))
                        worked(2.2)
                dve.wait_ge(exp_ready, l + 1)
                chain(dve.tensor_reduce(zsum[:], topv[:], AX, ALU.add))
                chain(dve.reciprocal(zsum[:], zsum[:]))
                dve.tensor_tensor(gate, topv[:], zsum[:].unsqueeze(3).to_broadcast([P, NT, HEADS, TOPK]),
                                  ALU.mult).then_inc(slots_ready, 1)
                ahead(first + HALF - 1)
                dve.wait_ge(slots_mm, l + 1)
                dve.tensor_copy(slotT[:, 0:2, 0:S], ps[:, 4, :].rearrange("p (a t) -> p a t", a=2)
                                ).then_inc(hi_bank_free, 1)
                chain(dve.tensor_scalar(gate_h[:], ps[:, 5, 0:S], GATE_SCALE, None, ALU.mult))
                dve.tensor_copy(slotT[:, 2, 0:S], gate_h[:])
                dve.scalar_tensor_tensor(out=slotT[:, 3, 0:S], in0=ps[:, 5, 0:S], scalar=GATE_SCALE, in1=gate_h[:],
                                         op0=ALU.mult, op1=ALU.subtract).then_inc(hi_bank_free, 1)
                dve.wait_ge(hi_bank_free, HI * l + 6)

                def one_hots(half, group, turn):
                    for k in range(GROUP):
                        col = offset(turn, TURN * GROUP, group * GROUP + k)
                        if k < ACT_TOKEN:
                            dve.tensor_scalar(hots_i[:, group % 2, k, :], iota[:], slotT[:, 0, bass.ds(col, 1)],
                                              None, ALU.is_equal)
                        i = dve.scalar_tensor_tensor(
                            out=hots_j[:, group % 2, k],
                            in0=iota[:, half * HALF:(half + 1) * HALF].unsqueeze(1).to_broadcast([P, 2, HALF]),
                            scalar=slotT[:, 1, bass.ds(col, 1)],
                            in1=slotT[:, 2:4, bass.ds(col, 1)].to_broadcast([P, 2, HALF]),
                            op0=ALU.is_equal, op1=ALU.mult)
                    i.then_inc(hot_ready, 1)

                def weigh(half, r, turn0, turn, last=False):
                    group = r - TURN * turn0
                    dve.wait_ge(w_mm, offset(turn, TURN, GROUPS * (2 * l + half) + group + 1))
                    g = G[:, half * HALF:(half + 1) * HALF, bass.ds(offset(turn, TURN * GROUP, group * GROUP), GROUP)]
                    dve.scalar_tensor_tensor(
                        out=g, in0=ps[:, 4 + r % 4, 0:GROUP * HALF].rearrange("p (t j) -> p j t", t=GROUP),
                        scalar=1.0 / GATE_SCALE, in1=g, op0=ALU.mult, op1=ALU.mult).then_inc(hi_bank_free, 1)
                    if not last:
                        one_hots(half, group + 2, turn)

                one_hots(0, 0, None)
                one_hots(0, 1, None)
                dve.wait_ge(lo_bank_free, LO * l + 4 + HALF // 2)
                with dve.Fori(HALF // TURN, U_E // TURN) as turn:
                    for r in range(TURN):
                        weigh(0, r, HALF // TURN, turn)
                        low(first + r + AHEAD, turn)
                looped(HALF)

                first = unit_of[f"v{l}"]

                def put(pair, turn):
                    dve.wait_ge(stage_h_ready, offset(turn, TURN // 2, U_E // 2 * l + pair + 1))
                    dve.tensor_tensor(stage_l[:, pair % 2, :],
                                      G[:, bass.ds(offset(turn, TURN, 2 * pair), 2), :].rearrange("p j t -> p (j t)"),
                                      stage_h[:, pair % 2, :].bitcast(F32), ALU.subtract).then_inc(stage_ready, 1)

                for half in range(2):
                    put(HALF // 2 * half, None)
                    if half == 0:
                        dve.wait_ge(hot_ready, HOT * l + GROUPS + 2)
                        one_hots(1, 0, None)
                        one_hots(1, 1, None)
                        dve.wait_ge(lo_bank_free, LO * (l + 1))
                    with dve.Fori(half * HALF // TURN, (half + 1) * HALF // TURN - 1) as turn:
                        for r in range(TURN):
                            if r % 2 == 0:
                                put(r // 2 + 1, turn)
                            if half == 0:
                                weigh(1, r, 0, turn)
                            low(first + r + AHEAD, turn)
                    looped(HALF - TURN)
                    for u in range((half + 1) * HALF - TURN, (half + 1) * HALF):
                        if u % 2 == 0 and u < (half + 1) * HALF - 2:
                            put(u // 2 + 1, None)
                        if half == 0:
                            weigh(1, u, 0, None, last=u >= GROUPS - 2)
                        ahead(first + u)
                for t in range(NT):
                    for nb in range(2):
                        dve.wait_ge(used, unit_of[f"v{l}"] + U_E)
                        dve.tensor_copy(x[:, t, nb * 512:(nb + 1) * 512], ps[:, 2 * t + nb, :]).then_inc(x_ready, 1)

            ffn(0)
            norm(3, 2)
            transposed(3, gain(2))
            chain(dve.tensor_copy(trig[:, 0, :, 0], pos_i[:]))
            for k in range(ROPE_HALF):
                i = dve.tensor_scalar(trig[:, 1, :, k], trig[:, 0, :, 0], float(ROPE_INV[k]), None, ALU.mult)
            chain(i)
            chain(dve.tensor_scalar(trig[:, 2], trig[:, 1], 1.0 / TWO_PI, None, ALU.mult))
            chain(dve.tensor_copy(trig_i[:], trig[:, 2]))
            chain(dve.tensor_copy(trig[:, 2], trig_i[:]))
            for c in (PI_1, PI_2, PI_3):
                chain(dve.scalar_tensor_tensor(out=trig[:, 1], in0=trig[:, 2], scalar=-c, in1=trig[:, 1],
                                               op0=ALU.mult, op1=ALU.add))
            for sign, cmp in ((-1.0, ALU.is_gt), (1.0, ALU.is_lt)):
                chain(dve.tensor_scalar(trig[:, 3], trig[:, 1], -sign * float(np.pi), sign * TWO_PI, cmp, ALU.mult))
                chain(dve.tensor_tensor(trig[:, 1], trig[:, 1], trig[:, 3], ALU.add))
            chain(dve.tensor_scalar(trig[:, 2], trig[:, 1], float(np.pi / 2), None, ALU.add))
            chain(dve.tensor_scalar(trig[:, 3], trig[:, 2], float(np.pi), -TWO_PI, ALU.is_gt, ALU.mult))
            chain(dve.tensor_tensor(trig[:, 2], trig[:, 2], trig[:, 3], ALU.add))
            dve.tensor_scalar(trig[:, 4:6], trig[:, 1:3], PI_SAFE, -PI_SAFE, ALU.min, ALU.max).then_inc(trig_step, 1)
            lv = sm[:, SM_LAM:SM_LAM + 256].rearrange("p (a d) -> p a d", a=4)
            chain(dve.tensor_tensor(sq_da[:, 0, 0:128].rearrange("p (a d) -> p a d", a=2), lv[:, 0:4:2, :],
                                    lv[:, 1:4:2, :], ALU.mult))
            dve.tensor_reduce(lam[:, 0:2], sq_da[:, 0, 0:128].rearrange("p (a d) -> p a d", a=2), AX, ALU.add
                              ).then_inc(lam_ready, 1)
            dve.wait_ge(lam_ready, 2)
            chain(dve.tensor_tensor(lam[:, 4:5], lam[:, 3:4], lam[:, 2:3], ALU.subtract))
            chain(dve.tensor_scalar(lam[:, 5:6], lam[:, 4:5], LAMBDA_INIT, None, ALU.subtract))
            chain(dve.tensor_scalar(lam[:, 6:7], sm[:, SM_SUBLN:SM_SUBLN + 1], 1.0 - LAMBDA_INIT, None, ALU.mult))

            def qk_mean(nb):
                dve.wait_ge(qk_sq_ready, nb + 1)
                g = gss[:, :, 8 * nb:8 * nb + 8]
                chain(dve.tensor_reduce(g, sq_da[:, :, nb * 512:(nb + 1) * 512].rearrange("p t (g d) -> p t g d", d=64),
                                        AX, ALU.add))
                dve.tensor_scalar(g, g, 1.0 / 64, EPS, ALU.mult, ALU.add).then_inc(qk_var_ready, 1)

            def qk_norm(nb):
                dve.wait_ge(qk_std_ready, nb + 1)
                g = gss[:, :, 8 * nb:8 * nb + 8]
                chain(dve.reciprocal(g, g))
                q4 = QK[:, :, nb * 512:(nb + 1) * 512].rearrange("p t (g d) -> p t g d", d=64)
                wide = [P, NT, 8, 64]
                chain(dve.tensor_tensor(q4, q4, g.unsqueeze(3).to_broadcast(wide), ALU.mult))
                at_ = SM_QG + 64 * (nb // 2)
                for t in range(NT):
                    i = dve.tensor_tensor(q4[:, t], q4[:, t],
                                          sm[:, at_:at_ + 64].unsqueeze(1).to_broadcast([P, 8, 64]), ALU.mult)
                chain(i)
                x1, x2 = q4[:, :, :, 0:8], q4[:, :, :, 8:16]
                sin_ = trig[:, 6].unsqueeze(2).to_broadcast([P, NT, 8, ROPE_HALF])
                cos_ = trig[:, 7].unsqueeze(2).to_broadcast([P, NT, 8, ROPE_HALF])
                dve.tensor_tensor(rt[:, 0], x1, cos_, ALU.mult)
                dve.tensor_tensor(rt[:, 1], x2, sin_, ALU.mult)
                dve.tensor_tensor(rt[:, 2], x2, cos_, ALU.mult)
                chain(dve.tensor_tensor(rt[:, 3], x1, sin_, ALU.mult))
                dve.tensor_tensor(x1, rt[:, 0], rt[:, 1], ALU.subtract)
                dve.tensor_tensor(x2, rt[:, 2], rt[:, 3], ALU.add).then_inc(qkn_ready, 1)
                dve.wait_ge(qkn_ready, nb + 1)

            dve.wait_ge(trig_step, 2)
            for nb in range(6):
                tokens_made(dve, ahead, qkv_mm, "qkv", nb, 0)
                if nb < 4:
                    dst = QK[:, 0, nb * 512:(nb + 1) * 512]
                else:
                    dst = v_da[:, 0, (nb - 4) * 512:(nb - 3) * 512]
                dve.tensor_copy(dst, ps[:, 4 + 2 * (nb % 2), :]).then_inc(qkv_out_v, 1)
                if nb < 4:
                    qk_mean(nb)
                if 1 <= nb <= 4:
                    qk_norm(nb - 1)
            ahead(unit_of["qkv"] + U_QKV - 1)

            def da_max(n):
                dve.wait_ge(s_mm, n + 1)
                b = 2 * (n % 2)
                chain(dve.tensor_reduce(mx[:, n, :], ps[:, b:b + 2, 0:S], AX, ALU.max))
                dve.tensor_scalar(mx[:, n, :], mx[:, n, :], -DA_SCALE, None, ALU.mult).then_inc(mx_ready, 1)

            def da_sums(n):
                dve.wait_ge(pe_ready, 2 * n + 2)
                chain(dve.reciprocal(zz[:, n, 2:4], zz[:, n, 0:2]))
                dve.tensor_scalar(zz[:, n, 3:4], zz[:, n, 3:4], lam[:, 5:6], None, ALU.mult).then_inc(rz_ready, 1)
                dve.wait_ge(e1_ready, n + 1)
                if n >= 2:
                    dve.wait_ge(aT_mm, n - 1)
                dve.scalar_tensor_tensor(out=a_da[:, n % 2, :], in0=e_da[:, n % 2, 0, :], scalar=zz[:, n, 2:3],
                                         in1=e1_da[:], op0=ALU.mult, op1=ALU.add).then_inc(a_ready, 1)

            def da_got(n):
                dve.wait_ge(o_mm, n + 1)
                dve.tensor_copy(o_da[:, n % 2, n // 2, :], ps[:, 6 + n % 2, 0:P]).then_inc(o_got, 1)

            for n in range(16):
                da_max(n)
                if n >= 2:
                    da_got(n - 2)
                da_sums(n)
            da_got(14)
            da_got(15)
            head_norm(o_da, 2)
            dve.wait_ge(loaded_small, 48)
            transposed(4, lambda kd: lam[:, 6:7])
            add_to_x(1)
            ffn(1)

        @block.tensor
        def _(pe):
            def split(unit, turn=None):
                pe.wait_ge(split_ready, offset(turn, TURN, unit + 1))
                return wh[:, unit % RING, :], wl[:, unit % RING, :]

            def transposes(n):
                for b in range(4):
                    for kd in (2 * b, 2 * b + 1):
                        for t in range(NT):
                            if b == 0:
                                pe.wait_ge(xn_ready, 2 * n + t + 1)
                            at_ = (kd % 2) * S + t * P
                            i = pe.transpose(ps[:, b, at_:at_ + P], xn[:, t, kd * P:(kd + 1) * P], ident[:])
                    i.then_inc(xT_ready, 1)
                fresh[:] = [n]

            fresh = []

            def tokens_ready(kd):
                if fresh and kd % 2 == 0:
                    pe.wait_ge(hT_ready, 4 * fresh[0] + kd // 2 + 1)
                if kd == KD - 1:
                    fresh.clear()

            def up_projection(out, unit, turn=None):
                w_h, w_l = (w.rearrange("p (k c) -> p k c", k=KD) for w in split(unit, turn))
                for kd in range(KD):
                    tokens_ready(kd)
                    pe.matmul(out, w_h[:, kd, :], hTh[:, kd, :], start=(kd == 0), stop=False)
                    pe.matmul(out, w_h[:, kd, :], hTl[:, kd, :], start=False, stop=False)
                    i = pe.matmul(out, w_l[:, kd, :], hTh[:, kd, :], start=False, stop=(kd == KD - 1))
                i.then_inc(used, 1)

            def by_columns(unit0, units, bank, before):
                for u in range(units):
                    before(u)
                    up_projection(ps[:, bank(u), 0:S], unit0 + u)

            def by_tokens(unit0, blocks, bank, done, before):
                for nb in range(blocks):
                    for q in range(4):
                        w_h, w_l = (w.rearrange("p (k c) -> p k c", k=2) for w in split(unit0 + 4 * nb + q))
                        tokens_ready(2 * q)
                        tokens_ready(2 * q + 1)
                        for t in range(NT):
                            if q == 0:
                                before(nb, t)
                            for k in range(2):
                                kd = 2 * q + k
                                h_h, h_l = hTh[:, kd, t * P:(t + 1) * P], hTl[:, kd, t * P:(t + 1) * P]
                                out_ = ps[:, bank(nb, t), :]
                                pe.matmul(out_, h_h, w_h[:, k, :], start=(kd == 0), stop=False)
                                pe.matmul(out_, h_h, w_l[:, k, :], start=False, stop=False)
                                i = pe.matmul(out_, h_l, w_h[:, k, :], start=False, stop=(kd == KD - 1))
                            if q == 3 and t == 0:
                                i.then_inc(done, 1)
                        i.then_inc(used, 1)

            pe.wait_ge(consts, CONSTS)
            transposes(0)
            pe.wait_ge(loaded_small, 48)
            for t in range(NT):
                for kd in range(KD):
                    tokens_ready(kd)
                    for part in (hTh, hTl):
                        i = pe.matmul(ps[:, 7, t * 32:(t + 1) * 32], part[:, kd, t * P:(t + 1) * P].bitcast(F32),
                                      wg[:, kd, :], start=(kd == 0 and part is hTh),
                                      stop=(kd == KD - 1 and part is hTl))
            i.then_inc(gate_mm, 1)

            def qk_bank(u):
                if u >= 3:
                    pe.wait_ge(qk_out, u - 2)

            by_columns(unit_of["qk"], U_QK, lambda u: 4 + u % 3, qk_bank)
            pe.wait_ge(lgate_ready, 1)
            for k in range(2):
                for t in range(NT):
                    at_ = k * S + t * P
                    pe.matmul(ps[0:16, 7, at_:at_ + P], lgate[:, t, 2 * k, :], ident[:], start=True, stop=False)
                    i = pe.matmul(ps[0:16, 7, at_:at_ + P], lgate[:, 1 - t, 2 * k + 1, :], flip[:],
                                  start=False, stop=True)
            i.then_inc(rows_mm, 1)

            def vo_bank(nb, t):
                if nb == 2:
                    pe.wait_ge(v_out, t + 1)
                if nb == 3:
                    pe.wait_ge(v_out, 2 + t + 1)

            by_tokens(unit_of["vo"], 4, lambda nb, t: 2 * (nb % 2) + t, vo_mm, vo_bank)
            pe.wait_ge(em_ready, 1)
            for t in range(NT):
                for k in range(3):
                    at_ = t * 48 + k * 16
                    i = pe.matmul(ps[:, 7, at_:at_ + 16], rows[0:16, k, t * P:(t + 1) * P], ident[0:16, 0:16],
                                  start=True, stop=True)
            i.then_inc(cols_mm, 1)
            pe.wait_ge(colC_ready, 1)
            for t in range(NT):
                i = pe.matmul(ps[:, 7, t * 48:(t + 1) * 48], flip[:], colC[:, 1 - t, :], start=True, stop=True)
            i.then_inc(flip_mm, 1)
            pe.wait_ge(colD_ready, 1)
            pe.wait_ge(o_out, 4)
            pe.wait_ge(v_out, 4)
            pe.wait_ge(qk_out, U_QK)

            def ml_scores(h):
                if h >= 1:
                    pe.wait_ge(e_ready, h)
                if h >= 2:
                    pe.wait_ge(p_ready, h - 1)
                lo = (h % 2) * 64
                for s in range(NT):
                    pe.matmul(ps[:, h % 2, s * S:(s + 1) * S], qkT[lo:lo + 64, 4 + h // 2, s * P:(s + 1) * P],
                              qkT[lo:lo + 64, h // 2, :], start=True, stop=True)
                for b, col, c, blocks, m in ((2, colC, 16 + h, ((0, 0), (0, 1), (1, 1)), mask_f),
                                             (3, colD, 24 + h, ((0, 0), (1, 0), (1, 1)), mask_b)):
                    for s, t in blocks:
                        o = ps[:, b, s * S + t * P:s * S + (t + 1) * P]
                        i = pe.matmul(o, col[:, t, c:c + 1].to_broadcast([P, P]), ident[:], start=True, stop=(s != t))
                        if s == t:
                            i = pe.matmul(o, ident_b[:], m[:], start=False, stop=True)
                i.then_inc(se_mm, 1)

            def ml_values(h):
                pe.wait_ge(p_ready, h + 1)
                if h >= 2:
                    pe.wait_ge(hs_ready, 2 * h - 2)
                for d, sources in ((0, ((0,), (0, 1))), (1, ((0, 1), (1,)))):
                    for t in range(NT):
                        for s in sources[t]:
                            i = pe.matmul(ps[:, 4 + 2 * (h % 2) + d, t * 129:(t + 1) * 129],
                                          p_ml[:, h % 2, d, s * S + t * P:s * S + (t + 1) * P], v_ml[:, s, h, :],
                                          start=(s == sources[t][0]), stop=(s == sources[t][-1]))
                i.then_inc(av_mm, 1)

            ml_scores(0)
            for h in range(HEADS):
                if h + 1 < HEADS:
                    ml_scores(h + 1)
                ml_values(h)
            transposes(1)
            by_tokens(unit_of["wo0"], 2, lambda nb, t: 4 + 2 * nb + t, wo_mm, lambda nb, t: None)

            def ffn(l):
                transposes((2, 5)[l])

                def wq_bank(u):
                    if u >= 4:
                        pe.wait_ge((wq_out_a, wq_out_v)[u % 2], U_WQ // 2 * l + (u - 4) // 2 + 1)

                by_columns(unit_of[f"wq{l}"], U_WQ, lambda u: 4 + u % 4, wq_bank)
                pe.wait_ge(wq_out_a, U_WQ // 2 * (l + 1))
                pe.wait_ge(wq_out_v, U_WQ // 2 * (l + 1))
                pe.wait_ge(loaded_keys[l], 16)
                for t in range(NT):
                    for b in range(4):
                        for k in range(4):
                            q = 4 * b + k
                            i = pe.matmul(ps[:, 4 * t + b, k * P:(k + 1) * P], qT[:, q, t * P:(t + 1) * P],
                                          keysT[:, q, :], start=True, stop=True)
                        i.then_inc(score_mm, 1)
                first = unit_of[f"u{l}"]

                def up(r, turn):
                    if r % 2 == 0:
                        pe.wait_ge(lo_bank_free, TURN // 2 * turn + (LO * l + r // 2 + 1))
                    up_projection(ps[:, r // 2, (r % 2) * S:(r % 2 + 1) * S], first + r, turn)

                def weights(half, r, turn0, turn):
                    w = offset(turn, TURN, r - TURN * turn0)
                    pe.wait_ge(hot_ready, w + (HOT * l + (GROUPS + 2) * half + 1))
                    pe.wait_ge(hot_ready_a, w + (HOT * l + (GROUPS + 2) * half + 1))
                    pe.wait_ge(hi_bank_free, w + (HI * l + GROUPS * half + 3))
                    for k in range(GROUP):
                        for part in range(2):
                            i = pe.matmul(ps[:, 4 + r % 4, k * HALF:(k + 1) * HALF], hots_i[:, r % 2, k, :],
                                          hots_j[:, r % 2, k, part, :], start=(part == 0), stop=(part == 1))
                    i.then_inc(w_mm, 1)

                with pe.Fori(0, HALF // TURN) as turn:
                    for r in range(TURN):
                        up(r, turn)
                pe.wait_ge(slots_ready, l + 1)
                pe.wait_ge(hi_bank_free, HI * l + 4)
                for k in range(3):
                    for t in range(NT):
                        i = pe.transpose(ps[:, 4 + k // 2, (k % 2) * S + t * P:(k % 2) * S + (t + 1) * P],
                                         slotv[:, k, t, :], ident[:])
                i.then_inc(slots_mm, 1)
                pe.wait_ge(hi_bank_free, HI * l + 6)
                with pe.Fori(HALF // TURN, U_E // TURN) as turn:
                    for r in range(TURN):
                        weights(0, r, HALF // TURN, turn)
                        up(r, turn)
                pe.wait_ge(lo_bank_free, LO * (l + 1))
                for t in range(NT):
                    for nb in range(2):
                        pe.matmul(ps[:, 2 * t + nb, :], ident[:], x[:, t, nb * 512:(nb + 1) * 512], start=True,
                                  stop=False, skip_group_check=True)
                first = unit_of[f"v{l}"]
                for half in range(2):
                    with pe.Fori(half * HALF // TURN, (half + 1) * HALF // TURN) as turn:
                        for r in range(TURN):
                            if half == 0:
                                weights(1, r, 0, turn)
                            if r % 2 == 0:
                                pe.wait_ge(stage_ready, TURN // 2 * turn + (U_E // 2 * l + r // 2 + 1))
                            w_h, w_l = split(first + r, turn)
                            for t in range(NT):
                                at_ = (r % 2) * S + t * P
                                g_h = stage_h[:, r // 2 % 2, at_:at_ + P]
                                g_l = stage_l[:, r // 2 % 2, at_:at_ + P]
                                for a, b in ((g_h, w_h), (g_h, w_l), (g_l, w_h)):
                                    for nb in range(2):
                                        i = pe.matmul(ps[:, 2 * t + nb, :], a, b[:, nb * 512:(nb + 1) * 512],
                                                      start=False, stop=False, skip_group_check=True)
                            i.then_inc(used, 1)

            ffn(0)
            transposes(3)

            def qkv_bank(nb, t):
                if nb >= 2:
                    pe.wait_ge((qkv_out_v, qkv_out_a)[t], nb - 1)

            by_tokens(unit_of["qkv"], 6, lambda nb, t: 4 + 2 * (nb % 2) + t, qkv_mm, qkv_bank)
            pe.wait_ge(qkn_ready, 4)
            pe.wait_ge(qkv_out_v, 6)
            pe.wait_ge(qkv_out_a, 6)
            for b in range(8):
                for k in range(2):
                    for t in range(NT):
                        q = 2 * b + k
                        i = pe.transpose(ps[:, b, k * S + t * P:k * S + (t + 1) * P], QK[:, t, q * P:(q + 1) * P],
                                         ident[:])
                i.then_inc(qkt_mm, 1)
            pe.wait_ge(qkt_out, 8)

            def da_scores(n):
                h, t = n // 2, n % 2
                if n >= 2:
                    pe.wait_ge(pe_ready, 2 * n - 2)
                for c in range(2):
                    i = pe.matmul(ps[:, 2 * (n % 2) + c, 0:S], qkT_da[64 * c:64 * c + 64, h, t * P:(t + 1) * P],
                                  qkT_da[64 * c:64 * c + 64, 8 + h, :], start=True, stop=True)
                i.then_inc(s_mm, 1)

            def da_turn(n):
                pe.wait_ge(a_ready, n + 1)
                if n >= 2:
                    pe.wait_ge(aT_out, n - 1)
                for k in range(NT):
                    i = pe.transpose(ps[:, 4 + n % 2, k * P:(k + 1) * P], a_da[:, n % 2, k * P:(k + 1) * P], ident[:])
                i.then_inc(aT_mm, 1)

            def da_values(n):
                pe.wait_ge(aT_out, n + 1)
                if n >= 2:
                    pe.wait_ge(o_got, n - 1)
                h = n // 2
                for k in range(NT):
                    i = pe.matmul(ps[:, 6 + n % 2, 0:P], aT_da[:, n % 2, k, :], v_da[:, k, h * P:(h + 1) * P],
                                  start=(k == 0), stop=(k == NT - 1))
                i.then_inc(o_mm, 1)

            for n in range(16 + 2):
                if n < 16:
                    da_scores(n)
                if 1 <= n <= 16:
                    da_turn(n - 1)
                if n >= 2:
                    da_values(n - 2)
            transposes(4)
            by_tokens(unit_of["wo1"], 2, lambda nb, t: 4 + 2 * nb + t, wo_mm, lambda nb, t: None)
            ffn(1)


def _by_columns(w):
    n = w.shape[1] // P
    return w.reshape(KD, P, n, P).transpose(2, 1, 0, 3).reshape(n, P, UNIT)


def _by_tokens(w):
    n = w.shape[1] // 512
    return w.reshape(4, 2, P, n, 512).transpose(3, 0, 2, 1, 4).reshape(4 * n, P, UNIT)


def _up(u):
    return u.reshape(NKEYS, NKEYS, KD, P).transpose(1, 3, 2, 0).reshape(NKEYS, P, UNIT)


def _down(v):
    return v.reshape(NKEYS, NKEYS, UNIT).transpose(1, 0, 2)


def kernel(**inputs):
    import concourse.bacc as bacc
    from concourse.bass_utils import run_bass_kernel_spmd

    a = {k: np.asarray(v) for k, v in inputs.items()}
    w_in, qkv = a["l0_w_in"], a["l1_w_qkv"]
    parts = [_by_columns(w_in[:, :D]), _by_tokens(w_in[:, D:3 * D]), _by_tokens(a["l0_w_out"]),
             _by_columns(a["l0_peer_wq"]), _up(a["l0_peer_u"]), _down(a["l0_peer_v"]),
             _by_tokens(qkv), _by_tokens(a["l1_w_out"]),
             _by_columns(a["l1_peer_wq"]), _up(a["l1_peer_u"]), _down(a["l1_peer_v"])]
    stream = np.concatenate(parts + [np.zeros((RING, P, UNIT), np.float32)])
    column = lambda g: g.reshape(-1, P).T
    all_rows = lambda g: np.broadcast_to(g.reshape(1, -1), (P, g.size))
    small = np.concatenate([column(a[k]) for k in ("l0_norm_mix", "l0_norm_ffn", "l1_norm_mix", "l1_norm_ffn",
                                                   "l0_head_norm", "l1_subln")]
                           + [all_rows(a[k]) for k in ("l0_b_gates", "l1_q_norm", "l1_k_norm", "l1_lambda_q1",
                                                       "l1_lambda_k1", "l1_lambda_q2", "l1_lambda_k2")], axis=1)
    keys = lambda k: np.ascontiguousarray(k.transpose(3, 0, 1, 2).reshape(P, 16, NKEYS))
    arrays = {
        "stream": stream,
        "small": np.ascontiguousarray(small),
        "w_gates": np.ascontiguousarray(w_in[:, 3 * D:].reshape(KD, P, 32).transpose(1, 0, 2)),
        "keys0": keys(a["l0_peer_keys"]),
        "keys1": keys(a["l1_peer_keys"]),
        "positions": np.ascontiguousarray(a["positions"].reshape(NT, P).T),
        "x_in": np.ascontiguousarray(a["x"].reshape(NT, P, D).transpose(1, 0, 2)),
    }
    nc = bacc.Bacc("TRN2", target_bir_lowering=False, num_devices=1, dynamic_dma_scratch_size=1024)
    aps = {k: nc.dram_tensor(k, v.shape, mybir.dt.from_np(v.dtype), kind="ExternalInput").ap()
           for k, v in arrays.items()}
    out = nc.dram_tensor("out", (NT, P, D), F32, kind="ExternalOutput").ap()
    program(nc, out=out, **aps)
    r = run_bass_kernel_spmd(nc, [arrays], core_ids=[0])
    return np.asarray(r.results[0]["out"]).reshape(1, S, D)
```

```python
from contextlib import ExitStack

import numpy as np

import concourse.bass as bass
from concourse import mybir

F32 = mybir.dt.float32
F32R = mybir.dt.float32r
F16 = mybir.dt.float16
BF16 = mybir.dt.bfloat16
U32 = mybir.dt.uint32
I32 = mybir.dt.int32
ALU = mybir.AluOpType
ACT = mybir.ActivationFunctionType
AX = mybir.AxisListType.X

P = 128
S = 256
D = 1024
NT = S // P
KD = D // P
HEADS = 8
EPS = 1e-6
NEG = -1e30
ML_DQK = 64
ML_SCALE = ML_DQK ** -0.5
DA_SCALE = 64 ** -0.5
LAMBDA_INIT = 0.8 - 0.6 * float(np.exp(-0.3))
ROPE_HALF = 8
ROPE_INV = (np.float32(500000.0) ** (-np.arange(ROPE_HALF, dtype=np.float32) * np.float32(2.0)
                                     / np.float32(16))).astype(np.float32)
TOPK = 16
NKEYS = 128
SLOTS = HEADS * TOPK
UNIT = 1024
RING = 4
AHEAD = RING - 1
HALF = NKEYS // 2
GROUP = 4
GATE_SCALE = 2.0 ** 14
TURN = 8

U_GATE, U_QK, U_VO, U_WO, U_WQ, U_E, U_QKV = 1, 8, 16, 8, 16, NKEYS, 24
UNITS_0 = U_GATE + U_QK + U_VO + U_WO
UNITS_FFN = U_WQ + 2 * U_E
UNITS_1 = U_QKV + U_WO
UNITS = UNITS_0 + UNITS_FFN + UNITS_1 + UNITS_FFN

TAIL = AHEAD + -(UNITS + AHEAD) % RING

SM_GAIN = 0
SM_SUBLN = SM_GAIN + 5 * KD
SM_BGATE = SM_SUBLN + 1
SM_QG = SM_BGATE + 32
SM_LAM = SM_QG + 128
SM_COLS = SM_LAM + 256

TWO_PI = 2.0 * np.pi
PI_1 = 6.28125
PI_2 = float(np.float32(TWO_PI - PI_1))
PI_2 = float(np.array(np.array(PI_2, np.float32).view(np.uint32) & np.uint32(0xFFFFF000)).view(np.float32))
PI_3 = float(np.float32(TWO_PI - PI_1 - PI_2))
PI_SAFE = 3.1415925


def program(nc, stream, small, keys0, keys1, positions, x_in, out):
    with ExitStack() as ctx:
        def sb(name, shape, dt=F32):
            return ctx.enter_context(nc.sbuf_tensor(name, shape, dt))

        def sem(name):
            return ctx.enter_context(nc.semaphore(name))

        ps = ctx.enter_context(nc.psum_tensor("ps", [P, 8, 512], F32))

        big = sb("big", [P, NKEYS * S])
        raw = sb("raw", [P, RING, UNIT])
        wh = sb("wh", [P, RING, UNIT], F32R)
        wl = sb("wl", [P, RING, UNIT], F32R)
        x = sb("x", [P, NT, D])
        hTh = sb("hTh", [P, KD, S], F32R)
        hTl = sb("hTl", [P, KD, S], F32R)
        sm = sb("sm", [P, SM_COLS])
        pos_i = sb("pos_i", [P, NT], I32)
        ident = sb("ident", [P, P])
        iota = sb("iota", [P, P])
        iota_h = sb("iota_h", [P, TOPK], F16)
        ident_b = sb("ident_b", [P, P], BF16)
        zero_b = sb("zero_b", [P, 1], BF16)
        ssq = sb("ssq", [P, NT, 2])
        var = sb("var", [P, NT])
        table = sb("table", [P, 1])
        rstd = sb("rstd", [P, NT])
        slotT = sb("slotT", [P, 4, S])
        gate_h = sb("gate_h", [P, S], F16)
        hots_i = sb("hots_i", [P, 2, GROUP, P], F16)
        hots_j = sb("hots_j", [P, 2, GROUP, 2, HALF], F16)
        stage_h = sb("stage_h", [P, 2, 2 * S], F32R)
        stage_l = sb("stage_l", [P, 2, 2 * S], F32R)
        lam = sb("lam", [P, 8])

        def area(at, *shape, dt=F32):
            n = int(np.prod(shape))
            v = big[:, at:at + (n // 2 if dt in (BF16, F16) else n)]
            if dt != F32:
                v = v.bitcast(dt)
            names = "abcd"[:len(shape)]
            if len(shape) > 1:
                v = v.rearrange(f"p ({' '.join(names)}) -> p {' '.join(names)}",
                                **{k: s for k, s in zip(names, shape)})
            return v

        G = area(0, NKEYS, S)
        xn = area(0, NT, D)
        keysT = area(24576, 16, NKEYS)
        qkT = area(2048, KD, S)
        v_ml = area(4096, NT, HEADS, P + 1)
        so = area(6160, NT, D)
        hs = area(8208, NT, HEADS, P)
        hg = area(18688, NT, HEADS, P)
        e_ml = area(10256, 2, 2, 512)
        p_ml = area(12304, 2, 2, 512)
        sq = area(14352, NT, D)
        gsb = area(16400, NT, 32)
        lgate = area(16464, NT, 4, 16)
        ftmp = area(16592, 3, NT, 2, HEADS)
        rows = area(16688, 5, S)
        colC = area(17968, NT, 48)
        colD = area(18064, NT, 48)
        zrow = area(18160, S)
        flip = area(26624, P)
        mask_f = area(26752, P, dt=BF16)
        mask_b = area(26880, P, dt=BF16)
        iota_i = area(27008, P, dt=I32)
        gT = area(27136, S)
        den = area(18416, 2, 2, NT)
        hss = area(22144, NT, HEADS)
        QK = area(2048, NT, 2 * D)
        v_da = area(6144, NT, D)
        qkT_da = area(8192, 16, S)
        sq_da = area(12288, NT, 2 * D)
        e_da = area(22976, 3, 2, S)
        e1_da = area(16384, 2, S)
        a_da = area(17664, 2, S)
        aT_da = area(18176, 2, NT, P)
        o_da = area(18688, NT, HEADS, P)
        gss = area(20736, NT, 32)
        trig = area(20800, 12, NT, ROPE_HALF)
        rt = area(20992, 4, NT, 8, ROPE_HALF)
        zz = area(22016, 16, 4)
        mx = area(22080, 16, 2)
        trig_i = area(22112, NT, ROPE_HALF, dt=I32)
        ROUTE_J = 80
        qT = area(14336, 16, S)
        r0 = ROUTE_J * S
        val = area(r0, NT, 16, TOPK)
        idx = area(r0 + 512, NT, 16, TOPK, dt=U32)
        idxf = area(r0 + 1024, NT, 16, TOPK, dt=F16)
        topv = area(r0 + 1536, NT, HEADS, TOPK)
        topp = area(r0 + 1792, NT, HEADS * TOPK, dt=U32)
        digit = area(r0 + 2048, 2, NT, SLOTS, dt=U32)
        digitf = area(r0 + 2560, 2, NT, SLOTS, dt=F16)
        zsum = area(r0 + 3072, NT, HEADS)
        slotv = area(r0 + 3200, 3, NT, SLOTS)
        cand = area(24576, NT, HEADS, TOPK * TOPK)
        sc = area(28672, NT, 16, NKEYS)
        eq = area(28672, NT, SLOTS, TOPK, dt=F16)

        landed = [sem(f"landed{r}") for r in range(RING)]
        high_ready = sem("high_ready")
        split_ready = sem("split_ready")
        used = sem("used")
        loaded_x = sem("loaded_x")
        loaded_small = sem("loaded_small")
        loaded_keys = [sem("loaded_keys0"), sem("loaded_keys1")]
        stored = sem("stored")
        consts = sem("consts")
        dve_step = sem("dve_step")
        act_step = sem("act_step")
        x_ready = sem("x_ready")
        ssq_ready = sem("ssq_ready")
        var_ready = sem("var_ready")
        std_ready = sem("std_ready")
        xn_ready = sem("xn_ready")
        xT_ready = sem("xT_ready")
        hTh_ready = sem("hTh_ready")
        hT_ready = sem("hT_ready")
        gT_ready = sem("gT_ready")
        gate_mm = sem("gate_mm")
        fabs_ready = sem("fabs_ready")
        softplus_ready = sem("softplus_ready")
        lgate_ready = sem("lgate_ready")
        rows_mm = sem("rows_mm")
        negm_ready = sem("negm_ready")
        em_ready = sem("em_ready")
        cols_mm = sem("cols_mm")
        colC_ready = sem("colC_ready")
        flip_mm = sem("flip_mm")
        colD_ready = sem("colD_ready")
        qk_out = sem("qk_out")
        vo_mm = sem("vo_mm")
        v_out = sem("v_out")
        o_out = sem("o_out")
        se_mm = sem("se_mm")
        e_ready = sem("e_ready")
        p_ready = sem("p_ready")
        av_mm = sem("av_mm")
        den_ready = sem("den_ready")
        hf_ready = sem("hf_ready")
        hs_ready = sem("hs_ready")
        sq_ready = sem("sq_ready")
        qk_sq_ready = sem("qk_sq_ready")
        qk_var_ready = sem("qk_var_ready")
        qk_std_ready = sem("qk_std_ready")
        hvar_ready = sem("hvar_ready")
        hstd_ready = sem("hstd_ready")
        wo_mm = sem("wo_mm")
        wq_out_a = sem("wq_out_a")
        wq_out_v = sem("wq_out_v")
        score_mm = sem("score_mm")
        lo_bank_free = sem("lo_bank_free")
        hi_bank_free = sem("hi_bank_free")
        val_ready = sem("val_ready")
        cand_ready = sem("cand_ready")
        top_ready = sem("top_ready")
        exp_ready = sem("exp_ready")
        slots_ready = sem("slots_ready")
        slots_mm = sem("slots_mm")
        hot_ready = sem("hot_ready")
        abs_ready = sem("abs_ready")
        hot_ready_a = sem("hot_ready_a")
        w_mm = sem("w_mm")
        stage_h_ready = sem("stage_h_ready")
        stage_ready = sem("stage_ready")
        trig_step = sem("trig_step")
        lam_ready = sem("lam_ready")
        qkv_mm = sem("qkv_mm")
        qkv_out_a = sem("qkv_out_a")
        qkv_out_v = sem("qkv_out_v")
        qkn_ready = sem("qkn_ready")
        qkt_mm = sem("qkt_mm")
        qkt_out_a = sem("qkt_out_a")
        qkt_out_v = sem("qkt_out_v")
        s_mm = sem("s_mm")
        mx_ready = sem("mx_ready")
        pe_ready = sem("pe_ready")
        rz_ready = sem("rz_ready")
        e1_ready = sem("e1_ready")
        a_ready = sem("a_ready")
        aT_mm = sem("aT_mm")
        aT_out = sem("aT_out")
        o_mm = sem("o_mm")
        o_got = sem("o_got")

        unit_of = {}
        at = 0
        for name, n in (("gate", U_GATE), ("qk", U_QK), ("vo", U_VO), ("wo0", U_WO),
                        ("wq0", U_WQ), ("u0", U_E), ("v0", U_E), ("qkv", U_QKV), ("wo1", U_WO), ("wq1", U_WQ), ("u1", U_E), ("v1", U_E)):
            unit_of[name] = at
            at += n
        X_AFTER = {2: 4, 3: 8, 5: 12}
        GROUPS = S // GROUP
        LO = 4 + U_E // 2
        HI = 4 + 2 + 2 * GROUPS
        HOT = 2 * GROUPS
        EXP_AT = 48
        SLOTS_AT = HALF - 2
        ACT_TOKEN = 1

        def offset(turn, per_turn, value):
            return value if turn is None else per_turn * turn + value

        def lead(eng, split, first):
            done = [first]

            def ahead(unit):
                while done[0] <= unit + AHEAD:
                    split(done[0], None)
                    done[0] += 1

            def looped(units):
                done[0] += units

            return ahead, looped

        def tokens_made(eng, ahead, done, part, nb, t, before=0):
            last = unit_of[part] + 4 * nb + 3
            ahead(last)
            if t == 0:
                eng.wait_ge(done, before + nb + 1)
            else:
                eng.wait_ge(used, last + 1)

        block = ctx.enter_context(nc.Block())

        @block.sync
        def _(sp):
            sp.dma_start(x[:], x_in).then_inc(loaded_x, 16)
            for r in range(RING):
                sp.dma_start(raw[:, r, :], stream[r]).then_inc(landed[r], 16)
            with sp.Fori(1, (UNITS + TAIL) // RING) as turn:
                for r in range(RING):
                    sp.wait_ge(split_ready, RING * turn + (r + 1 - RING))
                    sp.dma_start(raw[:, r, :],
                                 stream[bass.ds(RING * turn + r, 1)].rearrange("a p f -> (a p) f")
                                 ).then_inc(landed[r], 16)
            for r in range(RING):
                sp.wait_ge(landed[r], 16 * ((UNITS + TAIL) // RING))
            for i in range(2 * NT):
                sp.wait_ge(x_ready, 12 + i + 1)
                half = slice((i % 2) * 512, (i % 2 + 1) * 512)
                sp.dma_start(out[i // 2][:, half], x[:, i // 2, half]).then_inc(stored, 16)
            sp.wait_ge(stored, 16 * 2 * NT)

        CONSTS = 13

        @block.gpsimd
        def _(pool):
            pool.memset(ident[:], 0.0).then_inc(consts, 1)
            pool.memset(flip[:], 0.0).then_inc(consts, 1)
            pool.memset(mask_f[:], 0.0).then_inc(consts, 1)
            pool.memset(mask_b[:], 0.0).then_inc(consts, 1)
            pool.wait_ge(consts, 4)
            pool.affine_select(out=ident[:], in_=ident[:], compare_op=ALU.not_equal, fill=1.0, base=0,
                               pattern=[[-1, P]], channel_multiplier=1).then_inc(consts, 1)
            pool.affine_select(out=flip[:], in_=flip[:], compare_op=ALU.not_equal, fill=1.0, base=1 - P,
                               pattern=[[1, P]], channel_multiplier=1).then_inc(consts, 1)
            pool.affine_select(out=mask_f[:], in_=mask_f[:], compare_op=ALU.is_ge, fill=NEG, base=0,
                               pattern=[[1, P]], channel_multiplier=-1).then_inc(consts, 1)
            pool.affine_select(out=mask_b[:], in_=mask_b[:], compare_op=ALU.is_ge, fill=NEG, base=0,
                               pattern=[[-1, P]], channel_multiplier=1).then_inc(consts, 1)
            pool.iota(iota_i[:], pattern=[[1, P]], base=0, channel_multiplier=0).then_inc(consts, 1)
            pool.wait_ge(consts, 9)
            pool.tensor_copy(iota[:], iota_i[:]).then_inc(consts, 1)
            pool.tensor_copy(ident_b[:], ident[:]).then_inc(consts, 1)
            pool.tensor_copy(iota_h[:], iota_i[:, 0:TOPK]).then_inc(consts, 1)
            pool.memset(zero_b[:], 0.0).then_inc(consts, 1)
            for l in range(2):
                for t in range(NT):
                    pool.wait_ge(val_ready, NT * l + t + 1)
                    pool.wait_ge(hi_bank_free, HI * l + 4)
                    v2 = val[:, t].rearrange("p (h s) k -> p h s k", s=2)
                    pool.tensor_tensor(cand[:, t].rearrange("p h (a b) -> p h a b", a=TOPK),
                                       v2[:, :, 0, :].unsqueeze(3).to_broadcast([P, HEADS, TOPK, TOPK]),
                                       v2[:, :, 1, :].unsqueeze(2).to_broadcast([P, HEADS, TOPK, TOPK]), ALU.add
                                       ).then_inc(cand_ready, 1)

        @block.scalar
        def _(act):
            steps = [0]

            def chain(ins):
                steps[0] += 1
                ins.then_inc(act_step, 1)
                act.wait_ge(act_step, steps[0])

            def high(unit, turn):
                r = unit % RING
                act.wait_ge(landed[r], offset(turn, 16 * TURN // RING, 16 * (unit // RING + 1)))
                if turn is not None or unit >= RING:
                    act.wait_ge(used, offset(turn, TURN, unit - RING + 1))
                act.activation(wh[:, r, :], raw[:, r, :], ACT.Copy).then_inc(high_ready, 1)

            ahead, looped = lead(act, high, 0)

            act.dma_start(sm[:], small).then_inc(loaded_small, 16)
            act.dma_start(pos_i[:], positions).then_inc(loaded_small, 16)
            act.dma_start(keysT[:], keys0).then_inc(loaded_keys[0], 16)

            def norm(n, k):
                order = [(0, 0), (1, 0), (0, 1), (1, 1)] if n in (2, 5) else [(0, 0), (0, 1), (1, 0), (1, 1)]
                for i, (t, nb) in enumerate(order):
                    if n == 0:
                        act.wait_ge(loaded_x, 16)
                    else:
                        act.wait_ge(x_ready, X_AFTER[n] - 3 + i)
                    half = slice(nb * 512, (nb + 1) * 512)
                    act.activation(xn[:, t, half], x[:, t, half], ACT.Square, accum_out=ssq[:, t, nb:nb + 1]
                                   ).then_inc(ssq_ready, 1)
                act.wait_ge(var_ready, k + 1)
                act.activation(rstd[:], var[:], ACT.Sqrt).then_inc(std_ready, 1)

            def preload(func):
                act.activation(table[:], ident[:, 0:1], func)

            def transposed(n, scale):
                act.wait_ge(loaded_small, 32)
                for b in range(4):
                    act.wait_ge(xT_ready, 4 * n + b + 1)
                    for kd in (2 * b, 2 * b + 1):
                        i = act.activation(hTh[:, kd, :], ps[:, b, (kd % 2) * S:(kd % 2 + 1) * S], ACT.Copy,
                                           scale=scale(kd))
                    i.then_inc(hTh_ready, 1)

            def gain(g):
                return lambda kd: sm[:, SM_GAIN + g * KD + kd:SM_GAIN + g * KD + kd + 1]

            act.wait_ge(consts, CONSTS)
            preload(ACT.Sqrt)
            norm(0, 0)
            ahead(-2)
            transposed(0, gain(0))
            ahead(unit_of["qk"])
            act.wait_ge(fabs_ready, 1)
            chain(act.activation(ftmp[:, 1], ftmp[:, 0], ACT.Exp, scale=-1.0))
            act.activation(ftmp[:, 2], ftmp[:, 1], ACT.Ln, bias=1.0).then_inc(softplus_ready, 1)
            for u in range(U_QK):
                ahead(unit_of["qk"] + u)
                act.wait_ge(used, unit_of["qk"] + u + 1)
                act.activation(qkT[:, u, :], ps[:, 4 + u % 3, 0:S], ACT.Copy,
                               scale=ML_SCALE if u < 4 else 1.0).then_inc(qk_out, 1)
            act.wait_ge(negm_ready, 1)
            act.activation(rows[0:16, 2, :], rows[0:16, 3, :], ACT.Exp, scale=-1.0).then_inc(em_ready, 1)
            for nb in (2, 3):
                for t in range(NT):
                    tokens_made(act, ahead, vo_mm, "vo", nb, t)
                    act.activation(so[:, t, (nb - 2) * 512:(nb - 1) * 512], ps[:, 2 * (nb % 2) + t, :],
                                   ACT.Sigmoid).then_inc(o_out, 1)
            act.wait_ge(colC_ready, 1)
            act.wait_ge(colD_ready, 1)

            def ml_exp(h):
                act.wait_ge(se_mm, h + 1)
                if h >= 2:
                    act.wait_ge(p_ready, h - 1)
                af, ab = colC, colD
                act.activation(e_ml[:, h % 2, 0, 0:S], ps[:, 2, 0:S], ACT.Exp, bias=af[:, 0, h:h + 1])
                act.activation(e_ml[:, h % 2, 0, 384:512], ps[:, 2, 384:512], ACT.Exp, bias=af[:, 1, h:h + 1])
                act.activation(e_ml[:, h % 2, 1, 0:P], ps[:, 3, 0:P], ACT.Exp, bias=ab[:, 0, 8 + h:9 + h])
                act.activation(e_ml[:, h % 2, 1, S:512], ps[:, 3, S:512], ACT.Exp,
                               bias=ab[:, 1, 8 + h:9 + h]).then_inc(e_ready, 1)

            def ml_forward(h):
                act.wait_ge(den_ready, h + 1)
                for t in range(NT):
                    act.activation(hs[:, t, h, :], ps[:, 4 + 2 * (h % 2), t * 129:t * 129 + P], ACT.Copy,
                                   scale=den[:, h % 2, 0, t:t + 1]).then_inc(hf_ready, 1)

            def head_squares(y, h, t, ready):
                act.wait_ge(*ready)
                act.activation(sq[:, t, h * P:(h + 1) * P], y[:, t, h, :], ACT.Square,
                               accum_out=hss[:, t, h:h + 1]).then_inc(sq_ready, 1)

            for h in range(HEADS + 2):
                if h < HEADS:
                    ml_exp(h)
                if h == HEADS:
                    preload(ACT.Sqrt)
                if 1 <= h <= HEADS:
                    ml_forward(h - 1)
                if h >= 2:
                    for t in range(NT):
                        head_squares(hs, h - 2, t, (hs_ready, 2 * (h - 2) + t + 1))
            act.wait_ge(hvar_ready, 1)
            act.activation(hss[:], hss[:], ACT.Sqrt).then_inc(hstd_ready, 1)
            transposed(1, gain(4))
            ahead(unit_of["wo0"] + U_WO - 1)

            def ffn(l):
                n = (2, 5)[l]
                norm(n, (1, 3)[l])
                transposed(n, gain((1, 3)[l]))
                for u in range(U_WQ):
                    unit = unit_of[f"wq{l}"] + u
                    ahead(unit)
                    if u % 2 == 0:
                        act.wait_ge(used, unit + 1)
                        act.activation(qT[:, u, :], ps[:, 4 + u % 4, 0:S], ACT.Copy).then_inc(wq_out_a, 1)
                for b in range(8):
                    act.wait_ge(score_mm, 8 * l + b + 1)
                    act.activation(sc[:, b // 4, (b % 4) * 4:(b % 4) * 4 + 4, :].rearrange("p a n -> p (a n)"),
                                   ps[:, b, :], ACT.Copy).then_inc(lo_bank_free if b < 4 else hi_bank_free, 1)

                first = unit_of[f"u{l}"]

                def rows_of_i(half, group, turn):
                    tokens = range(ACT_TOKEN, GROUP)
                    made = offset(turn, TURN, HOT * l + GROUPS * half + group + 1)
                    for k in tokens:
                        col = offset(turn, TURN * GROUP, group * GROUP + k)
                        i = act.activation(hots_i[:, group % 2, k, :], iota[:], ACT.Abs, scale=-1.0,
                                           bias=slotT[:, 0, bass.ds(col, 1)])
                    i.then_inc(abs_ready, 1)
                    act.wait_ge(abs_ready, made)
                    for k in tokens:
                        i = act.activation(hots_i[:, group % 2, k, :], hots_i[:, group % 2, k, :], ACT.Relu,
                                           scale=-1.0, bias=1.0)
                    i.then_inc(hot_ready_a, 1)

                def next_rows(half, r, turn0, turn):
                    group = r - TURN * turn0
                    act.wait_ge(w_mm, offset(turn, TURN, GROUPS * (2 * l + half) + group + 1))
                    if turn is not None or group < GROUPS - 2:
                        rows_of_i(half, group + 2, turn)
                    elif half == 0:
                        rows_of_i(1, group + 2 - GROUPS, None)

                def gelu(r, turn):
                    act.wait_ge(used, offset(turn, TURN, first + r + 1))
                    act.activation(G[:, bass.ds(offset(turn, TURN, r - 1), 2), :].rearrange("p j t -> p (j t)"),
                                   ps[:, r // 2 % 4, :], ACT.Gelu).then_inc(lo_bank_free, 1)

                def up(a, b, weights=False):
                    with act.Fori(a // TURN, b // TURN) as turn:
                        for r in range(TURN):
                            high(first + r + AHEAD, turn)
                            if r % 2 == 1:
                                gelu(r, turn)
                            if weights:
                                next_rows(0, r, a // TURN, turn)
                    looped(b - a)

                preload(ACT.Gelu)
                up(0, EXP_AT)
                act.wait_ge(top_ready, l + 1)
                act.activation(topv[:], topv[:], ACT.Exp).then_inc(exp_ready, 1)
                preload(ACT.Gelu)
                up(EXP_AT, HALF - TURN)
                for u in range(HALF - TURN, HALF):
                    ahead(first + u)
                    if u == SLOTS_AT:
                        act.wait_ge(hi_bank_free, HI * l + 6)
                        rows_of_i(0, 0, None)
                        rows_of_i(0, 1, None)
                    if u % 2 == 1:
                        gelu(u, None)
                up(HALF, U_E - TURN, weights=True)
                for u in range(U_E - TURN, U_E):
                    if u < U_E - 1:
                        ahead(first + u)
                    if u % 2 == 1:
                        gelu(u, None)
                    if u < U_E - 1:
                        next_rows(0, u, HALF // TURN, None)

                first = unit_of[f"v{l}"]

                def put(pair, turn):
                    act.wait_ge(used, offset(turn, TURN, first + 2 * pair - 2))
                    act.activation(stage_h[:, pair % 2, :],
                                   G[:, bass.ds(offset(turn, TURN, 2 * pair), 2), :].rearrange("p j t -> p (j t)"),
                                   ACT.Copy).then_inc(stage_h_ready, 1)

                for half in range(2):
                    act.wait_ge(hi_bank_free, HI * l + 6 + GROUPS * (half + 1))
                    put(HALF // 2 * half, None)
                    if half == 0:
                        next_rows(0, U_E - 1, HALF // TURN, None)
                    ahead(first + half * HALF - 1)
                    with act.Fori(half * HALF // TURN, (half + 1) * HALF // TURN - 1) as turn:
                        for r in range(TURN):
                            if r % 2 == 0:
                                put(r // 2 + 1, turn)
                            high(first + r + AHEAD, turn)
                            if half == 0:
                                next_rows(1, r, 0, turn)
                    looped(HALF - TURN)
                    for u in range((half + 1) * HALF - TURN, (half + 1) * HALF):
                        if u % 2 == 0 and u < (half + 1) * HALF - 2:
                            put(u // 2 + 1, None)
                        if u != HALF - 1:
                            ahead(first + u)
                        if half == 0 and u < HALF - 2:
                            next_rows(1, u, 0, None)

            ffn(0)
            act.wait_ge(stage_ready, U_E // 2)
            act.dma_start(keysT[:], keys1).then_inc(loaded_keys[1], 16)
            preload(ACT.Sqrt)
            norm(3, 2)
            transposed(3, gain(2))
            ahead(unit_of["qkv"])
            act.wait_ge(trig_step, 1)
            act.activation(trig[:, 6:8], trig[:, 4:6], ACT.Sin).then_inc(trig_step, 1)
            act.wait_ge(lam_ready, 1)
            act.activation(lam[:, 2:4], lam[:, 0:2], ACT.Exp).then_inc(lam_ready, 1)
            for nb in range(6):
                tokens_made(act, ahead, qkv_mm, "qkv", nb, 1)
                bank_ = ps[:, 5 + 2 * (nb % 2), :]
                if nb == 4:
                    preload(ACT.Exp)
                if nb >= 4:
                    act.activation(v_da[:, 1, (nb - 4) * 512:(nb - 3) * 512], bank_, ACT.Copy).then_inc(qkv_out_a, 1)
                    continue
                cols = slice(nb * 512, (nb + 1) * 512)
                act.activation(QK[:, 1, cols], bank_, ACT.Copy)
                act.activation(sq_da[:, 1, cols], bank_, ACT.Square).then_inc(qkv_out_a, 1)
                act.wait_ge(qkv_out_v, nb + 1)
                act.activation(sq_da[:, 0, cols], QK[:, 0, cols], ACT.Square).then_inc(qk_sq_ready, 1)
                ahead(unit_of["qkv"] + 4 * nb + 4)
                act.wait_ge(qk_var_ready, nb + 1)
                act.activation(gss[:, :, 8 * nb:8 * nb + 8], gss[:, :, 8 * nb:8 * nb + 8], ACT.Sqrt
                               ).then_inc(qk_std_ready, 1)
                ahead(unit_of["qkv"] + 4 * nb + 5)
            for b in range(0, 8, 2):
                act.wait_ge(qkt_mm, b + 1)
                act.activation(qkT_da[:, 2 * b:2 * b + 2, :].rearrange("p a t -> p (a t)"), ps[:, b, :], ACT.Copy
                               ).then_inc(qkt_out_a, 1)

            def da_exp(n):
                act.wait_ge(mx_ready, n + 1)
                if n >= 3:
                    act.wait_ge(a_ready, n - 2)
                for c in range(2):
                    act.activation(e_da[:, n % 3, c, :], ps[:, 2 * (n % 2) + c, 0:S], ACT.Exp, scale=DA_SCALE,
                                   bias=mx[:, n, c:c + 1], accum_out=zz[:, n, c:c + 1]).then_inc(pe_ready, 1)

            def da_second(n):
                act.wait_ge(rz_ready, n + 1)
                if n >= 2:
                    act.wait_ge(a_ready, n - 1)
                act.activation(e1_da[:, n % 2], e_da[:, n % 3, 1, :], ACT.Copy, scale=zz[:, n, 3:4]).then_inc(e1_ready, 1)

            def da_out(n):
                act.wait_ge(aT_mm, n + 1)
                act.activation(aT_da[:, n % 2].rearrange("p a t -> p (a t)"), ps[:, 4 + n % 2, 0:S], ACT.Copy
                               ).then_inc(aT_out, 1)

            for n in range(16 + 6):
                if n < 16:
                    da_exp(n)
                if n == 16:
                    preload(ACT.Sqrt)
                if 1 <= n < 17:
                    da_second(n - 1)
                if 3 <= n < 19:
                    da_out(n - 3)
                if n >= 6:
                    head_squares(o_da, (n - 6) // 2, (n - 6) % 2, (o_got, n - 5))
            act.wait_ge(hvar_ready, 2)
            act.activation(hss[:], hss[:], ACT.Sqrt).then_inc(hstd_ready, 1)
            transposed(4, lambda kd: lam[:, 6:7])
            ahead(unit_of["wo1"] + U_WO - 1)
            ffn(1)

        @block.vector
        def _(dve):
            steps = [0]

            def chain(ins):
                steps[0] += 1
                ins.then_inc(dve_step, 1)
                dve.wait_ge(dve_step, steps[0])

            def norm(n, k):
                dve.wait_ge(ssq_ready, 4 * k + 4)
                chain(dve.tensor_tensor(var[:], ssq[:, :, 0], ssq[:, :, 1], ALU.add))
                dve.tensor_scalar(var[:], var[:], 1.0 / D, EPS, ALU.mult, ALU.add).then_inc(var_ready, 1)
                dve.wait_ge(std_ready, k + 1)
                chain(dve.reciprocal(var[:], rstd[:]))
                for nb in range(2):
                    for t in range(NT):
                        half = slice(nb * 512, (nb + 1) * 512)
                        dve.tensor_scalar(xn[:, t, half], x[:, t, half], var[:, t:t + 1], None, ALU.mult
                                          ).then_inc(xn_ready, 1)

            def low(unit, turn):
                dve.wait_ge(high_ready, offset(turn, TURN, unit + 1))
                r = unit % RING
                dve.tensor_tensor(wl[:, r, :], raw[:, r, :], wh[:, r, :].bitcast(F32), ALU.subtract
                                  ).then_inc(split_ready, 1)

            ahead, looped = lead(dve, low, 0)

            def transposed(n, scale):
                for b in range(4):
                    dve.wait_ge(hTh_ready, 4 * n + b + 1)
                    for kd in (2 * b, 2 * b + 1):
                        i = dve.scalar_tensor_tensor(out=hTl[:, kd, :], in0=ps[:, b, (kd % 2) * S:(kd % 2 + 1) * S],
                                                     scalar=scale(kd), in1=hTh[:, kd, :].bitcast(F32),
                                                     op0=ALU.mult, op1=ALU.subtract)
                    i.then_inc(hT_ready, 1)

            def gain(g):
                return lambda kd: sm[:, SM_GAIN + g * KD + kd:SM_GAIN + g * KD + kd + 1]

            def add_to_x(l):
                for nb in range(2):
                    for t in range(NT):
                        tokens_made(dve, ahead, wo_mm, f"wo{l}", nb, t, 2 * l)
                        dve.tensor_tensor(x[:, t, nb * 512:(nb + 1) * 512], x[:, t, nb * 512:(nb + 1) * 512],
                                          ps[:, 4 + 2 * nb + t, :], ALU.add).then_inc(x_ready, 1)

            def head_norm(y, k):
                dve.wait_ge(sq_ready, 2 * HEADS * k)
                dve.tensor_scalar(hss[:], hss[:], 1.0 / P, EPS, ALU.mult, ALU.add).then_inc(hvar_ready, 1)
                dve.wait_ge(hstd_ready, k)
                chain(dve.reciprocal(hss[:], hss[:]))
                for a in (0, HEADS // 2):
                    for t in range(NT):
                        r = hss[:, t, a:a + 4].unsqueeze(2).to_broadcast([P, 4, P])
                        dve.tensor_tensor(xn[:, t, a * P:(a + 4) * P].rearrange("p (h d) -> p h d", h=4),
                                          y[:, t, a:a + 4], r, ALU.mult).then_inc(xn_ready, 1)

            norm(0, 0)
            ahead(-2)
            dve.wait_ge(loaded_small, 32)
            transposed(0, gain(0))
            ahead(0)
            dve.memset(v_ml[:, :, :, P:P + 1], 1.0)
            dve.memset(zrow[0:16, :], 0.0)
            dve.memset(slotT[:], 0.0)
            chain(dve.memset(lgate[:], 0.0))
            dve.wait_ge(used, unit_of["gate"] + 1)
            dve.tensor_copy(gT[0:32, :], ps[0:32, 7, 0:S]).then_inc(gT_ready, 1)
            ahead(unit_of["qk"])
            dve.wait_ge(gate_mm, 1)
            chain(dve.tensor_tensor(gsb[:], ps[:, 7, S:S + NT * 32].rearrange("p (t g) -> p t g", t=NT),
                                    sm[:, SM_BGATE:SM_BGATE + 32].unsqueeze(1).to_broadcast([P, NT, 32]), ALU.add))
            g4 = gsb[:].rearrange("p t (d k h) -> p t d k h", d=2, k=2)
            for t in range(NT):
                i = dve.scalar_tensor_tensor(out=ftmp[:, 0, t], in0=g4[:, t, :, 1, :], scalar=-1.0,
                                             in1=g4[:, t, :, 1, :], op0=ALU.mult, op1=ALU.max)
            i.then_inc(fabs_ready, 1)
            dve.tensor_copy(lgate[:, :, 0, 0:8], g4[:, :, 0, 0, :])
            dve.tensor_copy(lgate[:, :, 1, 8:16], g4[:, :, 1, 0, :])
            dve.wait_ge(softplus_ready, 1)
            for d in range(2):
                i = dve.scalar_tensor_tensor(out=lgate[:, :, 2 + d, 8 * d:8 * d + 8], in0=g4[:, :, d, 1, :], scalar=0.0,
                                             in1=ftmp[:, 2, :, d, :], op0=ALU.min, op1=ALU.subtract)
            i.then_inc(lgate_ready, 1)
            ahead(unit_of["qk"] + U_QK - 1)
            dve.wait_ge(rows_mm, 1)
            chain(dve.tensor_copy(rows[0:16, 3:5, :], ps[0:16, 7, :].rearrange("p (a t) -> p a t", a=2)))
            chain(dve.tensor_tensor_scan(rows[0:16, 2, :], rows[0:16, 4, :], zrow[0:16, :], 0.0, ALU.add, ALU.add))
            chain(dve.tensor_tensor(rows[0:16, 0, :], rows[0:16, 3, :], rows[0:16, 2, :], ALU.subtract))
            chain(dve.tensor_tensor_scan(rows[0:16, 1, :], rows[0:16, 0, :], rows[0:16, 0, :], NEG, ALU.max, ALU.max))
            chain(dve.tensor_tensor(rows[0:16, 3, :], rows[0:16, 2, :], rows[0:16, 1, :], ALU.add))
            dve.tensor_scalar(rows[0:16, 1, :], rows[0:16, 1, :], -1.0, None, ALU.mult).then_inc(negm_ready, 1)
            for nb in range(2):
                for t in range(NT):
                    tokens_made(dve, ahead, vo_mm, "vo", nb, t)
                    dve.tensor_copy(v_ml[:, t, 4 * nb:4 * nb + 4, 0:P],
                                    ps[:, 2 * nb + t, :].rearrange("p (h d) -> p h d", h=4)).then_inc(v_out, 1)
            ahead(unit_of["vo"] + U_VO - 1)
            dve.wait_ge(cols_mm, 1)
            dve.tensor_copy(colC[:], ps[:, 7, 0:96].rearrange("p (t c) -> p t c", t=NT)).then_inc(colC_ready, 1)
            dve.wait_ge(flip_mm, 1)
            dve.tensor_copy(colD[:], ps[:, 7, 0:96].rearrange("p (t c) -> p t c", t=NT)).then_inc(colD_ready, 1)
            dve.wait_ge(colC_ready, 1)
            dve.wait_ge(colD_ready, 1)

            def ml_weights(h):
                dve.wait_ge(e_ready, h + 1)
                if h >= 2:
                    dve.wait_ge(av_mm, h - 1)
                sp_, e, p = ps[:, h % 2, :], e_ml[:, h % 2], p_ml[:, h % 2]
                for d, a, b in ((0, 0, 256), (0, 384, 512), (1, 0, 128), (1, 256, 512)):
                    i = dve.tensor_tensor(p[:, d, a:b], sp_[:, a:b], e[:, d, a:b], ALU.mult)
                i.then_inc(p_ready, 1)

            def ml_output(h):
                dve.wait_ge(av_mm, h + 1)
                if h >= 2:
                    dve.wait_ge(hf_ready, 2 * h - 2)
                b = 4 + 2 * (h % 2)
                for d, col in ((0, colC), (1, colD)):
                    o = ps[:, b + d, 0:258].rearrange("p (t c) -> p t c", t=NT)
                    i = dve.scalar_tensor_tensor(out=den[:, h % 2, d, :].unsqueeze(2), in0=o[:, :, P:P + 1],
                                                 scalar=-1.0, in1=col[:, :, 32 + 8 * d + h:33 + 8 * d + h],
                                                 op0=ALU.mult, op1=ALU.max)
                chain(i)
                for d in range(2):
                    o = ps[:, b + d, 0:258].rearrange("p (t c) -> p t c", t=NT)
                    dv = den[:, h % 2, d, :].unsqueeze(2)
                    i = dve.tensor_tensor(dv, o[:, :, P:P + 1], dv, ALU.max)
                chain(i)
                dve.reciprocal(den[:, h % 2], den[:, h % 2]).then_inc(den_ready, 1)
                dve.wait_ge(den_ready, h + 1)
                for t in range(NT):
                    dve.wait_ge(hf_ready, 2 * h + t + 1)
                    dve.scalar_tensor_tensor(out=hs[:, t, h, :], in0=ps[:, b + 1, t * 129:t * 129 + P],
                                             scalar=den[:, h % 2, 1, t:t + 1], in1=hs[:, t, h, :],
                                             op0=ALU.mult, op1=ALU.add).then_inc(hs_ready, 1)

            def ml_gate(h):
                dve.wait_ge(hs_ready, 2 * h + 2)
                i = dve.tensor_tensor(hg[:, :, h, :], hs[:, :, h, :],
                                      so[:, :, h * P:(h + 1) * P], ALU.mult)
                if h == HEADS - 1:
                    chain(i)

            dve.wait_ge(o_out, 4)
            for h in range(HEADS):
                ml_weights(h)
                if h >= 1:
                    ml_output(h - 1)
                if h >= 2:
                    ml_gate(h - 2)
            ml_output(HEADS - 1)
            ml_gate(HEADS - 2)
            ml_gate(HEADS - 1)
            head_norm(hg, 1)
            transposed(1, gain(4))
            add_to_x(0)

            def ffn(l):
                n = (2, 5)[l]
                norm(n, (1, 3)[l])
                transposed(n, gain((1, 3)[l]))
                for u in range(U_WQ):
                    unit = unit_of[f"wq{l}"] + u
                    ahead(unit)
                    if u % 2 == 1:
                        dve.wait_ge(used, unit + 1)
                        dve.tensor_copy(qT[:, u, :], ps[:, 4 + u % 4, 0:S]).then_inc(wq_out_v, 1)
                first = unit_of[f"u{l}"]
                work = [0.0, first]

                def worked(us, limit=HALF - 1):
                    work[0] += us
                    while work[0] > 0.0 and work[1] <= first + limit:
                        ahead(work[1])
                        work[1] += 1
                        work[0] -= 1.35

                def top16(rows_, values, places, us, ready=None):
                    for r, v, p_ in zip(rows_, values, places):
                        i = dve.max(v[:, 0:8], r)
                    chain(i)
                    for r, v, p_ in zip(rows_, values, places):
                        i = dve.max_index(p_[:, 0:8], v[:, 0:8], r)
                    worked(2 * us, EXP_AT - 1)
                    chain(i)
                    for r, v, p_ in zip(rows_, values, places):
                        i = dve.match_replace(r, v[:, 0:8], r, -3e38)
                    chain(i)
                    for r, v, p_ in zip(rows_, values, places):
                        i = dve.max(v[:, 8:16], r)
                    worked(2 * us, EXP_AT - 1)
                    chain(i)
                    for r, v, p_ in zip(rows_, values, places):
                        i = dve.max_index(p_[:, 8:16], v[:, 8:16], r)
                    if ready:
                        i.then_inc(*ready)
                        worked(us, EXP_AT - 1)
                    else:
                        worked(us, EXP_AT - 1)
                        chain(i)

                for t in range(NT):
                    for a in range(0, 16, 4):
                        if t == 0:
                            dve.wait_ge(lo_bank_free, LO * l + a // 4 + 1)
                        else:
                            dve.wait_ge(hi_bank_free, HI * l + a // 4 + 1)
                        g = range(a, a + 4)
                        top16([sc[:, t, q, :] for q in g], [val[:, t, q, :] for q in g], [idx[:, t, q, :] for q in g],
                              0.8, (val_ready, 1) if a == 12 else None)
                for t in range(NT):
                    dve.wait_ge(cand_ready, NT * l + t + 1)
                    for a in range(0, HEADS, 4):
                        g = range(a, a + 4)
                        top16([cand[:, t, q, :] for q in g], [topv[:, t, q, :] for q in g],
                              [topp[:, t, q * TOPK:(q + 1) * TOPK] for q in g], 1.3)
                gate = slotv[:, 2].rearrange("p t (h k) -> p t h k", h=HEADS)
                chain(dve.tensor_copy(zsum[:], topv[:, :, :, 0]))
                dve.tensor_tensor(topv[:], topv[:], zsum[:].unsqueeze(3).to_broadcast([P, NT, HEADS, TOPK]),
                                  ALU.subtract).then_inc(top_ready, 1)
                dve.tensor_copy(idxf[:], idx[:])
                dve.tensor_scalar(digit[:, 0], topp[:], 4, None, ALU.logical_shift_right)
                chain(dve.tensor_scalar(digit[:, 1], topp[:], 15, None, ALU.bitwise_and))
                chain(dve.tensor_copy(digitf[:], digit[:]))
                for s in range(2):
                    for t in range(NT):
                        chain(dve.tensor_tensor(eq[:, t],
                                                digitf[:, s, t].unsqueeze(2).to_broadcast([P, SLOTS, TOPK]),
                                                iota_h[:].unsqueeze(1).to_broadcast([P, SLOTS, TOPK]),
                                                ALU.is_equal))
                        worked(2.2)
                        e4 = eq[:, t].rearrange("p (h k) a -> p h k a", h=HEADS)
                        src = idxf[:, t].rearrange("p (h s) k -> p h s k", s=2)[:, :, s, :]
                        chain(dve.tensor_tensor(e4, e4, src.unsqueeze(2).to_broadcast([P, HEADS, TOPK, TOPK]), ALU.mult))
                        worked(1.1)
                        chain(dve.tensor_reduce(slotv[:, s, t], eq[:, t], AX, ALU.add))
                        worked(2.2)
                dve.wait_ge(exp_ready, l + 1)
                chain(dve.tensor_reduce(zsum[:], topv[:], AX, ALU.add))
                chain(dve.reciprocal(zsum[:], zsum[:]))
                dve.tensor_tensor(gate, topv[:], zsum[:].unsqueeze(3).to_broadcast([P, NT, HEADS, TOPK]),
                                  ALU.mult).then_inc(slots_ready, 1)
                ahead(first + SLOTS_AT - 1)
                dve.wait_ge(slots_mm, l + 1)
                dve.tensor_copy(slotT[:, 0:2, 0:S], ps[:, 4, :].rearrange("p (a t) -> p a t", a=2)
                                ).then_inc(hi_bank_free, 1)
                chain(dve.tensor_scalar(gate_h[:], ps[:, 5, 0:S], GATE_SCALE, None, ALU.mult))
                dve.tensor_copy(slotT[:, 2, 0:S], gate_h[:])
                dve.scalar_tensor_tensor(out=slotT[:, 3, 0:S], in0=ps[:, 5, 0:S], scalar=GATE_SCALE, in1=gate_h[:],
                                         op0=ALU.mult, op1=ALU.subtract).then_inc(hi_bank_free, 1)
                dve.wait_ge(hi_bank_free, HI * l + 6)

                def one_hots(half, group, turn):
                    for k in range(GROUP):
                        col = offset(turn, TURN * GROUP, group * GROUP + k)
                        if k < ACT_TOKEN:
                            dve.tensor_scalar(hots_i[:, group % 2, k, :], iota[:], slotT[:, 0, bass.ds(col, 1)],
                                              None, ALU.is_equal)
                        i = dve.scalar_tensor_tensor(
                            out=hots_j[:, group % 2, k],
                            in0=iota[:, half * HALF:(half + 1) * HALF].unsqueeze(1).to_broadcast([P, 2, HALF]),
                            scalar=slotT[:, 1, bass.ds(col, 1)],
                            in1=slotT[:, 2:4, bass.ds(col, 1)].to_broadcast([P, 2, HALF]),
                            op0=ALU.is_equal, op1=ALU.mult)
                    i.then_inc(hot_ready, 1)

                def weigh(half, r, turn0, turn):
                    group = r - TURN * turn0
                    dve.wait_ge(w_mm, offset(turn, TURN, GROUPS * (2 * l + half) + group + 1))
                    g = G[:, half * HALF:(half + 1) * HALF, bass.ds(offset(turn, TURN * GROUP, group * GROUP), GROUP)]
                    dve.scalar_tensor_tensor(
                        out=g, in0=ps[:, 4 + r % 4, 0:GROUP * HALF].rearrange("p (t j) -> p j t", t=GROUP),
                        scalar=1.0 / GATE_SCALE, in1=g, op0=ALU.mult, op1=ALU.mult).then_inc(hi_bank_free, 1)

                def next_hots(half, r, turn0, turn):
                    group = r - TURN * turn0
                    if turn is not None or group < GROUPS - 2:
                        one_hots(half, group + 2, turn)
                    elif half == 0:
                        one_hots(1, group + 2 - GROUPS, None)

                ahead(first + SLOTS_AT)
                one_hots(0, 0, None)
                one_hots(0, 1, None)
                ahead(first + HALF - 1)
                dve.wait_ge(lo_bank_free, LO * l + 4 + HALF // 2)
                with dve.Fori(HALF // TURN, U_E // TURN - 1) as turn:
                    for r in range(TURN):
                        weigh(0, r, HALF // TURN, turn)
                        next_hots(0, r, HALF // TURN, turn)
                        low(first + r + AHEAD, turn)
                looped(HALF - TURN)
                for u in range(U_E - TURN, U_E):
                    weigh(0, u, HALF // TURN, None)
                    if u < U_E - 1:
                        next_hots(0, u, HALF // TURN, None)
                        ahead(first + u)

                first = unit_of[f"v{l}"]

                def put(pair, turn):
                    dve.wait_ge(stage_h_ready, offset(turn, TURN // 2, U_E // 2 * l + pair + 1))
                    dve.tensor_tensor(stage_l[:, pair % 2, :],
                                      G[:, bass.ds(offset(turn, TURN, 2 * pair), 2), :].rearrange("p j t -> p (j t)"),
                                      stage_h[:, pair % 2, :].bitcast(F32), ALU.subtract).then_inc(stage_ready, 1)

                for half in range(2):
                    put(HALF // 2 * half, None)
                    if half == 0:
                        next_hots(0, U_E - 1, HALF // TURN, None)
                        dve.wait_ge(lo_bank_free, LO * (l + 1))
                    ahead(first + half * HALF - 1)
                    with dve.Fori(half * HALF // TURN, (half + 1) * HALF // TURN - 1) as turn:
                        for r in range(TURN):
                            if r % 2 == 0:
                                put(r // 2 + 1, turn)
                            if half == 0:
                                weigh(1, r, 0, turn)
                                next_hots(1, r, 0, turn)
                            low(first + r + AHEAD, turn)
                    looped(HALF - TURN)
                    for u in range((half + 1) * HALF - TURN, (half + 1) * HALF):
                        if u % 2 == 0 and u < (half + 1) * HALF - 2:
                            put(u // 2 + 1, None)
                        if half == 0:
                            weigh(1, u, 0, None)
                            next_hots(1, u, 0, None)
                        if u != HALF - 1:
                            ahead(first + u)
                for t in range(NT):
                    for nb in range(2):
                        dve.wait_ge(used, unit_of[f"v{l}"] + U_E)
                        xs = x[:, t, nb * 512:(nb + 1) * 512]
                        dve.tensor_tensor(xs, xs, ps[:, 2 * t + nb, :], ALU.add).then_inc(x_ready, 1)

            ffn(0)
            norm(3, 2)
            transposed(3, gain(2))
            ahead(unit_of["qkv"])
            chain(dve.tensor_copy(trig[:, 0, :, 0], pos_i[:]))
            for k in range(ROPE_HALF):
                i = dve.tensor_scalar(trig[:, 1, :, k], trig[:, 0, :, 0], float(ROPE_INV[k]), None, ALU.mult)
            chain(i)
            chain(dve.tensor_scalar(trig[:, 2], trig[:, 1], 1.0 / TWO_PI, None, ALU.mult))
            chain(dve.tensor_copy(trig_i[:], trig[:, 2]))
            chain(dve.tensor_copy(trig[:, 2], trig_i[:]))
            for c in (PI_1, PI_2, PI_3):
                chain(dve.scalar_tensor_tensor(out=trig[:, 1], in0=trig[:, 2], scalar=-c, in1=trig[:, 1],
                                               op0=ALU.mult, op1=ALU.add))
            for sign, cmp in ((-1.0, ALU.is_gt), (1.0, ALU.is_lt)):
                chain(dve.tensor_scalar(trig[:, 3], trig[:, 1], -sign * float(np.pi), sign * TWO_PI, cmp, ALU.mult))
                chain(dve.tensor_tensor(trig[:, 1], trig[:, 1], trig[:, 3], ALU.add))
            chain(dve.tensor_scalar(trig[:, 2], trig[:, 1], float(np.pi / 2), None, ALU.add))
            chain(dve.tensor_scalar(trig[:, 3], trig[:, 2], float(np.pi), -TWO_PI, ALU.is_gt, ALU.mult))
            chain(dve.tensor_tensor(trig[:, 2], trig[:, 2], trig[:, 3], ALU.add))
            dve.tensor_scalar(trig[:, 4:6], trig[:, 1:3], PI_SAFE, -PI_SAFE, ALU.min, ALU.max).then_inc(trig_step, 1)
            lv = sm[:, SM_LAM:SM_LAM + 256].rearrange("p (a d) -> p a d", a=4)
            chain(dve.tensor_tensor(sq_da[:, 0, 0:128].rearrange("p (a d) -> p a d", a=2), lv[:, 0:4:2, :],
                                    lv[:, 1:4:2, :], ALU.mult))
            dve.tensor_reduce(lam[:, 0:2], sq_da[:, 0, 0:128].rearrange("p (a d) -> p a d", a=2), AX, ALU.add
                              ).then_inc(lam_ready, 1)
            dve.wait_ge(lam_ready, 2)
            chain(dve.tensor_tensor(lam[:, 4:5], lam[:, 3:4], lam[:, 2:3], ALU.subtract))
            chain(dve.tensor_scalar(lam[:, 5:6], lam[:, 4:5], LAMBDA_INIT, None, ALU.subtract))
            chain(dve.tensor_scalar(lam[:, 6:7], sm[:, SM_SUBLN:SM_SUBLN + 1], 1.0 - LAMBDA_INIT, None, ALU.mult))

            def qk_mean(nb):
                dve.wait_ge(qk_sq_ready, nb + 1)
                g = gss[:, :, 8 * nb:8 * nb + 8]
                chain(dve.tensor_reduce(g, sq_da[:, :, nb * 512:(nb + 1) * 512].rearrange("p t (g d) -> p t g d", d=64),
                                        AX, ALU.add))
                dve.tensor_scalar(g, g, 1.0 / 64, EPS, ALU.mult, ALU.add).then_inc(qk_var_ready, 1)

            def qk_norm(nb, unit):
                dve.wait_ge(qk_std_ready, nb + 1)
                g = gss[:, :, 8 * nb:8 * nb + 8]
                chain(dve.reciprocal(g, g))
                q4 = QK[:, :, nb * 512:(nb + 1) * 512].rearrange("p t (g d) -> p t g d", d=64)
                wide = [P, NT, 8, 64]
                chain(dve.tensor_tensor(q4, q4, g.unsqueeze(3).to_broadcast(wide), ALU.mult))
                at_ = SM_QG + 64 * (nb // 2)
                for t in range(NT):
                    i = dve.tensor_tensor(q4[:, t], q4[:, t],
                                          sm[:, at_:at_ + 64].unsqueeze(1).to_broadcast([P, 8, 64]), ALU.mult)
                chain(i)
                if unit is not None:
                    ahead(unit)
                x1, x2 = q4[:, :, :, 0:8], q4[:, :, :, 8:16]
                sin_ = trig[:, 6].unsqueeze(2).to_broadcast([P, NT, 8, ROPE_HALF])
                cos_ = trig[:, 7].unsqueeze(2).to_broadcast([P, NT, 8, ROPE_HALF])
                dve.tensor_tensor(rt[:, 0], x1, cos_, ALU.mult)
                dve.tensor_tensor(rt[:, 1], x2, sin_, ALU.mult)
                dve.tensor_tensor(rt[:, 2], x2, cos_, ALU.mult)
                chain(dve.tensor_tensor(rt[:, 3], x1, sin_, ALU.mult))
                dve.tensor_tensor(x1, rt[:, 0], rt[:, 1], ALU.subtract)
                dve.tensor_tensor(x2, rt[:, 2], rt[:, 3], ALU.add).then_inc(qkn_ready, 1)
                dve.wait_ge(qkn_ready, nb + 1)

            dve.wait_ge(trig_step, 2)
            for nb in range(6):
                tokens_made(dve, ahead, qkv_mm, "qkv", nb, 0)
                if nb < 4:
                    dst = QK[:, 0, nb * 512:(nb + 1) * 512]
                else:
                    dst = v_da[:, 0, (nb - 4) * 512:(nb - 3) * 512]
                dve.tensor_copy(dst, ps[:, 4 + 2 * (nb % 2), :]).then_inc(qkv_out_v, 1)
                if nb < 4:
                    qk_mean(nb)
                    ahead(unit_of["qkv"] + 4 * nb + 4)
                if 1 <= nb <= 4:
                    qk_norm(nb - 1, unit_of["qkv"] + 4 * nb + 5 if nb < 4 else None)
            ahead(unit_of["qkv"] + U_QKV - 1)

            for b in range(1, 8, 2):
                dve.wait_ge(qkt_mm, b + 1)
                dve.tensor_copy(qkT_da[:, 2 * b:2 * b + 2, :].rearrange("p a t -> p (a t)"), ps[:, b, :]
                                ).then_inc(qkt_out_v, 1)

            def da_max(n):
                dve.wait_ge(s_mm, n + 1)
                b = 2 * (n % 2)
                chain(dve.tensor_reduce(mx[:, n, :], ps[:, b:b + 2, 0:S], AX, ALU.max))
                dve.tensor_scalar(mx[:, n, :], mx[:, n, :], -DA_SCALE, None, ALU.mult).then_inc(mx_ready, 1)

            def da_sums(n):
                dve.wait_ge(pe_ready, 2 * n + 2)
                chain(dve.reciprocal(zz[:, n, 2:4], zz[:, n, 0:2]))
                dve.tensor_scalar(zz[:, n, 3:4], zz[:, n, 3:4], lam[:, 5:6], None, ALU.mult).then_inc(rz_ready, 1)

            def da_difference(n):
                dve.wait_ge(e1_ready, n + 1)
                dve.wait_ge(rz_ready, n + 1)
                if n >= 2:
                    dve.wait_ge(aT_mm, n - 1)
                dve.scalar_tensor_tensor(out=a_da[:, n % 2, :], in0=e_da[:, n % 3, 0, :], scalar=zz[:, n, 2:3],
                                         in1=e1_da[:, n % 2], op0=ALU.mult, op1=ALU.add).then_inc(a_ready, 1)

            def da_got(n):
                dve.wait_ge(o_mm, n + 1)
                dve.tensor_copy(o_da[:, n % 2, n // 2, :], ps[:, 6 + n % 2, 0:P]).then_inc(o_got, 1)

            for n in range(16 + 5):
                if n < 16:
                    da_max(n)
                if 1 <= n < 17:
                    da_sums(n - 1)
                if 2 <= n < 18:
                    da_difference(n - 2)
                if n >= 5:
                    da_got(n - 5)
            head_norm(o_da, 2)
            dve.wait_ge(loaded_small, 32)
            transposed(4, lambda kd: lam[:, 6:7])
            add_to_x(1)
            ffn(1)

        @block.tensor
        def _(pe):
            def split(unit, turn=None):
                pe.wait_ge(split_ready, offset(turn, TURN, unit + 1))
                return wh[:, unit % RING, :], wl[:, unit % RING, :]

            def keep_warm(bank, count):
                for _ in range(count):
                    pe.matmul(ps[:, bank, :], ident_b[:], ident_b[:].unsqueeze(1).to_broadcast([P, 4, P]),
                              start=True, stop=True)

            def transposes(n):
                for b in range(4):
                    for kd in (2 * b, 2 * b + 1):
                        for t in range(NT):
                            if kd in (0, KD // 2):
                                pe.wait_ge(xn_ready, 4 * n + 2 * (b // 2) + t + 1)
                            at_ = (kd % 2) * S + t * P
                            i = pe.transpose(ps[:, b, at_:at_ + P], xn[:, t, kd * P:(kd + 1) * P], ident[:])
                    i.then_inc(xT_ready, 1)
                fresh[:] = [n]

            fresh = []

            def tokens_ready(kd):
                if fresh and kd % 2 == 0:
                    pe.wait_ge(hT_ready, 4 * fresh[0] + kd // 2 + 1)
                if kd == KD - 1:
                    fresh.clear()

            def up_projection(out, unit, turn=None):
                w_h, w_l = (w.rearrange("p (k c) -> p k c", k=KD) for w in split(unit, turn))
                for kd in range(KD):
                    tokens_ready(kd)
                    pe.matmul(out, w_h[:, kd, :], hTh[:, kd, :], start=(kd == 0), stop=False)
                    pe.matmul(out, w_h[:, kd, :], hTl[:, kd, :], start=False, stop=False)
                    i = pe.matmul(out, w_l[:, kd, :], hTh[:, kd, :], start=False, stop=(kd == KD - 1))
                i.then_inc(used, 1)

            def by_columns(unit0, units, bank, before):
                for u in range(units):
                    before(u)
                    up_projection(ps[:, bank(u), 0:S], unit0 + u)

            def by_tokens(unit0, blocks, bank, done, before):
                for nb in range(blocks):
                    for q in range(4):
                        w_h, w_l = (w.rearrange("p (k c) -> p k c", k=2) for w in split(unit0 + 4 * nb + q))
                        tokens_ready(2 * q)
                        tokens_ready(2 * q + 1)
                        for t in range(NT):
                            if q == 0:
                                before(nb, t)
                            for k in range(2):
                                kd = 2 * q + k
                                h_h, h_l = hTh[:, kd, t * P:(t + 1) * P], hTl[:, kd, t * P:(t + 1) * P]
                                out_ = ps[:, bank(nb, t), :]
                                pe.matmul(out_, h_h, w_h[:, k, :], start=(kd == 0), stop=False)
                                pe.matmul(out_, h_h, w_l[:, k, :], start=False, stop=False)
                                i = pe.matmul(out_, h_l, w_h[:, k, :], start=False, stop=(kd == KD - 1))
                            if q == 3 and t == 0:
                                i.then_inc(done, 1)
                        i.then_inc(used, 1)

            pe.wait_ge(consts, CONSTS)
            keep_warm(0, 12)
            transposes(0)
            up_projection(ps[:, 7, 0:S], unit_of["gate"])

            def qk_bank(u):
                if u == 1:
                    pe.wait_ge(gT_ready, 1)
                    for t in range(NT):
                        i = pe.transpose(ps[:, 7, S + t * 32:S + (t + 1) * 32], gT[0:32, t * P:(t + 1) * P],
                                         ident[0:32, 0:32])
                    i.then_inc(gate_mm, 1)
                if u >= 3:
                    pe.wait_ge(qk_out, u - 2)

            by_columns(unit_of["qk"], U_QK, lambda u: 4 + u % 3, qk_bank)
            pe.wait_ge(lgate_ready, 1)
            for k in range(2):
                for t in range(NT):
                    at_ = k * S + t * P
                    pe.matmul(ps[0:16, 7, at_:at_ + P], lgate[:, t, 2 * k, :], ident[:], start=True, stop=False)
                    i = pe.matmul(ps[0:16, 7, at_:at_ + P], lgate[:, 1 - t, 2 * k + 1, :], flip[:],
                                  start=False, stop=True)
            i.then_inc(rows_mm, 1)

            def vo_bank(nb, t):
                if nb == 2:
                    pe.wait_ge(v_out, t + 1)
                if nb == 3:
                    pe.wait_ge(v_out, 2 + t + 1)

            by_tokens(unit_of["vo"], 4, lambda nb, t: 2 * (nb % 2) + t, vo_mm, vo_bank)
            pe.wait_ge(em_ready, 1)
            for t in range(NT):
                for k in range(3):
                    at_ = t * 48 + k * 16
                    i = pe.matmul(ps[:, 7, at_:at_ + 16], rows[0:16, k, t * P:(t + 1) * P], ident[0:16, 0:16],
                                  start=True, stop=True)
            i.then_inc(cols_mm, 1)
            pe.wait_ge(colC_ready, 1)
            for t in range(NT):
                i = pe.matmul(ps[:, 7, t * 48:(t + 1) * 48], flip[:], colC[:, 1 - t, :], start=True, stop=True)
            i.then_inc(flip_mm, 1)
            pe.wait_ge(colD_ready, 1)
            pe.wait_ge(o_out, 4)
            pe.wait_ge(v_out, 4)
            pe.wait_ge(qk_out, U_QK)

            def ml_scores(h):
                if h >= 1:
                    pe.wait_ge(e_ready, h)
                if h >= 2:
                    pe.wait_ge(p_ready, h - 1)
                lo = (h % 2) * 64
                for s in range(NT):
                    pe.matmul(ps[:, h % 2, s * S:(s + 1) * S], qkT[lo:lo + 64, 4 + h // 2, s * P:(s + 1) * P],
                              qkT[lo:lo + 64, h // 2, :], start=True, stop=True)
                for b, col, c, blocks, m in ((2, colC, 16 + h, ((0, 0), (0, 1), (1, 1)), mask_f),
                                             (3, colD, 24 + h, ((0, 0), (1, 0), (1, 1)), mask_b)):
                    for s, t in blocks:
                        o = ps[:, b, s * S + t * P:s * S + (t + 1) * P]
                        i = pe.matmul(o, col[:, t, c:c + 1].to_broadcast([P, P]), ident[:], start=True, stop=(s != t))
                        if s == t:
                            i = pe.matmul(o, ident_b[:], m[:], start=False, stop=True)
                i.then_inc(se_mm, 1)

            def ml_values(h):
                pe.wait_ge(p_ready, h + 1)
                if h >= 2:
                    pe.wait_ge(hs_ready, 2 * h - 2)
                for d, sources in ((0, ((0,), (0, 1))), (1, ((0, 1), (1,)))):
                    for t in range(NT):
                        for s in sources[t]:
                            i = pe.matmul(ps[:, 4 + 2 * (h % 2) + d, t * 129:(t + 1) * 129],
                                          p_ml[:, h % 2, d, s * S + t * P:s * S + (t + 1) * P], v_ml[:, s, h, :],
                                          start=(s == sources[t][0]), stop=(s == sources[t][-1]))
                i.then_inc(av_mm, 1)

            ml_scores(0)
            for h in range(HEADS):
                if h + 1 < HEADS:
                    ml_scores(h + 1)
                ml_values(h)
            keep_warm(2, 16)
            transposes(1)
            by_tokens(unit_of["wo0"], 2, lambda nb, t: 4 + 2 * nb + t, wo_mm, lambda nb, t: None)

            def ffn(l):
                keep_warm(0, 10)
                transposes((2, 5)[l])

                def wq_bank(u):
                    if u >= 4:
                        pe.wait_ge((wq_out_a, wq_out_v)[u % 2], U_WQ // 2 * l + (u - 4) // 2 + 1)

                by_columns(unit_of[f"wq{l}"], U_WQ, lambda u: 4 + u % 4, wq_bank)
                pe.wait_ge(wq_out_a, U_WQ // 2 * (l + 1))
                pe.wait_ge(wq_out_v, U_WQ // 2 * (l + 1))
                pe.wait_ge(loaded_keys[l], 16)
                for t in range(NT):
                    for b in range(4):
                        for k in range(4):
                            q = 4 * b + k
                            i = pe.matmul(ps[:, 4 * t + b, k * P:(k + 1) * P], qT[:, q, t * P:(t + 1) * P],
                                          keysT[:, q, :], start=True, stop=True)
                        i.then_inc(score_mm, 1)
                first = unit_of[f"u{l}"]

                def up(r, turn):
                    if r % 2 == 0:
                        pe.wait_ge(lo_bank_free, offset(turn, TURN // 2, LO * l + r // 2 + 1))
                    up_projection(ps[:, r // 2 % 4, (r % 2) * S:(r % 2 + 1) * S], first + r, turn)

                def weights(half, r, turn0, turn):
                    w = offset(turn, TURN, r - TURN * turn0)
                    pe.wait_ge(hot_ready, w + (HOT * l + GROUPS * half + 1))
                    pe.wait_ge(hot_ready_a, w + (HOT * l + GROUPS * half + 1))
                    pe.wait_ge(hi_bank_free, w + (HI * l + GROUPS * half + 3))
                    for k in range(GROUP):
                        for part in range(2):
                            i = pe.matmul(ps[:, 4 + r % 4, k * HALF:(k + 1) * HALF], hots_i[:, r % 2, k, :],
                                          hots_j[:, r % 2, k, part, :], start=(part == 0), stop=(part == 1))
                    i.then_inc(w_mm, 1)

                def slots():
                    pe.wait_ge(hi_bank_free, HI * l + 4)
                    pe.wait_ge(slots_ready, l + 1)
                    for k in range(3):
                        for t in range(NT):
                            i = pe.transpose(ps[:, 4 + k // 2, (k % 2) * S + t * P:(k % 2) * S + (t + 1) * P],
                                             slotv[:, k, t, :], ident[:])
                    i.then_inc(slots_mm, 1)

                with pe.Fori(0, HALF // TURN - 1) as turn:
                    for r in range(TURN):
                        up(r, turn)
                for u in range(HALF - TURN, HALF):
                    if u == SLOTS_AT:
                        slots()
                    up(u, None)
                pe.wait_ge(hi_bank_free, HI * l + 6)
                with pe.Fori(HALF // TURN, U_E // TURN) as turn:
                    for r in range(TURN):
                        up(r, turn)
                        weights(0, r, HALF // TURN, turn)
                pe.wait_ge(lo_bank_free, LO * (l + 1) - 3)
                keep_warm(0, 12)
                pe.wait_ge(lo_bank_free, LO * (l + 1))
                for t in range(NT):
                    for nb in range(2):
                        pe.matmul(ps[:, 2 * t + nb, :], ident_b[:], zero_b[:].to_broadcast([P, 512]), start=True,
                                  stop=False, skip_group_check=True)
                first = unit_of[f"v{l}"]
                for half in range(2):
                    with pe.Fori(half * HALF // TURN, (half + 1) * HALF // TURN) as turn:
                        for r in range(TURN):
                            if half == 0:
                                weights(1, r, 0, turn)
                            if r % 2 == 0:
                                pe.wait_ge(stage_ready, TURN // 2 * turn + (U_E // 2 * l + r // 2 + 1))
                            w_h, w_l = split(first + r, turn)
                            for t in range(NT):
                                at_ = (r % 2) * S + t * P
                                g_h = stage_h[:, r // 2 % 2, at_:at_ + P]
                                g_l = stage_l[:, r // 2 % 2, at_:at_ + P]
                                for a, b in ((g_h, w_h), (g_h, w_l), (g_l, w_h)):
                                    for nb in range(2):
                                        i = pe.matmul(ps[:, 2 * t + nb, :], a, b[:, nb * 512:(nb + 1) * 512],
                                                      start=False, stop=False, skip_group_check=True)
                            i.then_inc(used, 1)

            ffn(0)
            keep_warm(4, 16)
            transposes(3)

            def qkv_bank(nb, t):
                if nb >= 2:
                    pe.wait_ge((qkv_out_v, qkv_out_a)[t], nb - 1)

            by_tokens(unit_of["qkv"], 6, lambda nb, t: 4 + 2 * (nb % 2) + t, qkv_mm, qkv_bank)
            pe.wait_ge(qkn_ready, 4)
            pe.wait_ge(qkv_out_v, 6)
            pe.wait_ge(qkv_out_a, 6)
            for b in range(8):
                for k in range(2):
                    for t in range(NT):
                        q = 2 * b + k
                        i = pe.transpose(ps[:, b, k * S + t * P:k * S + (t + 1) * P], QK[:, t, q * P:(q + 1) * P],
                                         ident[:])
                i.then_inc(qkt_mm, 1)
            pe.wait_ge(qkt_out_a, 4)
            pe.wait_ge(qkt_out_v, 4)

            def da_scores(n):
                h, t = n // 2, n % 2
                if n >= 2:
                    pe.wait_ge(pe_ready, 2 * n - 2)
                keep_warm(2 * (n % 2), 1)
                for c in range(2):
                    i = pe.matmul(ps[:, 2 * (n % 2) + c, 0:S], qkT_da[64 * c:64 * c + 64, h, t * P:(t + 1) * P],
                                  qkT_da[64 * c:64 * c + 64, 8 + h, :], start=True, stop=True)
                i.then_inc(s_mm, 1)

            def da_turn(n):
                pe.wait_ge(a_ready, n + 1)
                if n >= 2:
                    pe.wait_ge(aT_out, n - 1)
                for k in range(NT):
                    i = pe.transpose(ps[:, 4 + n % 2, k * P:(k + 1) * P], a_da[:, n % 2, k * P:(k + 1) * P], ident[:])
                i.then_inc(aT_mm, 1)

            def da_values(n):
                pe.wait_ge(aT_out, n + 1)
                if n >= 2:
                    pe.wait_ge(o_got, n - 1)
                h = n // 2
                for k in range(NT):
                    i = pe.matmul(ps[:, 6 + n % 2, 0:P], aT_da[:, n % 2, k, :], v_da[:, k, h * P:(h + 1) * P],
                                  start=(k == 0), stop=(k == NT - 1))
                i.then_inc(o_mm, 1)

            for n in range(16 + 4):
                if n < 16:
                    da_scores(n)
                if 3 <= n < 19:
                    da_turn(n - 3)
                if n >= 4:
                    da_values(n - 4)
            keep_warm(2, 12)
            transposes(4)
            by_tokens(unit_of["wo1"], 2, lambda nb, t: 4 + 2 * nb + t, wo_mm, lambda nb, t: None)
            ffn(1)


def _by_columns(w):
    n = w.shape[1] // P
    return w.reshape(KD, P, n, P).transpose(2, 1, 0, 3).reshape(n, P, UNIT)


def _by_tokens(w):
    n = w.shape[1] // 512
    return w.reshape(4, 2, P, n, 512).transpose(3, 0, 2, 1, 4).reshape(4 * n, P, UNIT)


def _up(u):
    return u.reshape(NKEYS, NKEYS, KD, P).transpose(1, 3, 2, 0).reshape(NKEYS, P, UNIT)


def _down(v):
    return v.reshape(NKEYS, NKEYS, UNIT).transpose(1, 0, 2)


def kernel(**inputs):
    import concourse.bacc as bacc
    from concourse.bass_utils import run_bass_kernel_spmd

    a = {k: np.asarray(v) for k, v in inputs.items()}
    w_in, qkv = a["l0_w_in"], a["l1_w_qkv"]
    parts = [_by_columns(np.pad(w_in[:, 3 * D:], ((0, 0), (0, P - 32)))), _by_columns(w_in[:, :D]),
             _by_tokens(w_in[:, D:3 * D]), _by_tokens(a["l0_w_out"]),
             _by_columns(a["l0_peer_wq"]), _up(a["l0_peer_u"]), _down(a["l0_peer_v"]),
             _by_tokens(qkv), _by_tokens(a["l1_w_out"]),
             _by_columns(a["l1_peer_wq"]), _up(a["l1_peer_u"]), _down(a["l1_peer_v"])]
    stream = np.concatenate(parts + [np.zeros((TAIL, P, UNIT), np.float32)])
    column = lambda g: g.reshape(-1, P).T
    all_rows = lambda g: np.broadcast_to(g.reshape(1, -1), (P, g.size))
    small = np.concatenate([column(a[k]) for k in ("l0_norm_mix", "l0_norm_ffn", "l1_norm_mix", "l1_norm_ffn",
                                                   "l0_head_norm", "l1_subln")]
                           + [all_rows(a[k]) for k in ("l0_b_gates", "l1_q_norm", "l1_k_norm", "l1_lambda_q1",
                                                       "l1_lambda_k1", "l1_lambda_q2", "l1_lambda_k2")], axis=1)
    keys = lambda k: np.ascontiguousarray(k.transpose(3, 0, 1, 2).reshape(P, 16, NKEYS))
    arrays = {
        "stream": stream,
        "small": np.ascontiguousarray(small),
        "keys0": keys(a["l0_peer_keys"]),
        "keys1": keys(a["l1_peer_keys"]),
        "positions": np.ascontiguousarray(a["positions"].reshape(NT, P).T),
        "x_in": np.ascontiguousarray(a["x"].reshape(NT, P, D).transpose(1, 0, 2)),
    }
    nc = bacc.Bacc("TRN2", target_bir_lowering=False, num_devices=1, dynamic_dma_scratch_size=1024)
    aps = {k: nc.dram_tensor(k, v.shape, mybir.dt.from_np(v.dtype), kind="ExternalInput").ap()
           for k, v in arrays.items()}
    out = nc.dram_tensor("out", (NT, P, D), F32, kind="ExternalOutput").ap()
    program(nc, out=out, **aps)
    r = run_bass_kernel_spmd(nc, [arrays], core_ids=[0])
    return np.asarray(r.results[0]["out"]).reshape(1, S, D)
```
